# Optimizing a Trainium2 kernel written in Bass

```python
import math
import jax, jax.numpy as jnp
from jax import lax
import numpy as np

D_MODEL = 1024
BATCH = 1
SEQ = 512
DEPTH = 2

SSM_GROUP = 16
N_GROUPS = D_MODEL // SSM_GROUP
SSM_STATE = 64
DT_MIN = 1e-3
DT_MAX = 1e-1
N_HEADS = 8
QK_NOPE = 128
QK_ROPE = 64
V_HEAD = 128
Q_LORA = 384
KV_LORA = 256
ROPE_THETA = 10000.0
Q_BLOCK = 128
SM_SCALE = (QK_NOPE + QK_ROPE) ** -0.5
NEG_INF = -1e30
D_FF = 4 * D_MODEL
N_A_LAYERS = DEPTH // 2
N_B_LAYERS = DEPTH - N_A_LAYERS
DN_ALPHA = (2 * DEPTH) ** 0.25
DN_BETA = (8 * DEPTH) ** -0.25
LN_EPS = 1e-5
RMS_EPS = 1e-6


def layer_norm(x, g, b):
    xf = x.astype(jnp.float32)
    mu = jnp.mean(xf, axis=-1, keepdims=True)
    var = jnp.mean(jnp.square(xf - mu), axis=-1, keepdims=True)
    y = (xf - mu) * lax.rsqrt(var + LN_EPS) * g.astype(jnp.float32) + b.astype(jnp.float32)
    return y.astype(x.dtype)

def rms_norm(x, g):
    xf = x.astype(jnp.float32)
    y = xf * lax.rsqrt(jnp.mean(jnp.square(xf), axis=-1, keepdims=True) + RMS_EPS) * g.astype(jnp.float32)
    return y.astype(x.dtype)

def rope_tables(positions):
    half = QK_ROPE // 2
    inv_freq = ROPE_THETA ** (-jnp.arange(half, dtype=jnp.float32) / half)
    ang = positions.astype(jnp.float32)[..., None] * inv_freq
    return jnp.cos(ang), jnp.sin(ang)

def apply_rope(x, cos, sin):
    x1, x2 = jnp.split(x.astype(jnp.float32), 2, axis=-1)
    return jnp.concatenate([x1 * cos - x2 * sin, x1 * sin + x2 * cos], axis=-1).astype(x.dtype)

def _complex_linear_combine(left, right):
    ar_l, ai_l, hr_l, hi_l = left
    ar_r, ai_r, hr_r, hi_r = right
    return (ar_r * ar_l - ai_r * ai_l,
            ar_r * ai_l + ai_r * ar_l,
            ar_r * hr_l - ai_r * hi_l + hr_r,
            ar_r * hi_l + ai_r * hr_l + hi_r)

def s5_mixer(x, lam_re, lam_im, log_dt, b_re, b_im, c_re, c_im, d_skip, w_glu, w_out):
    f32 = jnp.float32
    bsz, seq, _ = x.shape
    u = x.astype(f32).reshape(bsz, seq, N_GROUPS, SSM_GROUP)
    lr = lam_re.astype(f32)
    li = lam_im.astype(f32)
    dt = jnp.exp(log_dt.astype(f32))[:, None]
    mag = jnp.exp(lr * dt)
    a_re = mag * jnp.cos(li * dt)
    a_im = mag * jnp.sin(li * dt)
    inv_den = 1.0 / (lr * lr + li * li)
    coef_re = ((a_re - 1.0) * lr + a_im * li) * inv_den
    coef_im = (a_im * lr - (a_re - 1.0) * li) * inv_den
    br = b_re.astype(f32)
    bi = b_im.astype(f32)
    bb_re = coef_re[..., None] * br - coef_im[..., None] * bi
    bb_im = coef_re[..., None] * bi + coef_im[..., None] * br
    bu_re = jnp.einsum('bsgc,gpc->bsgp', u, bb_re)
    bu_im = jnp.einsum('bsgc,gpc->bsgp', u, bb_im)
    shape_a = (1, seq, N_GROUPS, SSM_STATE)
    a_re_t = jnp.broadcast_to(a_re, shape_a)
    a_im_t = jnp.broadcast_to(a_im, shape_a)
    _, _, h_re, h_im = lax.associative_scan(
        _complex_linear_combine, (a_re_t, a_im_t, bu_re, bu_im), axis=1)
    y = (jnp.einsum('bsgp,gcp->bsgc', h_re, c_re.astype(f32))
         - jnp.einsum('bsgp,gcp->bsgc', h_im, c_im.astype(f32)))
    y = y + d_skip.astype(f32).reshape(N_GROUPS, SSM_GROUP) * u
    y = jax.nn.gelu(y.reshape(bsz, seq, D_MODEL)).astype(x.dtype)
    val, gate = jnp.split(y @ w_glu, 2, axis=-1)
    return (val * jax.nn.sigmoid(gate)) @ w_out

def mla_shared_kv(h, kv_w_a, kv_norm_g, kv_w_b, cos, sin):
    bsz, seq, _ = h.shape
    c_kv, k_rope = jnp.split(h @ kv_w_a, [KV_LORA], axis=-1)
    c_kv = rms_norm(c_kv, kv_norm_g)
    k_rope = apply_rope(k_rope, cos, sin)
    kv = (c_kv @ kv_w_b).reshape(bsz, seq, N_HEADS, QK_NOPE + V_HEAD)
    k_nope, v = jnp.split(kv, [QK_NOPE], axis=-1)
    return k_nope, k_rope, v

def mla_mixer(h, q_w_a, q_norm_g, q_w_b, w_o, k_nope, k_rope, v, cos, sin):
    bsz, seq, _ = h.shape
    c_q = rms_norm(h @ q_w_a, q_norm_g)
    q = (c_q @ q_w_b).reshape(bsz, seq, N_HEADS, QK_NOPE + QK_ROPE)
    q_nope, q_rope = jnp.split(q, [QK_NOPE], axis=-1)
    q_rope = apply_rope(q_rope, cos[:, :, None, :], sin[:, :, None, :])
    n_blocks = seq // Q_BLOCK

    def to_blocks(t):
        return t.reshape(bsz, n_blocks, Q_BLOCK, *t.shape[2:]).swapaxes(0, 1)

    key_pos = jnp.arange(seq)

    def attend_block(args):
        blk, qn, qr = args
        s = (jnp.einsum('bqhd,bkhd->bhqk', qn, k_nope, preferred_element_type=jnp.float32)
             + jnp.einsum('bqhr,bkr->bhqk', qr, k_rope, preferred_element_type=jnp.float32)) * SM_SCALE
        q_pos = blk * Q_BLOCK + jnp.arange(Q_BLOCK)
        s = jnp.where(key_pos[None, :] <= q_pos[:, None], s, NEG_INF)
        p = jax.nn.softmax(s, axis=-1).astype(v.dtype)
        return jnp.einsum('bhqk,bkhd->bqhd', p, v)

    o = lax.map(attend_block, (jnp.arange(n_blocks), to_blocks(q_nope), to_blocks(q_rope)))
    o = o.swapaxes(0, 1).reshape(bsz, seq, N_HEADS * V_HEAD)
    return o @ w_o

def sq_relu_mlp(h, w1, w2):
    return jnp.square(jax.nn.relu(h @ w1)) @ w2

def first_inputs(seed: int = 0) -> dict:
    key = jax.random.key(seed)
    k = jax.random.split(key, 24)
    f32 = jnp.float32

    def nrm(i, shape, scale):
        return jax.random.normal(k[i], shape, f32) * scale

    n_idx = jnp.arange(SSM_STATE, dtype=f32)
    return {
        'x': nrm(0, (BATCH, SEQ, D_MODEL), 1.0),
        'positions': jnp.broadcast_to(jnp.arange(SEQ, dtype=jnp.int32), (BATCH, SEQ)),
        'ln_mix_g': 1.0 + nrm(1, (DEPTH, D_MODEL), 0.02),
        'ln_mix_b': nrm(2, (DEPTH, D_MODEL), 0.02),
        'ln_ffn_g': 1.0 + nrm(3, (DEPTH, D_MODEL), 0.02),
        'ln_ffn_b': nrm(4, (DEPTH, D_MODEL), 0.02),
        'w_ff1': nrm(5, (DEPTH, D_MODEL, D_FF), D_MODEL ** -0.5),
        'w_ff2': nrm(6, (DEPTH, D_FF, D_MODEL), D_FF ** -0.5 * DN_BETA),
        'ssm_lam_re': -0.5 + nrm(7, (N_A_LAYERS, N_GROUPS, SSM_STATE), 0.01),
        'ssm_lam_im': math.pi * n_idx + nrm(8, (N_A_LAYERS, N_GROUPS, SSM_STATE), 0.01),
        'ssm_log_dt': jax.random.uniform(k[9], (N_A_LAYERS, N_GROUPS), f32, math.log(DT_MIN), math.log(DT_MAX)),
        'ssm_b_re': nrm(10, (N_A_LAYERS, N_GROUPS, SSM_STATE, SSM_GROUP), (2 * SSM_GROUP) ** -0.5),
        'ssm_b_im': nrm(11, (N_A_LAYERS, N_GROUPS, SSM_STATE, SSM_GROUP), (2 * SSM_GROUP) ** -0.5),
        'ssm_c_re': nrm(12, (N_A_LAYERS, N_GROUPS, SSM_GROUP, SSM_STATE), SSM_STATE ** -0.5),
        'ssm_c_im': nrm(13, (N_A_LAYERS, N_GROUPS, SSM_GROUP, SSM_STATE), SSM_STATE ** -0.5),
        'ssm_d': nrm(14, (N_A_LAYERS, D_MODEL), 1.0),
        'ssm_w_glu': nrm(15, (N_A_LAYERS, D_MODEL, 2 * D_MODEL), D_MODEL ** -0.5),
        'ssm_w_out': nrm(16, (N_A_LAYERS, D_MODEL, D_MODEL), D_MODEL ** -0.5 * DN_BETA),
        'kv_w_a': nrm(17, (D_MODEL, KV_LORA + QK_ROPE), D_MODEL ** -0.5),
        'kv_norm_g': 1.0 + nrm(18, (KV_LORA,), 0.02),
        'kv_w_b': nrm(19, (KV_LORA, N_HEADS * (QK_NOPE + V_HEAD)), KV_LORA ** -0.5),
        'q_w_a': nrm(20, (N_B_LAYERS, D_MODEL, Q_LORA), D_MODEL ** -0.5),
        'q_norm_g': 1.0 + nrm(21, (N_B_LAYERS, Q_LORA), 0.02),
        'q_w_b': nrm(22, (N_B_LAYERS, Q_LORA, N_HEADS * (QK_NOPE + QK_ROPE)), Q_LORA ** -0.5),
        'attn_w_o': nrm(23, (N_B_LAYERS, N_HEADS * V_HEAD, D_MODEL), (N_HEADS * V_HEAD) ** -0.5 * DN_BETA),
    }

def first_block(x, positions, ln_mix_g, ln_mix_b, ln_ffn_g, ln_ffn_b, w_ff1, w_ff2,
              ssm_lam_re, ssm_lam_im, ssm_log_dt, ssm_b_re, ssm_b_im, ssm_c_re, ssm_c_im,
              ssm_d, ssm_w_glu, ssm_w_out, kv_w_a, kv_norm_g, kv_w_b,
              q_w_a, q_norm_g, q_w_b, attn_w_o):
    cos, sin = rope_tables(positions)
    h = x
    k_nope = k_rope = v = None
    for layer in range(DEPTH):
        if layer < N_A_LAYERS:
            i = layer
            mix = s5_mixer(h, ssm_lam_re[i], ssm_lam_im[i], ssm_log_dt[i], ssm_b_re[i], ssm_b_im[i],
                           ssm_c_re[i], ssm_c_im[i], ssm_d[i], ssm_w_glu[i], ssm_w_out[i])
        else:
            if layer == N_A_LAYERS:
                k_nope, k_rope, v = mla_shared_kv(h, kv_w_a, kv_norm_g, kv_w_b, cos, sin)
            j = layer - N_A_LAYERS
            mix = mla_mixer(h, q_w_a[j], q_norm_g[j], q_w_b[j], attn_w_o[j], k_nope, k_rope, v, cos, sin)
        h = layer_norm(DN_ALPHA * h + mix, ln_mix_g[layer], ln_mix_b[layer])
        h = layer_norm(DN_ALPHA * h + sq_relu_mlp(h, w_ff1[layer], w_ff2[layer]), ln_ffn_g[layer], ln_ffn_b[layer])
    return h


CHUNK = 64
N_KV_HEADS = 2
HEAD_DIM = 64
ATTN_WIDTH = N_HEADS * HEAD_DIM
ROPE_DIM = HEAD_DIM // 4
ROPE_THETA_2 = 500000.0
N_IDX_HEADS = 4
IDX_DIM = 64
TOPK_MAX = 256
SGU_CHUNK = 128
SGU_GROUPS = 8
SGU_WIDTH = D_MODEL - ATTN_WIDTH
SGU_GROUP_DIM = SGU_WIDTH // SGU_GROUPS
D_FF_2 = -(-(8 * D_MODEL) // (3 * 256)) * 256
PLE_DIM = 256
ALPHA = (2 * DEPTH) ** 0.25
BETA = (8 * DEPTH) ** -0.25

Q_COLS = N_HEADS * HEAD_DIM
KV_COLS = N_KV_HEADS * HEAD_DIM
IQ_COLS = N_IDX_HEADS * IDX_DIM
IK_COLS = IDX_DIM
IW_COLS = N_IDX_HEADS
IN_SPLITS = (Q_COLS, KV_COLS, KV_COLS, IQ_COLS, IK_COLS, IW_COLS, SGU_WIDTH, SGU_WIDTH)
IN_COLS = Q_COLS + 2 * KV_COLS + IQ_COLS + IK_COLS + IW_COLS + 2 * SGU_WIDTH


def layer_norm_2(x, g, b):
    xf = x.astype(jnp.float32)
    mu = jnp.mean(xf, axis=-1, keepdims=True)
    var = jnp.mean(jnp.square(xf - mu), axis=-1, keepdims=True)
    y = (xf - mu) * lax.rsqrt(var + LN_EPS)
    return (y * g.astype(jnp.float32) + b.astype(jnp.float32)).astype(x.dtype)

def partial_rope(x, pos):
    half = ROPE_DIM // 2
    inv = ROPE_THETA_2 ** (-2.0 * jnp.arange(half, dtype=jnp.float32) / ROPE_DIM)
    ang = pos.astype(jnp.float32)[..., None] * inv
    cos = jnp.cos(ang)[:, :, None, :]
    sin = jnp.sin(ang)[:, :, None, :]
    xr = x[..., :ROPE_DIM].astype(jnp.float32)
    x1, x2 = xr[..., :half], xr[..., half:]
    rot = jnp.concatenate([x1 * cos - x2 * sin, x2 * cos + x1 * sin], axis=-1)
    return jnp.concatenate([rot.astype(x.dtype), x[..., ROPE_DIM:]], axis=-1)

def dsa_attention(q, k, v, qi, ki, wi):
    B, S = q.shape[0], q.shape[1]
    topk = min(TOPK_MAX, S // 4)
    nb = S // Q_BLOCK
    G = N_KV_HEADS
    R = N_HEADS // N_KV_HEADS
    key_chunk = jnp.arange(S) // CHUNK

    def to_blocks(a):
        return jnp.moveaxis(a.reshape((B, nb, Q_BLOCK) + a.shape[2:]), 1, 0)

    q_b = to_blocks(q.reshape(B, S, G, R, HEAD_DIM))
    qi_b = to_blocks(qi)
    wi_b = to_blocks(wi)
    t_b = jnp.arange(S).reshape(nb, Q_BLOCK)

    def block(args):
        qb, qib, wib, tb = args
        q_chunk = tb // CHUNK
        allowed = key_chunk[None, :] <= q_chunk[:, None]
        logits = jnp.einsum('bqhd,bsd->bqhs', qib, ki)
        score = jnp.einsum('bqhs,bqh->bqs', jax.nn.relu(logits), wib).astype(jnp.float32)
        score = jnp.where(allowed[None], score, -jnp.inf)
        _, idx = lax.top_k(score, topk)
        k_sel = jax.vmap(lambda kb, ib: kb[ib])(k, idx)
        v_sel = jax.vmap(lambda vb, ib: vb[ib])(v, idx)
        valid = key_chunk[idx] <= q_chunk[None, :, None]
        s = jnp.einsum('bqgrd,bqkgd->bqgrk', qb, k_sel).astype(jnp.float32) * (HEAD_DIM ** -0.5)
        s = jnp.where(valid[:, :, None, None, :], s, -jnp.inf)
        pr = jax.nn.softmax(s, axis=-1).astype(v.dtype)
        return jnp.einsum('bqgrk,bqkgd->bqgrd', pr, v_sel)

    out = lax.map(block, (q_b, qi_b, wi_b, t_b))
    return jnp.moveaxis(out, 0, 1).reshape(B, S, ATTN_WIDTH)

def spatial_gating(u, v, w_s, b_s, g, bta):
    B, S = u.shape[0], u.shape[1]
    v = layer_norm_2(v, g, bta)
    nc = S // SGU_CHUNK
    vb = v.reshape(B, nc, SGU_CHUNK, SGU_GROUPS, SGU_GROUP_DIM)
    tri = jnp.tril(jnp.ones((SGU_CHUNK, SGU_CHUNK), dtype=bool))
    w = jnp.where(tri[None], w_s, jnp.zeros_like(w_s))
    mixed = jnp.einsum('gts,bcsgd->bctgd', w, vb) + jnp.swapaxes(b_s, 0, 1)[None, None, :, :, None]
    return u * mixed.reshape(B, S, SGU_WIDTH)

def second_inputs(seed: int = 0) -> dict:
    key = jax.random.key(seed)
    ks = jax.random.split(key, 20)

    def nrm(k, shape, scale):
        return jax.random.normal(k, shape, jnp.float32) * scale

    x = nrm(ks[0], (BATCH, SEQ, D_MODEL), 1.0)
    p = nrm(ks[1], (DEPTH, BATCH, SEQ, PLE_DIM), 1.0)
    start = jax.random.randint(ks[2], (BATCH, 1), 0, 64, dtype=jnp.int32) * CHUNK
    positions = (start + jnp.arange(SEQ, dtype=jnp.int32)[None, :]).astype(jnp.int32)
    return {
        "x": x,
        "p": p,
        "positions": positions,
        "w_in": nrm(ks[3], (DEPTH, D_MODEL, IN_COLS), D_MODEL ** -0.5),
        "w_o": nrm(ks[4], (DEPTH, D_MODEL, D_MODEL), BETA * D_MODEL ** -0.5),
        "ln1_g": 1.0 + nrm(ks[5], (DEPTH, D_MODEL), 0.02),
        "ln1_b": nrm(ks[6], (DEPTH, D_MODEL), 0.02),
        "ln2_g": 1.0 + nrm(ks[7], (DEPTH, D_MODEL), 0.02),
        "ln2_b": nrm(ks[8], (DEPTH, D_MODEL), 0.02),
        "sgu_w": nrm(ks[9], (DEPTH, SGU_GROUPS, SGU_CHUNK, SGU_CHUNK), SGU_CHUNK ** -0.5),
        "sgu_b": 1.0 + nrm(ks[10], (DEPTH, SGU_GROUPS, SGU_CHUNK), 0.02),
        "sgu_ln_g": 1.0 + nrm(ks[11], (DEPTH, SGU_WIDTH), 0.02),
        "sgu_ln_b": nrm(ks[12], (DEPTH, SGU_WIDTH), 0.02),
        "w_ffn_in": nrm(ks[13], (DEPTH, D_MODEL, 2 * D_FF_2), D_MODEL ** -0.5),
        "w_ffn_out": nrm(ks[14], (DEPTH, D_FF_2, D_MODEL), BETA * D_FF_2 ** -0.5),
        "w_ple": nrm(ks[15], (DEPTH, PLE_DIM, D_MODEL), PLE_DIM ** -0.5),
        "w_ple_gate": nrm(ks[16], (DEPTH, D_MODEL, D_MODEL), D_MODEL ** -0.5),
    }

def second_block(x, p, positions, w_in, w_o, ln1_g, ln1_b, ln2_g, ln2_b, sgu_w, sgu_b,
              sgu_ln_g, sgu_ln_b, w_ffn_in, w_ffn_out, w_ple, w_ple_gate):
    B, S = x.shape[0], x.shape[1]
    split_points = [int(o) for o in np.cumsum(IN_SPLITS)[:-1]]
    for i in range(DEPTH):
        h = x @ w_in[i]
        q, k, v, qi, ki, wi, u, vs = jnp.split(h, split_points, axis=-1)
        q = partial_rope(q.reshape(B, S, N_HEADS, HEAD_DIM), positions)
        k = partial_rope(k.reshape(B, S, N_KV_HEADS, HEAD_DIM), positions)
        v = v.reshape(B, S, N_KV_HEADS, HEAD_DIM)
        qi = partial_rope(qi.reshape(B, S, N_IDX_HEADS, IDX_DIM), positions)
        ki = partial_rope(ki.reshape(B, S, 1, IDX_DIM), positions)[:, :, 0]
        wi = wi * ((N_IDX_HEADS * IDX_DIM) ** -0.5)
        a_out = dsa_attention(q, k, v, qi, ki, wi)
        b_out = spatial_gating(jax.nn.gelu(u), jax.nn.gelu(vs), sgu_w[i], sgu_b[i],
                               sgu_ln_g[i], sgu_ln_b[i])
        mix = jnp.concatenate([a_out, b_out], axis=-1) @ w_o[i]
        x = layer_norm_2(ALPHA * x + mix, ln1_g[i], ln1_b[i])
        gate, up = jnp.split(x @ w_ffn_in[i], 2, axis=-1)
        ffn = (jax.nn.silu(gate) * up) @ w_ffn_out[i]
        ple = (p[i] @ w_ple[i]) * jax.nn.sigmoid(x @ w_ple_gate[i])
        x = layer_norm_2(ALPHA * x + ffn + ple, ln2_g[i], ln2_b[i])
    return x


def setup_inputs(seed=0):
    out = dict(first_inputs(seed))
    for name, value in second_inputs(seed + 1).items():
        if name != "x":
            out[name + "_2"] = value
    return out


def reference(
    x, positions, ln_mix_g, ln_mix_b, ln_ffn_g, ln_ffn_b, w_ff1, w_ff2, ssm_lam_re, ssm_lam_im,
    ssm_log_dt, ssm_b_re, ssm_b_im, ssm_c_re, ssm_c_im, ssm_d, ssm_w_glu, ssm_w_out, kv_w_a,
    kv_norm_g, kv_w_b, q_w_a, q_norm_g, q_w_b, attn_w_o, p_2, positions_2, w_in_2, w_o_2,
    ln1_g_2, ln1_b_2, ln2_g_2, ln2_b_2, sgu_w_2, sgu_b_2, sgu_ln_g_2, sgu_ln_b_2, w_ffn_in_2,
    w_ffn_out_2, w_ple_2, w_ple_gate_2,
):
    x = first_block(
        x, positions, ln_mix_g, ln_mix_b, ln_ffn_g, ln_ffn_b, w_ff1, w_ff2, ssm_lam_re,
        ssm_lam_im, ssm_log_dt, ssm_b_re, ssm_b_im, ssm_c_re, ssm_c_im, ssm_d, ssm_w_glu,
        ssm_w_out, kv_w_a, kv_norm_g, kv_w_b, q_w_a, q_norm_g, q_w_b, attn_w_o,
    )
    return second_block(
        x, p_2, positions_2, w_in_2, w_o_2, ln1_g_2, ln1_b_2, ln2_g_2, ln2_b_2, sgu_w_2,
        sgu_b_2, sgu_ln_g_2, sgu_ln_b_2, w_ffn_in_2, w_ffn_out_2, w_ple_2, w_ple_gate_2,
    )


_drawn_inputs = setup_inputs


def setup_inputs(seed=0):
    import zlib

    import numpy as np

    out = dict(_drawn_inputs(seed))
    spreads = {}
    factors = {'ssm_lam_re': 64.0,
     'ssm_lam_im': 39.944,
     'ssm_log_dt': 40.568,
     'ssm_b_re': 53.68,
     'ssm_b_im': 54.608,
     'ssm_c_re': 54.0,
     'ssm_c_im': 54.256,
     'kv_norm_g': 8.0,
     'q_norm_g': 8.0,
     'sgu_b_2': 22.421,
     'sgu_ln_g_2': 90.073,
     'sgu_ln_b_2': 92.844}
    for name, (base, spread) in spreads.items():
        noise = np.random.default_rng([zlib.crc32(name.encode()), seed]).standard_normal(out[name].shape)
        drawn = base * np.exp(spread * noise) if base else spread * noise
        out[name] = __import__('jax').numpy.asarray(drawn.astype(out[name].dtype))
    for name, factor in factors.items():
        out[name] = (out[name] * factor).astype(out[name].dtype)
    return out
```

```python
import math
from contextlib import ExitStack

import concourse.bass as bass
from concourse import mybir

F32 = mybir.dt.float32
F32R = mybir.dt.float32r
I32 = mybir.dt.int32
ALU = mybir.AluOpType
ACT = mybir.ActivationFunctionType
AX = mybir.AxisListType

P = 128
D = 1024
S = 512
TT = S // P
KD = D // P
FF1 = 4 * D
FF2 = 2816
NF2 = FF2 // P
DEPTH = 2
ALPHA = (2 * DEPTH) ** 0.25
LN_EPS, RMS_EPS = 1e-5, 1e-6
G, GC, NS = 64, 16, 64
L = 8
NC = S // L
Q = G // 2
NH, NOPE, ROPE, VH, QL, KVL = 8, 128, 64, 128, 384, 256
SM_SCALE = (NOPE + ROPE) ** -0.5
THETA1, THETA2 = 10000.0, 500000.0
HD, NI, TOPK, ROT = 64, 4, 128, 16
IN2 = 2116
SGW, SGG, PLE = 512, 8, 256
CAP = 2048
NEG = -1.0e30
TAKEN = -3.0e38
MAGIC = 12582912.0
TWO_PI = (6.28125, 0.0019350051879882812, 3.019916050e-07)
PI_IN = 3.1415925


def stages_of(w):
    def ap(x):
        return x

    out = []

    def add(name, n, cols, parts):
        out.append((name, n, cols, parts))

    def rows(x, k0, nk, c0, nc):
        return x[k0 * P:(k0 + nk) * P, c0:c0 + nc].rearrange("(k p) n -> p k n", p=P)

    def cols_at(x, j, step, base, width):
        v = x.rearrange("(k p) n -> p k n", p=P)
        if isinstance(j, int):
            return v[:, :, base + j * step:base + j * step + width]
        return v[:, :, bass.ds(j * step + base, width)]

    def channel(name, x, n, c0, c1, step):
        k = x.shape[0]
        add(name, n, 2 * k, lambda j: [(0, cols_at(x, j, step, c0, P)), (k, cols_at(x, j, step, c1, P))])

    def token(name, x, k0, nk, c0, nc):
        at = 0
        while at < nk:
            m = min(4 if nc > 256 else 8, nk - at)
            h = (m + 1) // 2
            add(name, 1, m * nc, lambda j, a=at, m=m, h=h: [
                (0, rows(x, k0 + a, h, c0, nc)), (h * nc, rows(x, k0 + a + h, m - h, c0, nc))])
            at += m

    channel("glu", w["ssm_w_glu"][0], KD, 0, D, P)
    for n in range(2):
        token("ssm_out", w["ssm_w_out"][0], 0, KD, 512 * n, 512)

    def relu_mlp(l):
        for half in range(2):
            c0 = half * FF1 // 2
            channel("ff_in", w["w_ff1"][l], 8, c0, c0 + P, 2 * P)
            for n in range(2):
                token("ff_out", w["w_ff2"][l], half * 16, 16, 512 * n, 512)

    relu_mlp(0)
    token("kv_a", w["kv_w_a"], 0, KD, 0, KVL + ROPE)
    token("q_a", w["q_w_a"][0], 0, KD, 0, QL)
    for c in range(2):
        add("kv_b", 1, 2048, lambda j, c=c: [(k * 1024, rows(w["kv_w_b"], k, 1, 1024 * c, 1024)) for k in range(2)])
    for c in range(4):
        add("q_b", 1, 1152, lambda j, c=c: [(0, rows(w["q_w_b"][0], 0, 2, 384 * c, 384)),
                                            (768, rows(w["q_w_b"][0], 2, 1, 384 * c, 384))])
    for n in range(2):
        token("attn_o", w["attn_w_o"][0], 0, KD, 512 * n, 512)
    relu_mlp(1)
    for l in range(2):
        wi = w["w_in_2"][l]
        for c0, nc in ((0, 512), (512, 512), (1024, 68), (1092, 512), (1604, 512)):
            token("w_in", wi, 0, KD, c0, nc)
        for n in range(2):
            token("w_o", w["w_o_2"][l], 0, KD, 512 * n, 512)
        for n in range(2):
            token("ple", w["w_ple_2"][l], 0, 2, 512 * n, 512)
            token("ple_gate", w["w_ple_gate_2"][l], 0, KD, 512 * n, 512)
        for half in range(2):
            channel("ffn_in", w["w_ffn_in_2"][l], 11, half * 11 * P, FF2 + half * 11 * P, P)
            for n in range(2):
                token("ffn_out", w["w_ffn_out_2"][l], half * 11, 11, 512 * n, 512)
    return out


def two_blocks(nc, w, out, last=99):
    stream = stages_of(w)
    chunk_cols = [c for _, n, c, _ in stream for _ in range(n)]
    n_chunks = len(chunk_cols)

    with ExitStack() as ctx:
        sems = {}

        def sem(name):
            if name not in sems:
                sems[name] = ctx.enter_context(nc.semaphore(name))
            return sems[name]

        base = -(-nc.sbuf_base // 32) * 32
        KB = 1024

        def at(name, kb, shape, dt=F32):
            return nc.alloc_sbuf_tensor_at(name, shape, dt, offset=base + int(kb * KB))

        ctx.enter_context(nc.sbuf_tensor("arena_fence", [P, 207 * 256], F32))
        raw = at("raw", 0, [P, 2, CAP])
        whi = at("whi", 16, [P, 2, CAP], F32R)
        wlo = at("wlo", 32, [P, 2, CAP], F32R)
        res = at("res", 48, [P, TT, D])
        xh = at("xh", 64, [P, KD, S], F32R)
        xl = at("xl", 80, [P, KD, S], F32R)
        lnp = at("lnp", 96, [P, 2, D])
        rt = at("rt", 104, [P, 1024])
        ft = at("ft", 108, [P, 1024])
        ident = at("ident", 112, [P, 240])
        causal = at("causal", 113, [P, 512])
        chunkm = at("chunkm", 115, [P, P])
        cos1 = at("cos1", 115.5, [P, TT, 32])
        sin1 = at("sin1", 116, [P, TT, 32])
        cos2 = at("cos2", 116.5, [P, TT, 8])
        sin2 = at("sin2", 116.625, [P, TT, 8])
        pw = at("pw", 116.75, [P, 2, 9, Q])
        bst = at("bst", 119, [P, TT, 2, 6])
        mv = at("mv", 119.25, [P, TT, 2])
        sd = at("sd", 119.375, [P, TT])
        rstd = at("rstd", 119.4375, [P, TT])
        m8 = at("m8", 119.5, [P, 8])
        nmax = at("nmax", 119.5625, [P, 2])
        rsum = at("rsum", 119.625, [P, 2])
        rinv = at("rinv", 119.6875, [P, 2])
        consts = at("consts", 119.75, [P, 4])
        kvg = at("kvg", 119.8125, [P, 2])
        qg = at("qg", 119.875, [P, 3])
        bsT = at("bsT", 119.9375, [P, SGG])
        ustep = at("ustep", 120, [P, P])
        AR = 120.5
        hidh = at("hidh", AR, [P, 16, S], F32R)
        hidl = at("hidl", AR + 32, [P, 16, S], F32R)
        xc = at("xc", AR, [NC, L, D])
        xg = at("xg", 64, [NC, G, L * GC])
        yg = at("yg", AR, [NC, L, D])
        ab = at("ab", AR + 32, [P, 2, Q, L, GC])
        tm = at("tm", AR + 32, [P, L, 2, Q, GC])
        mt = at("mt", AR + 64, [P, Q, P])
        ca = at("ca", AR + 64, [P, Q // 2, 2, L, GC])
        b_in = at("b_in", AR + 64, [P, 2, Q, GC])
        bb = at("bb", AR + 68, [P, 2, Q, GC])
        sc = at("sc", AR + 72, [P, 20, Q])
        lam = at("lam", AR + 76, [Q, 3, P])
        ldt = at("ldt", AR + 78, [Q, 2])
        cc = at("cc", AR + 80, [P, 2, Q, GC])
        cn = at("cn", 104, [P, 2, 8, 2, NS])
        kk = at("kk", 96, [P, 2, Q, GC])
        dbc = at("dbc", 100, [P, Q, 2, GC])
        uu = at("uu", 48, [P, G, NC])
        sst = at("sst", 64, [P, 2, Q, NC])
        hst = at("hst", 80, [P, 2, Q, NC])
        posi = at("posi", AR + 79, [P, 2, TT], I32)
        posf = at("posf", AR + 79.0625, [P, 2, TT])
        inv1 = at("inv1", AR + 79.125, [P, 32])
        inv2 = at("inv2", AR + 79.25, [P, 8])
        ang = at("ang", AR + 84, [P, 2, 160])
        ckv = at("ckv", AR, [P, TT, KVL + ROPE])
        cq = at("cq", AR + 5, [P, TT, QL])
        krd = at("krd", AR + 11, [P, TT, 2 * ROPE])
        junk = at("junk", AR + 13, [P, QL])
        kn = at("kn", AR, [P, NH, S])
        vv = at("vv", AR + 16, [P, TT, NH * VH])
        qn = at("qn", AR + 32, [P, NH, S])
        qrT = at("qrT", AR + 48, [P, NH // 2, S])
        krT = at("krT", AR + 56, [P, S])
        qrt = at("qrt", AR + 58, [P, TT, NH * ROPE])
        ckvh = at("ckvh", AR + 66, [P, 2, S], F32R)
        ckvl = at("ckvl", AR + 70, [P, 2, S], F32R)
        cqh = at("cqh", AR + 74, [P, 3, S], F32R)
        cql = at("cql", AR + 80, [P, 3, S], F32R)
        pn1 = at("pn1", AR + 58, [P, 2, S])
        pt1 = [at("pt1a", AR + 62, [P, TT, S]), at("pt1b", AR + 70, [P, TT, S])]
        sm1 = at("sm1", AR + 78, [P, 2, S])
        qT = at("qT", AR, [P, 4, S])
        kT = at("kT", AR + 8, [P, 2, S])
        qiT = at("qiT", AR + 12, [P, 2, S])
        kiT = at("kiT", AR + 16, [P, S])
        kvq = at("kvq", AR + 18, [P, TT, 512])
        qtok = at("qtok", AR + 26, [P, TT, 512])
        gu = at("gu", AR + 34, [P, TT, 512])
        vs = at("vs", AR + 42, [P, TT, 512])
        kiw = at("kiw", AR + 50, [P, TT, 68])
        kid = at("kid", AR + 52, [P, TT, 128])
        kdd = at("kdd", AR + 54, [P, TT, 256])
        mask = at("mask", AR + 58, [P, TT, S])
        scr = at("scr", AR + 66, [P, 3, S])
        pn2 = at("pn2", AR + 72, [P, 2, S])
        pt2 = [at("pt2a", AR + 26, [P, TT, S]), at("pt2b", AR + 76, [P, TT, S])]
        sm2 = at("sm2", AR + 54, [P, 2, S])
        rl = at("rl", AR + 76, [P, NI, S])
        wsn = at("wsn", 104, [P, SGG, P])
        wsT = at("wsT", 108, [P, SGG, P])
        sgp = at("sgp", 96, [P, 2, SGW])
        bsn = at("bsn", AR + 84, [SGG, P])
        pin = at("pin", AR + 64, [P, TT, PLE])
        pTh = at("pTh", AR + 68, [P, 2, S], F32R)
        pTl = at("pTl", AR + 72, [P, 2, S], F32R)
        plt = at("plt", AR + 76, [P, TT, 512])
        ps = ctx.enter_context(nc.psum_tensor("ps", [P, 8, 512], F32))

        landed = [sem("landed0"), sem("landed1")]
        hi_ready = sem("hi_ready")
        lo_ready = sem("lo_ready")
        chunk_used = sem("chunk_used")
        act_r = sem("act_r")
        dve_f = sem("dve_f")
        act_h = sem("act_h")
        dve_l = sem("dve_l")
        b_done = sem("b_done")
        b_free = [sem(f"b_free{t}") for t in range(TT)]

        def val(b, i, per):
            return b if i is None else i * per + b

        def pairs(eng, n, first, tail, body):
            m = (n - first - tail) // 2
            for j in range(first):
                body(j, None)
            if m > 1:
                with eng.Fori(0, m) as i:
                    body(first, i)
                    body(first + 1, i)
            else:
                m = 0
            for j in range(first + 2 * m, n):
                body(j, None)

        def f32(x):
            return x.bitcast(F32)

        block = ctx.enter_context(nc.Block())

        @block.sync
        def _(sp):
            sp.dma_start(xc[:], w["x"][0].rearrange("(c j) d -> c j d", j=L)).then_inc(sem("x_in"), 16)
            g = 0

            def load(g0, parts, cols, j, i):
                gg = g0 + j
                if gg >= 2:
                    sp.wait_ge(lo_ready, val(gg - 1, i, 2))
                s = gg % 2
                idx = j if i is None else i * 2 + j
                for c0, src in parts(idx):
                    k, m = src.shape[1], src.shape[2]
                    dst = raw[:, s, c0:c0 + k * m].rearrange("p (k n) -> p k n", k=k)
                    sp.dma_start(dst, src).then_inc(landed[s], 16)

            for name, n, cols, parts in stream:
                pairs(sp, n, 2 if g == 0 else 0, 0, lambda j, i: load(g, parts, cols, j, i))
                g += n
            sp.wait_ge(sem("ln_ok"), 4 * N_LN)
            for t in range(TT):
                sp.dma_start(out[0, t * P:(t + 1) * P, :], res[:, t, :]).then_inc(sem("stored"), 16)
            sp.wait_ge(sem("stored"), 16 * TT)

        @block.gpsimd
        def _(pool):
            seq = sem("pool_seq")
            n = [0]

            def link(ins):
                n[0] += 1
                ins.then_inc(seq, 1)
                pool.wait_ge(seq, n[0])

            def load(dst, src, name, slow=False):
                pool.dma_start(dst, src, allow_slow_non_contiguous=slow).then_inc(sem(name), 16)

            for i, nm in enumerate(("ssm_lam_re", "ssm_lam_im")):
                load(lam[:, i, :].rearrange("q (a p) -> q a p", a=2),
                     w[nm][0].rearrange("(q a) p -> q a p", a=2), "ssm_in")
            load(ldt[:], w["ssm_log_dt"][0].rearrange("(q a) -> q a", a=2), "ssm_in")
            for i, nm in enumerate(("ssm_b_re", "ssm_b_im")):
                load(b_in[:, i], w[nm][0].rearrange("(q a) p c -> (a p) q c", a=2), "ssm_in")
            for i, nm in enumerate(("ssm_c_re", "ssm_c_im")):
                for d in range(2):
                    load(cn[:, i, :, d, :], w[nm][0].rearrange("(n g) c p -> (g c) n p", g=8), "ssm_in")
            load(dbc[:].rearrange("p q a c -> p (q a c)"), w["ssm_d"][0].partition_broadcast(P), "ssm_in")
            for i, nm in enumerate(("positions", "positions_2")):
                load(posi[:, i, :], w[nm][0].rearrange("(t p) -> p t", p=P), "ssm_in", slow=True)
            load(kvg[:], w["kv_norm_g"].rearrange("(k p) -> p k", p=P), "ssm_in", slow=True)
            load(qg[:], w["q_norm_g"][0].rearrange("(k p) -> p k", p=P), "ssm_in", slow=True)
            link(pool.memset(ident[:], 0.0))
            link(pool.memset(causal[:], 0.0))
            link(pool.memset(chunkm[:], 0.0))
            link(pool.memset(ustep[:], 1.0))
            link(pool.affine_select(out=ustep[:], in_=ustep[:], compare_op=ALU.is_ge, fill=0.0, base=0,
                                    pattern=[[1, P]], channel_multiplier=-1))
            link(pool.affine_select(out=ident[:], in_=ident[:], compare_op=ALU.not_equal, fill=1.0, base=0,
                                    pattern=[[-1, 240]], channel_multiplier=1))
            link(pool.affine_select(out=causal[:, 384:512], in_=causal[:, 384:512], compare_op=ALU.is_ge,
                                    fill=NEG, base=0, pattern=[[-1, P]], channel_multiplier=1))
            link(pool.memset(chunkm[0:64, 64:128], NEG))
            for i, v in enumerate((LN_EPS, RMS_EPS, math.pi / 2)):
                link(pool.memset(consts[:, i:i + 1], v))
            for i in range(32):
                pool.memset(inv1[:, i:i + 1], THETA1 ** (-i / 32))
            for i in range(8):
                ins = pool.memset(inv2[:, i:i + 1], THETA2 ** (-2.0 * i / ROT))
            ins.then_inc(sem("pool_const"), 1)
            pool.wait_ge(sem("y_mm"), 16)
            for t in range(TT):
                load(res[:, t, :], w["x"][0, t * P:(t + 1) * P, :], "res_in")

            def ln_params(k, gname, bname, l):
                if k > 0:
                    pool.wait_ge(sem("ln_ok"), 4 * k)
                load(lnp[:, 0, :], w[gname][l].partition_broadcast(P), "lnp_in")
                load(lnp[:, 1, :], w[bname][l].partition_broadcast(P), "lnp_in")

            k = 0
            for l in range(2):
                ln_params(k, "ln_mix_g", "ln_mix_b", l)
                ln_params(k + 1, "ln_ffn_g", "ln_ffn_b", l)
                k += 2
            for l in range(2):
                pool.wait_ge(sem("ln_ok"), 4 * k)
                load(sgp[:, 0, :], w["sgu_ln_g_2"][l].partition_broadcast(P), "sgu_in")
                load(sgp[:, 1, :], w["sgu_ln_b_2"][l].partition_broadcast(P), "sgu_in")
                load(wsn[:], w["sgu_w_2"][l].rearrange("g t s -> t g s"), "sgu_in")
                load(bsn[:], w["sgu_b_2"][l], "sgu_in")
                pool.wait_ge(sem("vs_ok"), 4 * (l + 1))
                ln_sem = sem("lnp_in")
                load(lnp[:, 0, :], w["ln1_g_2"][l].partition_broadcast(P), "lnp_in")
                load(lnp[:, 1, :], w["ln1_b_2"][l].partition_broadcast(P), "lnp_in")
                pool.wait_ge(sem("ln_ok"), 4 * (k + 1))
                load(pin[:], w["p_2"][l, 0].rearrange("(t p) c -> p t c", p=P), "p_in")
                load(lnp[:, 0, :], w["ln2_g_2"][l].partition_broadcast(P), "lnp_in")
                load(lnp[:, 1, :], w["ln2_b_2"][l].partition_broadcast(P), "lnp_in")
                k += 2

        @block.tensor
        def _(pe):
            st = {"g": 0, "a": 0, "b": 0, "u": 0}

            def mm3(o, lh, ll, rh, rl, start, stop):
                pe.matmul(o, lh, rh, start=start, stop=False)
                pe.matmul(o, lh, rl, start=False, stop=False)
                return pe.matmul(o, ll, rh, start=False, stop=stop)

            def channel_major(n, k_tiles, ah, al, first):
                g0, a0 = st["g"], st["a"]

                def body(j, i):
                    s, pair = (g0 + j) % 2, (a0 + j) % 2
                    pe.wait_ge(lo_ready, val(g0 + j + 1, i, 2))
                    if a0 + j >= 2:
                        pe.wait_ge(dve_f, val(a0 + j - 1, i, 2))
                    for o in range(2):
                        for k in range(k_tiles):
                            c = (o * k_tiles + k) * P
                            ins = mm3(ps[:, 2 * pair + o, :], whi[:, s, c:c + P], wlo[:, s, c:c + P],
                                      ah[:, k, :], al[:, k, :], k == 0, k == k_tiles - 1)
                    ins.then_inc(chunk_used, 1)

                pairs(pe, n, first, 0, body)
                st["g"] += n
                st["a"] += n

            def token_major(k_tiles, width, ah, al, k0=0):
                k = 0
                while k < k_tiles:
                    s = st["g"] % 2
                    m = min(4 if width > 256 else 8, k_tiles - k)
                    pe.wait_ge(lo_ready, st["g"] + 1)
                    for t in range(TT):
                        if k == 0 and st["b"] > 0:
                            pe.wait_ge(b_free[t], st["b"])
                        for q in range(m):
                            ins = mm3(ps[:, 4 + t, 0:width], ah[:, k0 + k + q, t * P:(t + 1) * P],
                                      al[:, k0 + k + q, t * P:(t + 1) * P],
                                      whi[:, s, q * width:(q + 1) * width], wlo[:, s, q * width:(q + 1) * width],
                                      k + q == 0, k + q == k_tiles - 1)
                        if k + m == k_tiles and t < TT - 1:
                            ins.then_inc(b_done, 1)
                    ins.then_inc(chunk_used, 1)
                    st["g"] += 1
                    k += m
                st["b"] += 1

            def to_channels(k, src, ready):
                for t in range(TT):
                    pe.wait_ge(ready, 4 * k + t + 1)
                    if t >= 2:
                        pe.wait_ge(sem("xt_lo"), 4 * k + t - 1)
                    for c in range(KD):
                        ins = pe.transpose(ps[:, 2 * (t % 2) + c // 4, (c % 4) * P:(c % 4 + 1) * P],
                                           src[:, t, c * P:(c + 1) * P], ident[:, 0:P])
                    ins.then_inc(sem("xt_pe"), 1)

            def turn(name, parts):
                for n, piece in enumerate(parts):
                    if n >= 4:
                        pe.wait_ge(sem(name + "_rd"), n - 3)
                    for t in range(TT):
                        ins = pe.transpose(ps[:, n % 4, t * P:(t + 1) * P], piece(t), ident[:, 0:P])
                    ins.then_inc(sem(name + "_pe"), 1)

            pe.wait_ge(sem("ssm_in"), 16 * N_SSM_IN)
            pe.wait_ge(sem("pool_const"), 1)
            pe.wait_ge(sem("ldt_wide"), 1)
            for i in range(3):
                ins = pe.transpose(ps[:, 0, i * Q:(i + 1) * Q], lam[:, i, :], ident[0:Q, 0:Q])
            ins.then_inc(sem("lam_pe"), 1)
            for i in range(2):
                for n in range(8):
                    ins = pe.transpose(ps[:, 1 + 2 * i + n // 4, (n % 4) * P:(n % 4 + 1) * P],
                                       cn[:, i, n].rearrange("r d p -> r (d p)"), ident[:, 0:P])
            ins.then_inc(sem("c_pe"), 1)
            pe.wait_ge(sem("x_in"), 16)
            for n in range(8):
                if n == 1:
                    pe.wait_ge(sem("c_rd"), 4)
                if n >= 3:
                    pe.wait_ge(sem("u_rd"), n - 2)
                pe.wait_ge(sem("xg_ok"), n + 1)
                for gg in range(8):
                    ins = pe.transpose(ps[:, 5 + n % 3, gg * NC:(gg + 1) * NC], xg[:, 8 * n + gg, :],
                                       ident[0:NC, 0:NC])
                ins.then_inc(sem("u_pe"), 1)
            pe.wait_ge(sem("ab_ok"), 1)
            for a in range(2):
                for q in range(Q):
                    for r in range(2):
                        ins = pe.matmul(ps[:, 1 + a, q * GC:(q + 1) * GC], ab[a * NS:(a + 1) * NS, r, q],
                                        cc[a * NS:(a + 1) * NS, r, q, :], start=r == 0, stop=r == 1)
            ins.then_inc(sem("kk_pe"), 1)
            for r in range(2):
                for n in range(8):
                    if n >= 2 or r > 0:
                        pe.wait_ge(sem("mt_rd"), 8 * r + n - 1)
                    if n == 0 and r == 1:
                        pe.wait_ge(sem("s_pe"), 4)
                    for qq in range(4):
                        ins = pe.transpose(ps[:, 3 + n % 2, qq * P:(qq + 1) * P], ab[:, r, 4 * n + qq].rearrange("p j c -> p (j c)"),
                                           ident[:, 0:P])
                    ins.then_inc(sem("mt_pe"), 1)
                pe.wait_ge(sem("mt_rd"), 8 * (r + 1))
                pe.wait_ge(sem("u_rd"), 8)
                for n in range(4):
                    m = 4 * r + n
                    if m >= 2:
                        pe.wait_ge(sem("s_rd"), m - 1)
                    for qq in range(8):
                        q = 8 * n + qq
                        for a in range(2):
                            ins = pe.matmul(ps[a * NS:(a + 1) * NS, 5 + m % 2, qq * NC:(qq + 1) * NC],
                                            mt[:, q, a * NS:(a + 1) * NS], uu[:, 2 * q + a, :], start=True, stop=True)
                    ins.then_inc(sem("s_pe"), 1)
            pe.wait_ge(sem("kk_ok"), 1)
            for i in range(L):
                for a in range(2):
                    n = 2 * i + a
                    if n >= 2:
                        pe.wait_ge(sem("tm_rd"), n - 1)
                    pe.matmul(ps[:, 1 + n % 2, :], ident[:, (L - 1 - i) * GC:(L - 1 - i) * GC + P],
                              kk[:, a].rearrange("p q c -> p (q c)"), start=True, stop=True).then_inc(sem("tm_pe"), 1)
            for hf in range(2):
                pe.wait_ge(sem("ca_ok"), hf + 1)
                if hf == 0:
                    pe.wait_ge(sem("scan"), 6 * (NC - 1))
                    pe.wait_ge(sem("tm_rd"), 16)
                for n in range(8):
                    m = 8 * hf + n
                    if m >= 2:
                        pe.wait_ge(sem("y_rd"), m - 1)
                    for a in range(2):
                        for qq in range(2):
                            ql = 2 * n + qq
                            q = 16 * hf + ql
                            o = ps[0:NC, 2 * (m % 2) + a, qq * P:(qq + 1) * P]
                            for r in range(2):
                                pe.matmul(o, hst[a * NS:(a + 1) * NS, r, q, :], ca[a * NS:(a + 1) * NS, ql, r],
                                          start=r == 0, stop=False)
                            ins = pe.matmul(o, uu[:, 2 * q + a, :], tm[:, :, a, q, :], start=False, stop=True)
                    ins.then_inc(sem("y_mm"), 1)
            pe.wait_ge(sem("y_rd"), 16)
            for c in range(KD):
                if c >= 4:
                    pe.wait_ge(sem("yt_lo"), c - 3)
                for j in range(L):
                    ins = pe.transpose(ps[:, c % 4, j * NC:(j + 1) * NC], yg[:, j, c * P:(c + 1) * P], ident[0:NC, 0:NC])
                ins.then_inc(sem("yt_pe"), 1)
            pe.wait_ge(sem("yt_lo"), KD)

            def relu_mlp(k):
                pe.wait_ge(sem("xt_lo"), 4 * k)
                for half in range(2):
                    channel_major(8, KD, xh, xl, 0)
                    pe.wait_ge(dve_l, st["a"])
                    for n in range(2):
                        token_major(16, 512, hidh, hidl)

            channel_major(KD, KD, xh, xl, 2)
            pe.wait_ge(dve_l, st["a"])
            for n in range(2):
                token_major(KD, 512, hidh, hidl)
            to_channels(0, res, sem("ln_ok"))
            relu_mlp(1)
            to_channels(1, res, sem("ln_ok"))

            pe.wait_ge(sem("xt_lo"), 8)
            token_major(KD, KVL + ROPE, xh, xl)
            token_major(KD, QL, xh, xl)
            pe.wait_ge(sem("rms_ok"), 1)
            turn("lat", [lambda t, c=c: ckv[:, t, c * P:(c + 1) * P] for c in range(2)]
                 + [lambda t, c=c: cq[:, t, c * P:(c + 1) * P] for c in range(3)] + [lambda t: krd[:, t, :]])
            pe.wait_ge(sem("lat_rd"), 6)
            for c in range(2):
                s = st["g"] % 2
                pe.wait_ge(lo_ready, st["g"] + 1)
                if c > 0:
                    pe.wait_ge(sem("kn_rd"), c)
                for h in range(4):
                    for k in range(2):
                        o = k * 1024 + h * 256
                        ins = mm3(ps[:, h, :], whi[:, s, o:o + P], wlo[:, s, o:o + P], ckvh[:, k, :], ckvl[:, k, :],
                                  k == 0, k == 1)
                ins.then_inc(sem("kn_pe"), 1)
                if c > 0:
                    pe.wait_ge(sem("v_rd"), c)
                else:
                    for t in range(TT):
                        pe.wait_ge(b_free[t], st["b"])
                for t in range(TT):
                    for k in range(2):
                        def part(x):
                            v = x[:, s, k * 1024:(k + 1) * 1024].rearrange("p (h n) -> p h n", h=4)
                            return v[:, :, NOPE:NOPE + VH]
                        ins = mm3(ps[:, 4 + t, :], ckvh[:, k, t * P:(t + 1) * P], ckvl[:, k, t * P:(t + 1) * P],
                                  part(whi), part(wlo), k == 0, k == 1)
                ins.then_inc(chunk_used, 1)
                st["g"] += 1
            for c in range(4):
                s = st["g"] % 2
                pe.wait_ge(lo_ready, st["g"] + 1)
                if c == 0:
                    pe.wait_ge(sem("kn_rd"), 2)
                    pe.wait_ge(sem("v_rd"), 2)
                if c >= 2:
                    pe.wait_ge(sem("qn_rd"), c - 1)
                    pe.wait_ge(sem("qr_rd"), c - 1)
                for h in range(2):
                    for k in range(3):
                        o = k * 384 + h * 192
                        mm3(ps[:, 2 * (c % 2) + h, :], whi[:, s, o:o + P], wlo[:, s, o:o + P], cqh[:, k, :],
                            cql[:, k, :], k == 0, k == 2)
                for t in range(TT):
                    for k in range(3):
                        def part(x):
                            v = x[:, s, k * 384:(k + 1) * 384].rearrange("p (h n) -> p h n", h=2)
                            return v[:, :, NOPE:NOPE + ROPE]
                        ins = mm3(ps[:, 4 + c % 2, t * P:(t + 1) * P], cqh[:, k, t * P:(t + 1) * P],
                                  cql[:, k, t * P:(t + 1) * P], part(whi), part(wlo), k == 0, k == 2)
                ins.then_inc(chunk_used, 1)
                st["g"] += 1
            pe.wait_ge(sem("qrope_ok"), TT)
            pe.wait_ge(sem("qn_rd"), 4)
            turn("qrt", [lambda t, c=c: qrt[:, t, c * P:(c + 1) * P] for c in range(4)])
            pe.wait_ge(sem("qrt_rd"), 4)

            def attention(name, score, value, pt, per):
                units = [(h, t) for h in range(NH) for t in range(TT)]

                def scores(u):
                    if u >= 2:
                        pe.wait_ge(sem(name + "_s_rd"), u - 1)
                    score(*units[u], ps[:, u % 2, 0:(units[u][1] + 1) * P]).then_inc(sem(name + "_s"), 1)

                scores(0)
                for u, (h, t) in enumerate(units):
                    if u + 1 < len(units):
                        scores(u + 1)
                    pe.wait_ge(sem(name + "_pn"), u + 1)
                    if u >= 2:
                        pe.wait_ge(sem(name + "_pt"), u - 1)
                    for b in range(t + 1):
                        ins = pe.transpose(ps[:, 2 + u % 2, b * P:(b + 1) * P], pt[2][:, u % 2, b * P:(b + 1) * P],
                                           ident[:, 0:P])
                    ins.then_inc(sem(name + "_tp"), 1)
                    if t == TT - 1:
                        pe.wait_ge(sem(name + "_pt"), u + 1)
                        n = h // per
                        if h % per == 0 and n >= 2:
                            pe.wait_ge(sem(name + "_o_lo"), n - 1)
                        r0 = (h % per) * (P // per)
                        for b in range(TT):
                            ins = pe.matmul(ps[r0:r0 + P // per, 4 + n % 2, b * P:S], value(h, b),
                                            pt[h % 2][:, b, b * P:S], start=b == 0, stop=b == TT - 1)
                        ins.then_inc(sem(name + "_o"), 1)

            def mla_score(h, t, o):
                n = (t + 1) * P
                r = (h % 2) * ROPE
                pe.matmul(o, qn[:, h, t * P:(t + 1) * P], kn[:, h, 0:n], start=True, stop=False)
                return pe.matmul(o, qrT[r:r + ROPE, h // 2, t * P:(t + 1) * P], krT[r:r + ROPE, 0:n],
                                 start=False, stop=True)

            attention("mla", mla_score, lambda h, b: vv[:, b, h * VH:(h + 1) * VH], pt1 + [pn1], 1)
            pe.wait_ge(sem("mla_o_lo"), NH)
            for n in range(2):
                token_major(KD, 512, xh, xl)
            to_channels(2, res, sem("ln_ok"))
            relu_mlp(3)
            to_channels(3, res, sem("ln_ok"))

            for l in range(2):
                kx = 4 + 2 * l
                nm = f"dsa{l}"
                pe.wait_ge(sem("xt_lo"), 4 * kx)
                for width in (512, 512, 68, 512, 512):
                    token_major(KD, width, xh, xl)
                pe.wait_ge(sem("rope2_ok"), l + 1)
                turn(f"in{l}", [lambda t, c=c: qtok[:, t, c * P:(c + 1) * P] for c in range(4)]
                     + [lambda t, c=c: kdd[:, t, c * P:(c + 1) * P] for c in range(2)]
                     + [lambda t, c=c: kvq[:, t, 256 + c * P:256 + (c + 1) * P] for c in range(2)]
                     + [lambda t: kid[:, t, :]])
                pe.wait_ge(sem(f"in{l}_rd"), 9)
                for t in range(1, TT):
                    n = (t + 1) * P
                    for h in range(NI):
                        if t >= 2:
                            pe.wait_ge(sem("lg_rd"), 4 * (3 * l + t - 2) + h + 1)
                        r = (h % 2) * IXD
                        pe.matmul(ps[:, h, 0:n], qiT[r:r + IXD, h // 2, t * P:(t + 1) * P], kiT[r:r + IXD, 0:n],
                                  start=True, stop=True).then_inc(sem("lg_pe"), 1)
                pe.wait_ge(sem("sgu_in"), 64 * (l + 1))
                for t in range(TT):
                    pe.wait_ge(b_free[t], st["b"])
                for g in range(SGG):
                    ins = pe.transpose(ps[:, 4 + g // 4, (g % 4) * P:(g % 4 + 1) * P], wsn[:, g, :], ident[:, 0:P])
                ins.then_inc(sem("ws_pe"), 1)
                pe.transpose(ps[:, 6, 0:SGG], bsn[:], ident[0:SGG, 0:SGG]).then_inc(sem("ws_pe"), 1)
                pe.wait_ge(sem("ws_ok"), l + 1)
                pe.wait_ge(sem("vs_ok"), 4 * (l + 1))
                for g in range(SGG):
                    ins = pe.matmul(ps[:, 4 + g // 2, (g % 2) * 256:(g % 2 + 1) * 256], wsT[:, g, :],
                                    vs[:, :, g * 64:(g + 1) * 64], start=True, stop=True)
                ins.then_inc(sem("sg_pe"), 1)
                pe.wait_ge(sem("lg_rd"), 12 * (l + 1))
                pe.wait_ge(sem("bo_ok"), l + 1)
                turn(f"bo{l}", [lambda t, c=c: gu[:, t, c * P:(c + 1) * P] for c in range(4)])
                pe.wait_ge(sem(f"bo{l}_rd"), 4)

                def dsa_score(h, t, o):
                    r = (h % 2) * HD
                    return pe.matmul(o, qT[r:r + HD, h // 2, t * P:(t + 1) * P], kT[r:r + HD, h // 4, 0:(t + 1) * P],
                                     start=True, stop=True)

                attention(nm, dsa_score, lambda h, b: kvq[:, b, 128 + (h // 4) * HD:128 + (h // 4 + 1) * HD],
                          pt2 + [pn2], 2)
                pe.wait_ge(sem(nm + "_o_lo"), 4)
                for n in range(2):
                    token_major(KD, 512, xh, xl)
                to_channels(kx, res, sem("ln_ok"))
                pe.wait_ge(sem("p_in"), 16 * (l + 1))
                pe.wait_ge(sem("xt_lo"), 4 * (kx + 1))
                turn(f"pt{l}", [lambda t, c=c: pin[:, t, c * P:(c + 1) * P] for c in range(2)])
                pe.wait_ge(sem(f"pt{l}_rd"), 2)
                for n in range(2):
                    token_major(2, 512, pTh, pTl)
                    token_major(KD, 512, xh, xl)
                for half in range(2):
                    channel_major(11, KD, xh, xl, 0)
                    pe.wait_ge(dve_l, st["a"])
                    for n in range(2):
                        token_major(11, 512, hidh, hidl)
                if l == 0:
                    to_channels(kx + 1, res, sem("ln_ok"))

        @block.scalar
        def _(act):
            st = {"g": 0, "a": 0, "b": 0, "s": 0}
            seq = sem("act_seq")

            def link(ins):
                st["s"] += 1
                ins.then_inc(seq, 1)
                act.wait_ge(seq, st["s"])

            def split(g, i=None):
                if g >= n_chunks:
                    return
                s, n = g % 2, chunk_cols[g]
                act.wait_ge(landed[s], val(32 * (g // 2 + 1), i, 32))
                if g >= 2:
                    act.wait_ge(chunk_used, val(g - 1, i, 2))
                act.activation(whi[:, s, 0:n], raw[:, s, 0:n], ACT.Copy).then_inc(hi_ready, 1)

            def channel_major(n, kind, first):
                g0, a0 = st["g"], st["a"]
                tail = 0 if all(c == chunk_cols[g0] for c in chunk_cols[g0:g0 + n + 2]) else 2

                def body(j, i):
                    pair = (a0 + j) % 2
                    a = a0 + j
                    act.wait_ge(chunk_used, val(g0 + j + 1, i, 2))
                    if a >= 1:
                        act.wait_ge(dve_f, val(a, i, 2))
                    if kind == "relu2":
                        act.activation(rt[:], ps[:, 2 * pair:2 * pair + 2, :].rearrange("p b n -> p (b n)"),
                                       ACT.Relu).then_inc(act_r, 1)
                    elif kind == "glu":
                        act.activation(rt[:, 0:S], ps[:, 2 * pair + 1, :], ACT.Sigmoid).then_inc(act_r, 1)
                    else:
                        act.activation(rt[:, 0:S], ps[:, 2 * pair, :], ACT.Silu).then_inc(act_r, 1)
                    split(g0 + j + 2, i)
                    act.wait_ge(dve_f, val(a + 1, i, 2))
                    idx = j if i is None else i * 2 + j
                    if kind == "relu2":
                        o = hidh[:, 2 * j:2 * j + 2, :] if i is None else hidh[:, bass.ds(i * 4 + 2 * j, 2), :]
                        act.activation(o, ft[:].rearrange("p (b n) -> p b n", b=2), ACT.Copy).then_inc(act_h, 1)
                    else:
                        o = hidh[:, j:j + 1, :] if i is None else hidh[:, bass.ds(i * 2 + j, 1), :]
                        act.activation(o, ft[:, 0:S].rearrange("p (b n) -> p b n", b=1), ACT.Copy).then_inc(act_h, 1)

                pairs(act, n, first, tail, body)
                st["g"] += n
                st["a"] += n

            def token_major(k_tiles, width, evac=None, hold=False):
                k = 0
                while k < k_tiles:
                    m = min(4 if width > 256 else 8, k_tiles - k)
                    k += m
                    st["g"] += 1
                    if k == k_tiles:
                        if evac:
                            for t in range(TT):
                                if t < TT - 1:
                                    act.wait_ge(b_done, 3 * st["b"] + t + 1)
                                else:
                                    act.wait_ge(chunk_used, st["g"])
                                evac(t, ps[:, 4 + t, 0:width])
                        st["b"] += 1
                    if not (hold and k == k_tiles):
                        split(st["g"] + 1)

            def norm(k, last=False):
                for t in range(TT):
                    act.wait_ge(sem("ln_var"), 4 * k + t + 1)
                    act.activation(sd[:, t:t + 1], mv[:, t, 1:2], ACT.Sqrt, bias=consts[:, 0:1]).then_inc(sem("ln_sd"), 1)
                if not last:
                    for t in range(TT):
                        act.wait_ge(sem("xt_pe"), 4 * k + t + 1)
                        v = ps[:, 2 * (t % 2):2 * (t % 2) + 2, :].rearrange("p b (c n) -> p (b c) n", c=4)
                        act.activation(xh[:, :, t * P:(t + 1) * P], v, ACT.Copy).then_inc(sem("xt_hi"), 1)
                split(st["g"] + 1)

            def trig(sn, cs, r, absr):
                act.activation(sn, r, ACT.Sin)
                link(act.activation(absr, r, ACT.Abs))
                return act.activation(cs, absr, ACT.Sin, scale=-1.0, bias=consts[:, 2:3])

            act.wait_ge(sem("x_in"), 16)
            for n in range(8):
                act.activation(xg[:, 8 * n:8 * n + 8, :].rearrange("p g (j c) -> p g j c", j=L),
                               xc[:, :, n * P:(n + 1) * P].rearrange("p j (g c) -> p g j c", g=8),
                               ACT.Copy).then_inc(sem("xg_ok"), 1)
            split(0)
            split(1)
            act.wait_ge(sem("ssm_in"), 16 * N_SSM_IN)
            act.wait_ge(sem("pool_const"), 1)
            act.wait_ge(sem("lam_rd"), 1)
            act.activation(sc[:, 3, :], sc[:, 2, :], ACT.Exp).then_inc(sem("dt_ok"), 1)
            act.wait_ge(sem("ang_ok"), 2)
            act.activation(sc[:, 10, :], sc[:, 4, :], ACT.Exp).then_inc(sem("mag_ok"), 1)
            trig(sc[:, 8, :], sc[:, 9, :], sc[:, 6, :], sc[:, 7, :]).then_inc(sem("mag_ok"), 1)
            trig(sin1[:].rearrange("p t k -> p (t k)"), cos1[:].rearrange("p t k -> p (t k)"),
                 ang[:, 0, 0:128], ang[:, 1, 0:128])
            trig(sin2[:].rearrange("p t k -> p (t k)"), cos2[:].rearrange("p t k -> p (t k)"),
                 ang[:, 0, 128:160], ang[:, 1, 128:160]).then_inc(sem("trig_ok"), 1)
            for n in range(8):
                act.wait_ge(sem("u_pe"), n + 1)
                act.activation(uu[:, 8 * n:8 * n + 8, :], ps[:, 5 + n % 3, :].rearrange("p (g c) -> p g c", g=8),
                               ACT.Copy).then_inc(sem("u_rd"), 1)
            for r in range(2):
                for n in range(8):
                    act.wait_ge(sem("mt_pe"), 8 * r + n + 1)
                    act.activation(mt[:, 4 * n:4 * n + 4, :], ps[:, 3 + n % 2, :].rearrange("p (q c) -> p q c", q=4),
                                   ACT.Copy).then_inc(sem("mt_rd"), 1)
                for n in range(4):
                    m = 4 * r + n
                    act.wait_ge(sem("s_pe"), m + 1)
                    act.activation(sst[:, r, 8 * n:8 * n + 8, :],
                                   ps[:, 5 + m % 2, :].rearrange("p (q c) -> p q c", q=8),
                                   ACT.Copy).then_inc(sem("s_rd"), 1)
            for n in range(16):
                act.wait_ge(sem("tm_pe"), n + 1)
                act.activation(tm[:, n // 2, n % 2], ps[:, 1 + n % 2, :].rearrange("p (q c) -> p q c", q=Q),
                               ACT.Copy).then_inc(sem("tm_rd"), 1)
            for m in range(16):
                act.wait_ge(sem("y_mm"), m + 1)
                for a in range(2):
                    q0 = 2 * m
                    o = yg[:, :, q0 * 32:q0 * 32 + 64].rearrange("p j (q a c) -> p q a j c", q=2, a=2)[:, :, a]
                    v = ps[0:NC, 2 * (m % 2) + a, 0:256].rearrange("p (q j c) -> p q j c", q=2, j=L)
                    ins = act.activation(o, v, ACT.Gelu_apprx_tanh)
                ins.then_inc(sem("y_rd"), 1)
            for c in range(KD):
                act.wait_ge(sem("yt_pe"), c + 1)
                act.activation(xh[:, c, :].rearrange("p (n j) -> p n j", j=L),
                               ps[:, c % 4, :].rearrange("p (j n) -> p n j", j=L), ACT.Copy).then_inc(sem("yt_hi"), 1)

            def relu_mlp(last_k):
                for half in range(2):
                    channel_major(8, "relu2", 0)
                    for n in range(2):
                        token_major(16, 512, hold=half == 1 and n == 1)
                norm(last_k)

            channel_major(KD, "glu", 2)
            token_major(KD, 512)
            token_major(KD, 512, hold=True)
            norm(0)
            relu_mlp(1)

            def keep(dst):
                def evac(t, src):
                    act.activation(dst(t), src, ACT.Copy).then_inc(b_free[t], 1)
                return evac

            token_major(KD, KVL + ROPE, keep(lambda t: ckv[:, t, :]))
            token_major(KD, QL, keep(lambda t: cq[:, t, :]))
            for t in range(TT):
                act.wait_ge(b_free[t], st["b"])
            for t in range(TT):
                link(act.activation(junk[:, 0:KVL], ckv[:, t, 0:KVL], ACT.Square, accum_out=mv[:, t, 0:1]))
                link(act.activation(junk[:], cq[:, t, :], ACT.Square, accum_out=mv[:, t, 1:2]))
            link(act.activation(bst[:, :, 0, 0:1], mv[:, :, 0:1], ACT.Sqrt, scale=1.0 / KVL, bias=consts[:, 1:2]))
            act.activation(bst[:, :, 1, 0:1], mv[:, :, 1:2], ACT.Sqrt, scale=1.0 / QL, bias=consts[:, 1:2])\
               .then_inc(sem("rms_sd"), 1)
            for n, (dst, g) in enumerate([(ckvh[:, c, :], kvg[:, c:c + 1]) for c in range(2)]
                                         + [(cqh[:, c, :], qg[:, c:c + 1]) for c in range(3)]):
                act.wait_ge(sem("lat_pe"), n + 1)
                act.activation(dst, ps[:, n % 4, :], ACT.Identity, scale=g).then_inc(sem("lat_hi"), 1)
            for c in range(2):
                st["g"] += 1
                act.wait_ge(sem("kn_pe"), c + 1)
                act.activation(kn[:, 4 * c:4 * c + 4, :], ps[:, 0:4, :], ACT.Copy).then_inc(sem("kn_rd"), 1)
                split(st["g"] + 1)
            for c in range(4):
                st["g"] += 1
                act.wait_ge(chunk_used, st["g"])
                act.activation(qrt[:, :, c * P:(c + 1) * P], ps[:, 4 + c % 2, :].rearrange("p (t n) -> p t n", t=TT),
                               ACT.Copy).then_inc(sem("qr_rd"), 1)
                split(st["g"] + 1)
            for n in range(4):
                act.wait_ge(sem("qrt_pe"), n + 1)
                act.activation(qrT[:, n, :], ps[:, n % 4, :], ACT.Copy).then_inc(sem("qrt_rd"), 1)

            def attention(name, scale, sm, pt, per, dst):
                for u in range(NH * TT):
                    h, t = u // TT, u % TT
                    n = (t + 1) * P
                    act.wait_ge(sem(name + "_mx"), u + 1)
                    if u >= 2:
                        act.wait_ge(sem(name + "_tp"), u - 1)
                    act.activation(pt[2][:, u % 2, 0:n], sm[:, u % 2, 0:n], ACT.Exp, scale=scale,
                                   bias=nmax[:, u % 2:u % 2 + 1],
                                   accum_out=rsum[:, u % 2:u % 2 + 1]).then_inc(sem(name + "_e"), 1)
                    for v in ([u - 1] if u >= 1 else []) + ([u] if u == NH * TT - 1 else []):
                        h, t = v // TT, v % TT
                        act.wait_ge(sem(name + "_tp"), v + 1)
                        if t == 0 and h >= 2:
                            act.wait_ge(sem(name + "_o"), h - 1)
                        act.activation(pt[h % 2][:, 0:t + 1, t * P:(t + 1) * P],
                                       ps[:, 2 + v % 2, 0:(t + 1) * P].rearrange("p (b n) -> p b n", n=P),
                                       ACT.Copy).then_inc(sem(name + "_pt"), 1)
                        if t == TT - 1 and h >= per and h % per == per - 1:
                            n0 = h // per - 1
                            act.wait_ge(sem(name + "_o"), (n0 + 1) * per)
                            act.activation(xh[:, dst + n0, :], ps[:, 4 + n0 % 2, :], ACT.Copy).then_inc(sem(name + "_o_hi"), 1)
                n0 = NH // per - 1
                act.wait_ge(sem(name + "_o"), NH)
                act.activation(xh[:, dst + n0, :], ps[:, 4 + n0 % 2, :], ACT.Copy).then_inc(sem(name + "_o_hi"), 1)

            attention("mla", SM_SCALE, sm1, pt1 + [pn1], 1, 0)
            token_major(KD, 512)
            token_major(KD, 512, hold=True)
            norm(2)
            relu_mlp(3)

            for l in range(2):
                kx = 4 + 2 * l
                token_major(KD, 512, keep(lambda t: qtok[:, t, :]))
                token_major(KD, 512, keep(lambda t: kvq[:, t, :]))
                token_major(KD, 68, keep(lambda t: kiw[:, t, :]))

                def gelu(dst, name):
                    def evac(t, src):
                        act.activation(dst[:, t, :], src, ACT.Gelu_apprx_tanh).then_inc(b_free[t], 1)
                    return evac
                token_major(KD, 512, gelu(gu, "gu"))
                token_major(KD, 512, gelu(vs, "vs"))
                for n, dst in enumerate([qT[:, c, :] for c in range(4)] + [kT[:, c, :] for c in range(2)]
                                        + [qiT[:, c, :] for c in range(2)] + [kiT[:]]):
                    act.wait_ge(sem(f"in{l}_pe"), n + 1)
                    act.activation(dst, ps[:, n % 4, :], ACT.Copy).then_inc(sem(f"in{l}_rd"), 1)
                for t in range(1, TT):
                    for h in range(NI):
                        m = 4 * (3 * l + t - 1) + h
                        act.wait_ge(sem("lg_pe"), m + 1)
                        if t >= 2:
                            act.wait_ge(sem("sc_ok"), 4 * (3 * l + t - 2) + h + 1)
                        act.activation(rl[:, h, 0:(t + 1) * P], ps[:, h, 0:(t + 1) * P], ACT.Relu).then_inc(sem("lg_rd"), 1)
                for t in range(TT):
                    act.wait_ge(sem("vs_var"), 4 * l + t + 1)
                    act.activation(sd[:, t:t + 1], mv[:, t, 1:2], ACT.Sqrt, bias=consts[:, 0:1]).then_inc(sem("vs_sd"), 1)
                act.wait_ge(sem("ws_pe"), 2 * l + 1)
                act.activation(wsT[:], ps[:, 4:6, :].rearrange("p b (g n) -> p (b g) n", n=P), ACT.Copy)\
                   .then_inc(sem("ws_rd"), 1)
                for n in range(4):
                    act.wait_ge(sem(f"bo{l}_pe"), n + 1)
                    act.activation(xh[:, 4 + n, :], ps[:, n, :], ACT.Copy).then_inc(sem(f"bo{l}_hi"), 1)
                attention(f"dsa{l}", HD ** -0.5, sm2, pt2 + [pn2], 2, 0)
                token_major(KD, 512)
                token_major(KD, 512, hold=True)
                norm(kx)
                for n in range(2):
                    act.wait_ge(sem(f"pt{l}_pe"), n + 1)
                    act.activation(pTh[:, n, :], ps[:, n, :], ACT.Copy).then_inc(sem(f"pt{l}_hi"), 1)
                for n in range(2):
                    def ple_evac(t, src, n=n):
                        if n == 1:
                            act.wait_ge(sem("pg_ok"), 8 * l + t + 1)
                        act.activation(plt[:, t, :], src, ACT.Copy).then_inc(b_free[t], 1)

                    def gate_evac(t, src, n=n):
                        m = 8 * l + 4 * n + t
                        if m >= 2:
                            act.wait_ge(sem("pg_ok"), m - 1)
                        act.activation((rt, ft)[t % 2][:, 0:512], src, ACT.Sigmoid).then_inc(sem("pg_sig"), 1)

                    token_major(2, 512, ple_evac)
                    token_major(KD, 512, gate_evac)
                act.wait_ge(sem("pg_ok"), 8 * (l + 1))
                for half in range(2):
                    channel_major(11, "swiglu", 0)
                    for n in range(2):
                        token_major(11, 512, hold=half == 1 and n == 1)
                norm(kx + 1, last=l == 1)

        @block.vector
        def _(dve):
            st = {"g": 0, "a": 0, "b": 0, "s": 0}
            seq = sem("dve_seq")

            def link(ins):
                st["s"] += 1
                ins.then_inc(seq, 1)
                dve.wait_ge(seq, st["s"])

            def split(g, i=None):
                if g >= n_chunks:
                    return
                s, n = g % 2, chunk_cols[g]
                dve.wait_ge(hi_ready, val(g + 1, i, 2))
                dve.tensor_tensor(wlo[:, s, 0:n], raw[:, s, 0:n], f32(whi[:, s, 0:n]), ALU.subtract).then_inc(lo_ready, 1)

            def channel_major(n, kind, first):
                g0, a0 = st["g"], st["a"]
                tail = 0 if all(c == chunk_cols[g0] for c in chunk_cols[g0:g0 + n + 2]) else 2

                def body(j, i):
                    pair = (a0 + j) % 2
                    a = a0 + j
                    dve.wait_ge(act_r, val(a + 1, i, 2))
                    if a >= 1:
                        dve.wait_ge(act_h, val(a, i, 2))
                        dve.wait_ge(dve_l, val(a, i, 2))
                    if kind == "relu2":
                        dve.tensor_tensor(ft[:], rt[:], rt[:], ALU.mult).then_inc(dve_f, 1)
                    elif kind == "glu":
                        dve.tensor_tensor(ft[:, 0:S], rt[:, 0:S], ps[:, 2 * pair, :], ALU.mult).then_inc(dve_f, 1)
                    else:
                        dve.tensor_tensor(ft[:, 0:S], rt[:, 0:S], ps[:, 2 * pair + 1, :], ALU.mult).then_inc(dve_f, 1)
                    split(g0 + j + 2, i)
                    dve.wait_ge(act_h, val(a + 1, i, 2))
                    if kind == "relu2":
                        sl = slice(2 * j, 2 * j + 2) if i is None else bass.ds(i * 4 + 2 * j, 2)
                        v = ft[:].rearrange("p (b n) -> p b n", b=2)
                    else:
                        sl = slice(j, j + 1) if i is None else bass.ds(i * 2 + j, 1)
                        v = ft[:, 0:S].rearrange("p (b n) -> p b n", b=1)
                    dve.tensor_tensor(hidl[:, sl, :], v, f32(hidh[:, sl, :]), ALU.subtract).then_inc(dve_l, 1)

                pairs(dve, n, first, tail, body)
                st["g"] += n
                st["a"] += n

            def token_major(k_tiles, width, evac=None, hold=False):
                k = 0
                while k < k_tiles:
                    m = min(4 if width > 256 else 8, k_tiles - k)
                    k += m
                    st["g"] += 1
                    if k == k_tiles:
                        if evac:
                            for t in range(TT):
                                if t < TT - 1:
                                    dve.wait_ge(b_done, 3 * st["b"] + t + 1)
                                else:
                                    dve.wait_ge(chunk_used, st["g"])
                                evac(t, ps[:, 4 + t, 0:width])
                        st["b"] += 1
                    if not (hold and k == k_tiles):
                        split(st["g"] + 1)

            def add_to_res(n, alpha, then=None):
                def evac(t, src):
                    r = res[:, t, 512 * n:512 * n + 512]
                    if st["b"] > 0:
                        dve.wait_ge(b_free[t], st["b"])
                    dve.scalar_tensor_tensor(out=r, in0=r, scalar=alpha, in1=src, op0=ALU.mult, op1=ALU.add)\
                       .then_inc(b_free[t], 1)
                    if then:
                        dve.wait_ge(b_free[t], st["b"] + 1)
                        then(t)
                return evac

            def stats(x, t, width, name):
                for h in range(width // 512):
                    link(dve.bn_stats(bst[:, t, h, :], x[:, t, 512 * h:512 * h + 512]))
                dve.bn_aggr(mv[:, t, :], bst[:, t, 0:width // 512, :].rearrange("p h k -> p (h k)")).then_inc(sem(name), 1)

            def ln_stats(k):
                return lambda t: stats(res, t, D, "ln_var")

            def normalise(x, t, gb, sd_sem, sd_n, last_sem):
                dve.wait_ge(sd_sem, sd_n)
                link(dve.reciprocal(rstd[:, t:t + 1], sd[:, t:t + 1]))
                link(dve.tensor_scalar(x[:, t, :], x[:, t, :], mv[:, t, 0:1], rstd[:, t:t + 1], ALU.subtract, ALU.mult))
                link(dve.tensor_tensor(x[:, t, :], x[:, t, :], gb[:, 0, :], ALU.mult))
                dve.tensor_tensor(x[:, t, :], x[:, t, :], gb[:, 1, :], ALU.add).then_inc(last_sem, 1)

            def norm(k, last=False):
                dve.wait_ge(sem("lnp_in"), 32 * (k + 1))

                def low(t):
                    dve.wait_ge(sem("xt_hi"), 4 * k + t + 1)
                    v = ps[:, 2 * (t % 2):2 * (t % 2) + 2, :].rearrange("p b (c n) -> p (b c) n", c=4)
                    dve.tensor_tensor(xl[:, :, t * P:(t + 1) * P], v, f32(xh[:, :, t * P:(t + 1) * P]), ALU.subtract)\
                       .then_inc(sem("xt_lo"), 1)

                for t in range(TT):
                    normalise(res, t, lnp, sem("ln_sd"), 4 * k + t + 1, sem("ln_ok"))
                    if t >= 1 and not last:
                        low(t - 1)
                if not last:
                    low(TT - 1)
                    dve.wait_ge(sem("ln_ok"), 4 * (k + 1))
                split(st["g"] + 1)

            dve.wait_ge(sem("ssm_in"), 16 * N_SSM_IN)
            dve.tensor_copy(lam[:, 2, :].rearrange("q (a p) -> q a p", a=2),
                            ldt[:].unsqueeze(2).broadcast_to([Q, 2, NS])).then_inc(sem("ldt_wide"), 1)
            link(dve.tensor_copy(posf[:], posi[:]))
            dve.wait_ge(sem("pool_const"), 1)
            v1 = ang[:, 0, 0:128].rearrange("p (t k) -> p t k", t=TT)
            v2 = ang[:, 0, 128:160].rearrange("p (t k) -> p t k", t=TT)
            link(dve.tensor_tensor(v1, posf[:, 0, :].unsqueeze(2).broadcast_to([P, TT, 32]),
                                   inv1[:].unsqueeze(1).broadcast_to([P, TT, 32]), ALU.mult))
            link(dve.tensor_tensor(v2, posf[:, 1, :].unsqueeze(2).broadcast_to([P, TT, 8]),
                                   inv2[:].unsqueeze(1).broadcast_to([P, TT, 8]), ALU.mult))

            def wrap(x, n):
                link(dve.tensor_scalar(n, x, 1 / (2 * math.pi), MAGIC, ALU.mult, ALU.add))
                link(dve.tensor_scalar(n, n, -MAGIC, None, ALU.add))
                for c in TWO_PI:
                    link(dve.scalar_tensor_tensor(out=x, in0=n, scalar=-c, in1=x, op0=ALU.mult, op1=ALU.add))
                return dve.tensor_scalar(x, x, -PI_IN, PI_IN, ALU.max, ALU.min)

            wrap(ang[:, 0, :], ang[:, 1, :]).then_inc(sem("ang_ok"), 1)
            dve.wait_ge(sem("lam_pe"), 1)
            dve.tensor_copy(sc[:, 0:3, :], ps[:, 0, 0:3 * Q].rearrange("p (i q) -> p i q", i=3)).then_inc(sem("lam_rd"), 1)
            dve.wait_ge(sem("dt_ok"), 1)
            for i in range(2):
                link(dve.tensor_tensor(sc[:, 4 + i, :], sc[:, i, :], sc[:, 3, :], ALU.mult))
            link(dve.tensor_copy(sc[:, 6, :], sc[:, 5, :]))
            wrap(sc[:, 6, :], sc[:, 7, :]).then_inc(sem("ang_ok"), 1)
            dve.wait_ge(sem("mag_ok"), 2)
            link(dve.memset(pw[:, 0, 0, :], 1.0))
            link(dve.memset(pw[:, 1, 0, :], 0.0))
            link(dve.tensor_tensor(pw[:, 0, 1, :], sc[:, 10, :], sc[:, 9, :], ALU.mult))
            link(dve.tensor_tensor(pw[:, 1, 1, :], sc[:, 10, :], sc[:, 8, :], ALU.mult))
            link(dve.tensor_scalar(sc[:, 12, :], pw[:, 0, 1, :], -1.0, None, ALU.add))
            for o, a, b in ((13, 0, 0), (14, 1, 1)):
                link(dve.tensor_tensor(sc[:, o, :], sc[:, a, :], sc[:, b, :], ALU.mult))
            link(dve.tensor_tensor(sc[:, 13, :], sc[:, 13, :], sc[:, 14, :], ALU.add))
            link(dve.reciprocal(sc[:, 14, :], sc[:, 13, :]))
            link(dve.tensor_tensor(sc[:, 15, :], sc[:, 12, :], sc[:, 0, :], ALU.mult))
            link(dve.tensor_tensor(sc[:, 16, :], pw[:, 1, 1, :], sc[:, 1, :], ALU.mult))
            link(dve.tensor_tensor(sc[:, 15, :], sc[:, 15, :], sc[:, 16, :], ALU.add))
            link(dve.tensor_tensor(sc[:, 15, :], sc[:, 15, :], sc[:, 14, :], ALU.mult))
            link(dve.tensor_tensor(sc[:, 16, :], pw[:, 1, 1, :], sc[:, 0, :], ALU.mult))
            link(dve.tensor_tensor(sc[:, 17, :], sc[:, 12, :], sc[:, 1, :], ALU.mult))
            link(dve.tensor_tensor(sc[:, 16, :], sc[:, 16, :], sc[:, 17, :], ALU.subtract))
            link(dve.tensor_tensor(sc[:, 16, :], sc[:, 16, :], sc[:, 14, :], ALU.mult))

            def cmul(o_re, o_im, x_re, x_im, y_re, y_im, t0, t1, minus=False):
                link(dve.tensor_tensor(t0, x_re, y_re, ALU.mult))
                link(dve.tensor_tensor(t1, x_im, y_im, ALU.mult))
                link(dve.tensor_tensor(o_re, t0, t1, ALU.subtract))
                link(dve.tensor_tensor(t0, x_re, y_im, ALU.mult))
                link(dve.tensor_tensor(t1, x_im, y_re, ALU.mult))
                return dve.tensor_tensor(o_im, t0, t1, ALU.add)

            for lo, n in ((1, 1), (1, 2), (1, 4)):
                top = n
                bc = lambda r: pw[:, r, top:top + 1, :].broadcast_to([P, n, Q])
                t0, t1 = (rt[:, 512 * i:512 * i + n * Q].rearrange("p (n q) -> p n q", n=n) for i in range(2))
                dve.wait_ge(sem("c_pe"), 1)
                link(cmul(pw[:, 0, top + 1:top + 1 + n, :], pw[:, 1, top + 1:top + 1 + n, :],
                          pw[:, 0, 1:1 + n, :], pw[:, 1, 1:1 + n, :], bc(0), bc(1), t0, t1))
            for r in range(2):
                for a in range(2):
                    v = ps[a * NS:(a + 1) * NS, 1 + 2 * r:3 + 2 * r, :].rearrange("p b (q a c) -> p (b q) a c", a=2, c=GC)
                    ins = dve.tensor_scalar(cc[a * NS:(a + 1) * NS, r], v[:, :, a, :], 1.0 - 2.0 * r, None, ALU.mult)
                    ins.then_inc(sem("c_rd"), 1)
            dve.wait_ge(sem("c_rd"), 4)

            def wide(x):
                return x.unsqueeze(2).broadcast_to([P, Q, GC])
            T0, T1 = (x[:, 0:512].rearrange("p (q c) -> p q c", c=GC) for x in (rt, ft))
            link(cmul(bb[:, 0], bb[:, 1], wide(sc[:, 15, :]), wide(sc[:, 16, :]), b_in[:, 0], b_in[:, 1], T0, T1))
            for j in range(L):
                k = L - 1 - j
                ins = cmul(ab[:, 0, :, j, :], ab[:, 1, :, j, :], wide(pw[:, 0, k, :]), wide(pw[:, 1, k, :]),
                           bb[:, 0], bb[:, 1], T0, T1)
                if j < L - 1:
                    link(ins)
            ins.then_inc(sem("ab_ok"), 1)
            dve.wait_ge(sem("kk_pe"), 1)
            for a in range(2):
                link(dve.tensor_copy(kk[:, a], ps[:, 1 + a, :].rearrange("p (q c) -> p q c", c=GC)))
                dm = ident[:, (L - 1) * GC:L * GC].unsqueeze(1).broadcast_to([P, Q, GC])
                link(dve.tensor_tensor(T0, dbc[:, :, a, :], dm, ALU.mult))
                ins = dve.tensor_tensor(kk[:, a], kk[:, a], T0, ALU.add)
                if a == 0:
                    link(ins)
            ins.then_inc(sem("kk_ok"), 1)
            dve.wait_ge(sem("s_rd"), 8)
            link(dve.memset(hst[:, :, :, 0], 0.0))
            a8r = pw[:, 0, L, :].unsqueeze(1).broadcast_to([P, 2, Q])
            a8i = pw[:, 1, L, :]
            t1 = rt[:, 0:64].rearrange("p (a q) -> p a q", a=2)
            dve.wait_ge(sem("mt_pe"), 16)
            t0 = rt[:, 64:128].rearrange("p (a q) -> p a q", a=2)
            with dve.Fori(0, NC - 1) as c:
                h = hst[:, :, :, bass.ds(c, 1)].rearrange("p a q o -> p a (q o)")
                h2 = hst[:, :, :, bass.ds(c + 1, 1)].rearrange("p a q o -> p a (q o)")
                sv = sst[:, :, :, bass.ds(c, 1)].rearrange("p a q o -> p a (q o)")
                dve.tensor_tensor(t0, a8r, h, ALU.mult).then_inc(sem("scan"), 1)
                dve.tensor_tensor(t1[:, 0, :], a8i, h[:, 1, :], ALU.mult).then_inc(sem("scan"), 1)
                dve.tensor_tensor(t1[:, 1, :], a8i, h[:, 0, :], ALU.mult).then_inc(sem("scan"), 1)
                dve.wait_ge(sem("scan"), c * 6 + 3)
                dve.tensor_tensor(t0, t0, sv, ALU.add).then_inc(sem("scan"), 1)
                dve.wait_ge(sem("scan"), c * 6 + 4)
                dve.tensor_tensor(h2[:, 0, :], t0[:, 0, :], t1[:, 0, :], ALU.subtract).then_inc(sem("scan"), 1)
                dve.tensor_tensor(h2[:, 1, :], t0[:, 1, :], t1[:, 1, :], ALU.add).then_inc(sem("scan"), 1)
                dve.wait_ge(sem("scan"), c * 6 + 6)
            H = Q // 2
            for hf in range(2):
                if hf == 1:
                    dve.wait_ge(sem("y_mm"), 8)
                else:
                    dve.wait_ge(sem("s_pe"), 8)
                qs = slice(H * hf, H * hf + H)
                w0, w1 = (x[:, 256:512].rearrange("p (q c) -> p q c", c=GC) for x in (rt, ft))
                for i in range(L):
                    wd = lambda r: pw[:, r, i + 1, qs].unsqueeze(2).broadcast_to([P, H, GC])
                    link(dve.tensor_tensor(w0, cc[:, 0, qs], wd(0), ALU.mult))
                    link(dve.tensor_tensor(w1, cc[:, 1, qs], wd(1), ALU.mult))
                    link(dve.tensor_tensor(ca[:, :, 0, i, :], w0, w1, ALU.add))
                    link(dve.tensor_tensor(w0, cc[:, 1, qs], wd(0), ALU.mult))
                    link(dve.tensor_tensor(w1, cc[:, 0, qs], wd(1), ALU.mult))
                    ins = dve.tensor_tensor(ca[:, :, 1, i, :], w0, w1, ALU.subtract)
                    if i < L - 1:
                        link(ins)
                ins.then_inc(sem("ca_ok"), 1)
                if hf == 0:
                    split(0)
                    split(1)
            for c in range(KD):
                dve.wait_ge(sem("yt_hi"), c + 1)
                dve.tensor_tensor(xl[:, c, :].rearrange("p (n j) -> p n j", j=L),
                                  ps[:, c % 4, :].rearrange("p (j n) -> p n j", j=L),
                                  f32(xh[:, c, :]).rearrange("p (n j) -> p n j", j=L), ALU.subtract).then_inc(sem("yt_lo"), 1)

            def relu_mlp(k):
                for half in range(2):
                    channel_major(8, "relu2", 0)
                    for n in range(2):
                        token_major(16, 512, add_to_res(n, ALPHA if half == 0 else 1.0,
                                                        ln_stats(k) if half == 1 and n == 1 else None),
                                    hold=half == 1 and n == 1)
                norm(k)

            def out_proj(k):
                token_major(KD, 512, add_to_res(0, ALPHA))
                token_major(KD, 512, add_to_res(1, ALPHA, ln_stats(k)), hold=True)
                norm(k)

            channel_major(KD, "glu", 2)
            dve.wait_ge(sem("res_in"), 16 * TT)
            out_proj(0)
            relu_mlp(1)

            token_major(KD, KVL + ROPE)
            token_major(KD, QL)

            def rope(x1, x2, cs, sn, o1, o2, tmp):
                t = [tmp(i) for i in range(4)]
                dve.tensor_tensor(t[0], x1, cs, ALU.mult)
                dve.tensor_tensor(t[1], x2, sn, ALU.mult)
                dve.tensor_tensor(t[2], x1, sn, ALU.mult)
                link(dve.tensor_tensor(t[3], x2, cs, ALU.mult))
                dve.tensor_tensor(o1, t[0], t[1], ALU.subtract)
                return dve.tensor_tensor(o2, t[2], t[3], ALU.add)

            dve.wait_ge(sem("rms_sd"), 1)
            link(dve.reciprocal(mv[:], bst[:, :, :, 0]))
            for t in range(TT):
                link(dve.tensor_scalar(ckv[:, t, 0:KVL], ckv[:, t, 0:KVL], mv[:, t, 0:1], None, ALU.mult))
                link(dve.tensor_scalar(cq[:, t, :], cq[:, t, :], mv[:, t, 1:2], None, ALU.mult))
            link(rope(ckv[:, :, KVL:KVL + 32], ckv[:, :, KVL + 32:KVL + 64], cos1[:], sin1[:],
                 krd[:, :, 0:32], krd[:, :, 32:64], lambda i: rt[:, 128 * i:128 * i + 128].rearrange("p (t k) -> p t k", t=TT)))
            dve.tensor_copy(krd[:, :, 64:128], krd[:, :, 0:64]).then_inc(sem("rms_ok"), 1)
            for n, (lo, hi, g) in enumerate([(ckvl[:, c, :], ckvh[:, c, :], kvg[:, c:c + 1]) for c in range(2)]
                                            + [(cql[:, c, :], cqh[:, c, :], qg[:, c:c + 1]) for c in range(3)]):
                dve.wait_ge(sem("lat_hi"), n + 1)
                dve.scalar_tensor_tensor(out=lo, in0=ps[:, n % 4, :], scalar=g, in1=f32(hi), op0=ALU.mult,
                                         op1=ALU.subtract).then_inc(sem("lat_rd"), 1)
            dve.wait_ge(sem("lat_pe"), 6)
            dve.tensor_copy(krT[:], ps[:, 1, :]).then_inc(sem("lat_rd"), 1)
            for c in range(2):
                st["g"] += 1
                dve.wait_ge(chunk_used, st["g"])
                ins = dve.tensor_copy(vv[:, :, 512 * c:512 * c + 512], ps[:, 4:8, :])
                ins.then_inc(sem("v_rd"), 1)
                split(st["g"] + 1)
            for c in range(4):
                st["g"] += 1
                dve.wait_ge(chunk_used, st["g"])
                dve.tensor_copy(qn[:, 2 * c:2 * c + 2, :], ps[:, 2 * (c % 2):2 * (c % 2) + 2, :]).then_inc(sem("qn_rd"), 1)
                split(st["g"] + 1)
            dve.wait_ge(sem("qr_rd"), 4)
            for t in range(TT):
                v = qrt[:, t, :].rearrange("p (h d) -> p h d", h=NH)
                cs, sn = (x[:, t:t + 1, :].broadcast_to([P, NH, 32]) for x in (cos1, sin1))
                rope(v[:, :, 0:32], v[:, :, 32:64], cs, sn, v[:, :, 0:32], v[:, :, 32:64],
                     lambda i: rt[:, 256 * i:256 * i + 256].rearrange("p (h k) -> p h k", h=NH))\
                    .then_inc(sem("qrope_ok"), 1)
                dve.wait_ge(sem("qrope_ok"), t + 1)

            def attention(name, scale, sm, pt, per, add, dst):
                def first(u):
                    h, t = u // TT, u % TT
                    n = (t + 1) * P
                    dve.wait_ge(sem(name + "_s"), u + 1)
                    if u >= 2:
                        dve.wait_ge(sem(name + "_e"), u - 1)
                    dve.tensor_tensor(sm[:, u % 2, 0:n], ps[:, u % 2, 0:n], add(t, n), ALU.add).then_inc(sem(name + "_s_rd"), 1)
                    dve.wait_ge(sem(name + "_s_rd"), u + 1)
                    link(dve.reduce_max(nmax[:, u % 2:u % 2 + 1], sm[:, u % 2, 0:n], axis=AX.X))
                    dve.tensor_scalar(nmax[:, u % 2:u % 2 + 1], nmax[:, u % 2:u % 2 + 1], -scale, None,
                                      ALU.mult).then_inc(sem(name + "_mx"), 1)

                def low(n0):
                    dve.wait_ge(sem(name + "_o_hi"), n0 + 1)
                    dve.tensor_tensor(xl[:, dst + n0, :], ps[:, 4 + n0 % 2, :], f32(xh[:, dst + n0, :]), ALU.subtract)\
                       .then_inc(sem(name + "_o_lo"), 1)

                first(0)
                for u in range(NH * TT):
                    h, t = u // TT, u % TT
                    if u + 1 < NH * TT:
                        first(u + 1)
                    n = (t + 1) * P
                    dve.wait_ge(sem(name + "_e"), u + 1)
                    link(dve.reciprocal(rinv[:, u % 2:u % 2 + 1], rsum[:, u % 2:u % 2 + 1]))
                    dve.tensor_scalar(pt[2][:, u % 2, 0:n], pt[2][:, u % 2, 0:n], rinv[:, u % 2:u % 2 + 1], None,
                                      ALU.mult).then_inc(sem(name + "_pn"), 1)
                    if t == 1 and h >= per + 1 and (h - 1) % per == per - 1:
                        low((h - 1) // per - 1)
                for n0 in range(max(0, NH // per - 2), NH // per):
                    low(n0)

            def causal_mask(t, n):
                return causal[:, S - n:S]

            attention("mla", SM_SCALE, sm1, pt1 + [pn1], 1, causal_mask, 0)
            out_proj(2)
            relu_mlp(3)

            for l in range(2):
                kx = 4 + 2 * l
                for width in (512, 512, 68, 512):
                    token_major(KD, width)
                token_major(KD, 512)
                for t in range(TT):
                    dve.wait_ge(b_free[t], st["b"])
                for t in range(TT):
                    def heads(x, n):
                        return x.rearrange("p (h d) -> p h d", d=HD)
                    for x, n in ((qtok[:, t, :], 8), (kvq[:, t, 0:128], 2), (kvq[:, t, 256:512], 4), (kiw[:, t, 0:64], 1)):
                        v = heads(x, n)
                        cs, sn = (y[:, t:t + 1, :].broadcast_to([P, n, 8]) for y in (cos2, sin2))
                        link(rope(v[:, :, 0:8], v[:, :, 8:16], cs, sn, v[:, :, 0:8], v[:, :, 8:16],
                                  lambda i: ft[:, 64 * i:64 * i + 8 * n].rearrange("p (h k) -> p h k", h=n)))
                for t in range(TT):
                    v = kvq[:, t, 0:128].rearrange("p (g d) -> p g d", g=2).unsqueeze(2).broadcast_to([P, 2, 2, HD])
                    link(dve.tensor_copy(kdd[:, t, :].rearrange("p (g r d) -> p g r d", g=2, r=2), v))
                link(dve.tensor_scalar(kiw[:, :, 64:68], kiw[:, :, 64:68], (NI * IXD) ** -0.5, None, ALU.mult))
                link(dve.tensor_copy(kid[:, :, 0:64], kiw[:, :, 0:64]))
                dve.tensor_copy(kid[:, :, 64:128], kiw[:, :, 0:64]).then_inc(sem("rope2_ok"), 1)
                for t in range(1, TT):
                    n = (t + 1) * P
                    for h in range(NI):
                        m = 4 * (3 * l + t - 1) + h
                        dve.wait_ge(sem("lg_rd"), m + 1)
                        wcol = kiw[:, t, 64 + h:65 + h]
                        if h == 0:
                            ins = dve.tensor_scalar(scr[:, t - 1, 0:n], rl[:, h, 0:n], wcol, None, ALU.mult)
                        else:
                            ins = dve.scalar_tensor_tensor(out=scr[:, t - 1, 0:n], in0=rl[:, h, 0:n], scalar=wcol,
                                                           in1=scr[:, t - 1, 0:n], op0=ALU.mult, op1=ALU.add)
                        ins.then_inc(sem("sc_ok"), 1)
                        dve.wait_ge(sem("sc_ok"), m + 1)
                dve.wait_ge(sem("sgu_in"), 64 * (l + 1))
                for t in range(TT):
                    stats(vs, t, SGW, "vs_var")
                for t in range(TT):
                    normalise(vs, t, sgp, sem("vs_sd"), 4 * l + t + 1, sem("vs_ok"))
                dve.wait_ge(sem("ws_pe"), 2 * l + 2)
                link(dve.tensor_copy(bsT[:], ps[:, 6, 0:SGG]))
                dve.wait_ge(sem("ws_rd"), l + 1)
                dve.tensor_tensor(wsT[:], wsT[:], ustep[:].unsqueeze(1).broadcast_to([P, SGG, P]), ALU.mult)\
                   .then_inc(sem("ws_ok"), 1)
                dve.wait_ge(sem("sg_pe"), l + 1)
                for g in range(SGG):
                    v = ps[:, 4 + g // 2, (g % 2) * 256:(g % 2 + 1) * 256].rearrange("p (t c) -> p t c", t=TT)
                    o = gu[:, :, g * 64:(g + 1) * 64]
                    ins = dve.scalar_tensor_tensor(out=o, in0=v, scalar=bsT[:, g:g + 1], in1=o, op0=ALU.add, op1=ALU.mult)
                ins.then_inc(sem("bo_ok"), 1)
                for n in range(4):
                    dve.wait_ge(sem(f"bo{l}_hi"), n + 1)
                    dve.tensor_tensor(xl[:, 4 + n, :], ps[:, n, :], f32(xh[:, 4 + n, :]), ALU.subtract)\
                       .then_inc(sem(f"bo{l}_rd"), 1)
                link(dve.tensor_copy(mask[:, 0, 0:P], chunkm[:]))
                for t in range(1, TT):
                    n = (t + 1) * P
                    x = scr[:, t - 1, 0:n]
                    link(dve.tensor_tensor(x[:, n - P:n], x[:, n - P:n], chunkm[:], ALU.add))
                    for r in range(TOPK // 8):
                        link(dve.max(m8[:], x))
                        link(dve.match_replace(x, m8[:], x, TAKEN))
                    link(dve.tensor_scalar(mask[:, t, 0:n], x, TAKEN / 2, NEG, ALU.is_gt, ALU.mult))
                attention(f"dsa{l}", HD ** -0.5, sm2, pt2 + [pn2], 2, lambda t, n: mask[:, t, 0:n], 0)
                out_proj(kx)
                for n in range(2):
                    dve.wait_ge(sem(f"pt{l}_hi"), n + 1)
                    dve.tensor_tensor(pTl[:, n, :], ps[:, n, :], f32(pTh[:, n, :]), ALU.subtract).then_inc(sem(f"pt{l}_rd"), 1)

                for n in range(2):
                    def gate_evac(t, src, n=n):
                        m = 8 * l + 4 * n + t
                        dve.wait_ge(sem("pg_sig"), m + 1)
                        x = (rt, ft)[t % 2][:, 0:512]
                        dve.tensor_tensor(x, x, plt[:, t, :], ALU.mult).then_inc(b_free[t], 1)
                        dve.wait_ge(b_free[t], st["b"] + 1)
                        r = res[:, t, 512 * n:512 * n + 512]
                        dve.scalar_tensor_tensor(out=r, in0=r, scalar=ALPHA, in1=x, op0=ALU.mult, op1=ALU.add)\
                           .then_inc(sem("pg_ok"), 1)
                    token_major(2, 512)
                    token_major(KD, 512, gate_evac)
                for half in range(2):
                    channel_major(11, "swiglu", 0)
                    for n in range(2):
                        token_major(11, 512, add_to_res(n, 1.0, ln_stats(kx + 1) if half == 1 and n == 1 else None),
                                    hold=half == 1 and n == 1)
                norm(kx + 1, last=l == 1)


N_LN = 8
N_SSM_IN = 14
IXD = 64

_INS = ['x', 'positions', 'ln_mix_g', 'ln_mix_b', 'ln_ffn_g', 'ln_ffn_b', 'w_ff1', 'w_ff2', 'ssm_lam_re',
        'ssm_lam_im', 'ssm_log_dt', 'ssm_b_re', 'ssm_b_im', 'ssm_c_re', 'ssm_c_im', 'ssm_d', 'ssm_w_glu',
        'ssm_w_out', 'kv_w_a', 'kv_norm_g', 'kv_w_b', 'q_w_a', 'q_norm_g', 'q_w_b', 'attn_w_o', 'p_2',
        'positions_2', 'w_in_2', 'w_o_2', 'ln1_g_2', 'ln1_b_2', 'ln2_g_2', 'ln2_b_2', 'sgu_w_2', 'sgu_b_2',
        'sgu_ln_g_2', 'sgu_ln_b_2', 'w_ffn_in_2', 'w_ffn_out_2', 'w_ple_2', 'w_ple_gate_2']


def kernel(**inputs):
    import numpy as _np
    import concourse.bacc as _bacc
    from concourse import mybir as _mybir
    from concourse.bass_utils import run_bass_kernel_spmd as _run

    nc = _bacc.Bacc("TRN2", target_bir_lowering=False, num_devices=1)
    arrays, w = {}, {}
    for name in _INS:
        a = _np.ascontiguousarray(inputs[name])
        arrays[f"in_{name}_dram"] = a
        w[name] = nc.dram_tensor(f"in_{name}_dram", a.shape, _mybir.dt.from_np(a.dtype), kind="ExternalInput").ap()
    out = nc.dram_tensor("out_0_dram", (1, S, D), _mybir.dt.float32, kind="ExternalOutput").ap()
    two_blocks(nc, w, out)
    r = _run(nc, [arrays], core_ids=[0])
    return r.results[0]["out_0_dram"]
```

```python
import math
from contextlib import ExitStack

import concourse.bass as bass
from concourse import mybir

F32 = mybir.dt.float32
F32R = mybir.dt.float32r
I32 = mybir.dt.int32
BF16 = mybir.dt.bfloat16
ALU = mybir.AluOpType
ACT = mybir.ActivationFunctionType
AX = mybir.AxisListType

P = 128
D = 1024
S = 512
TT = S // P
KD = D // P
FF1 = 4 * D
FF2 = 2816
NF2 = FF2 // P
DEPTH = 2
ALPHA = (2 * DEPTH) ** 0.25
LN_EPS, RMS_EPS = 1e-5, 1e-6
G, GC, NS = 64, 16, 64
L = 8
NC = S // L
Q = G // 2
NH, NOPE, ROPE, VH, QL, KVL = 8, 128, 64, 128, 384, 256
SM_SCALE = (NOPE + ROPE) ** -0.5
THETA1, THETA2 = 10000.0, 500000.0
HD, NI, TOPK, ROT = 64, 4, 128, 16
IN2_GROUPS = ((512, 512), (1024, 68), (1604, 512), (1092, 512), (0, 512))
SGW, SGG, PLE = 512, 8, 256
MB = (3, 4, 7, 0)
AB_POOL = (5, 6)
SB_J = 8
SB = (0, 1, 6, 7)
CAP = 2048
NEG = -1.0e30
TAKEN = -3.0e38
MAGIC = 12582912.0
NORMS = [("ln_mix_", 0), ("ln_ffn_", 0), ("ln_mix_", 1), ("ln_ffn_", 1), ("ln1_", 0), ("ln2_", 0), ("ln1_", 1), ("ln2_", 1)]
N_LN = len(NORMS)
TWO_PI = (6.28125, 0.0019350051879882812, 3.019916050e-07)
PI_IN = 3.1415925


def stages_of(w):
    def ap(x):
        return x

    out = []

    def add(name, n, cols, parts):
        out.append((name, n, cols, parts))

    def rows(x, k0, nk, c0, nc):
        return x[k0 * P:(k0 + nk) * P, c0:c0 + nc].rearrange("(k p) n -> p k n", p=P)

    def cols_at(x, j, step, base, width):
        v = x.rearrange("(k p) n -> p k n", p=P)
        if isinstance(j, int):
            return v[:, :, base + j * step:base + j * step + width]
        return v[:, :, bass.ds(j * step + base, width)]

    def channel(name, x, n, c0, c1, step):
        k = x.shape[0]
        add(name, n, 2 * k, lambda j: [(0, cols_at(x, j, step, c0, P)), (k, cols_at(x, j, step, c1, P))])

    def token(name, x, k0, nk, c0, nc):
        at = 0
        while at < nk:
            m = min(4 if nc > 256 else 8, nk - at)
            h = (m + 1) // 2
            add(name, 1, m * nc, lambda j, a=at, m=m, h=h: [
                (0, rows(x, k0 + a, h, c0, nc)), (h * nc, rows(x, k0 + a + h, m - h, c0, nc))])
            at += m

    channel("glu", w["ssm_w_glu"][0], KD, 0, D, P)
    for n in range(2):
        token("ssm_out", w["ssm_w_out"][0], 0, KD, 512 * n, 512)

    def relu_mlp(l):
        for half in range(2):
            c0 = half * FF1 // 2
            channel("ff_in", w["w_ff1"][l], 8, c0, c0 + P, 2 * P)
            for n in range(2):
                token("ff_out", w["w_ff2"][l], half * 16, 16, 512 * n, 512)

    relu_mlp(0)
    token("kv_a", w["kv_w_a"], 0, KD, 0, KVL + ROPE)
    token("q_a", w["q_w_a"][0], 0, KD, 0, QL)
    for c in range(2):
        add("kv_b", 1, 2048, lambda j, c=c: [(k * 1024, rows(w["kv_w_b"], k, 1, 1024 * c, 1024)) for k in range(2)])
    for c in range(4):
        add("q_b", 1, 1152, lambda j, c=c: [(0, rows(w["q_w_b"][0], 0, 2, 384 * c, 384)),
                                            (768, rows(w["q_w_b"][0], 2, 1, 384 * c, 384))])
    for n in range(2):
        token("attn_o", w["attn_w_o"][0], 0, KD, 512 * n, 512)
    relu_mlp(1)
    for l in range(2):
        wi = w["w_in_2"][l]
        for c0, nc in IN2_GROUPS:
            token("w_in", wi, 0, KD, c0, nc)
        for n in range(2):
            token("w_o", w["w_o_2"][l], 0, KD, 512 * n, 512)
        for n in range(2):
            token("ple", w["w_ple_2"][l], 0, 2, 512 * n, 512)
            token("ple_gate", w["w_ple_gate_2"][l], 0, KD, 512 * n, 512)
        for half in range(2):
            channel("ffn_in", w["w_ffn_in_2"][l], 11, half * 11 * P, FF2 + half * 11 * P, P)
            for n in range(2):
                token("ffn_out", w["w_ffn_out_2"][l], half * 11, 11, 512 * n, 512)
    return out


def two_blocks(nc, w, out, last=99):
    stream = stages_of(w)
    chunk_cols = [c for _, n, c, _ in stream for _ in range(n)]
    n_chunks = len(chunk_cols)

    with ExitStack() as ctx:
        sems = {}

        def sem(name):
            if name not in sems:
                sems[name] = ctx.enter_context(nc.semaphore(name))
            return sems[name]

        base = -(-nc.sbuf_base // 32) * 32
        KB = 1024

        def at(name, kb, shape, dt=F32):
            return nc.alloc_sbuf_tensor_at(name, shape, dt, offset=base + int(kb * KB))

        ctx.enter_context(nc.sbuf_tensor("arena_fence", [P, 207 * 256], F32))
        raw = at("raw", 0, [P, 2, CAP])
        whi = at("whi", 16, [P, 2, CAP], F32R)
        wlo = at("wlo", 32, [P, 2, CAP], F32R)
        res = at("res", 48, [P, TT, D])
        xh = at("xh", 64, [P, KD, S], F32R)
        xl = at("xl", 80, [P, KD, S], F32R)
        lnp = at("lnp", 96, [P, 2, D])
        rt = at("rt", 104, [P, 1024])
        ft = at("ft", 108, [P, 1024])
        ident = at("ident", 112, [P, 240])
        causal = at("causal", 113, [P, P], BF16)
        identb = at("identb", 113.25, [P, P], BF16)
        scratch = at("scratch", 113.5, [P, P])
        lng = at("lng", 114, [P, N_LN, 2, KD])
        chunkm = at("chunkm", 115, [P, P])
        cos1 = at("cos1", 115.5, [P, TT, 32])
        sin1 = at("sin1", 116, [P, TT, 32])
        cos2 = at("cos2", 116.5, [P, TT, 8])
        sin2 = at("sin2", 116.625, [P, TT, 8])
        pw = at("pw", 116.75, [P, 2, 9, Q])
        bst = at("bst", 119, [P, TT, 2, 6])
        mv = at("mv", 119.25, [P, TT, 2])
        sd = at("sd", 119.375, [P, TT])
        rstd = at("rstd", 119.4375, [P, TT])
        m8 = at("m8", 119.5, [P, 8])
        nmax = at("nmax", 119.5625, [P, 4])
        rsum = at("rsum", 119.625, [P, 4])
        rinv = at("rinv", 119.6875, [P, 4])
        consts = at("consts", 119.75, [P, 4])
        kvg = at("kvg", 119.8125, [P, 2])
        qg = at("qg", 119.875, [P, 3])
        bsT = at("bsT", 119.9375, [P, SGG])
        ustep = at("ustep", 120, [P, P])
        nmr = at("nmr", 120.5, [P, TT])
        AR = 120.75
        hidh = at("hidh", AR, [P, 16, S], F32R)
        hidl = at("hidl", AR + 32, [P, 16, S], F32R)
        xc = at("xc", AR, [NC, L, D])
        xg = at("xg", 64, [NC, G, L * GC])
        yg = at("yg", AR, [NC, L, D])
        ab = at("ab", AR + 32, [P, 2, Q, L, GC])
        tm = at("tm", AR + 32, [P, L, 2, Q, GC])
        mt = [at("mt_re", AR + 64, [P, Q, P]), at("mt_im", 80, [P, Q, P])]
        ca = at("ca", 16, [P, Q, 2, L, GC])
        pa = [at("pa0", 0, [P, Q, GC]), at("pa1", 2, [P, Q, GC])]
        b_in = at("b_in", AR + 64, [P, 2, Q, GC])
        bb = at("bb", AR + 68, [P, 2, Q, GC])
        sc = at("sc", AR + 72, [P, 20, Q])
        lam = at("lam", AR + 76, [Q, 3, P])
        ldt = at("ldt", AR + 78, [Q, 2])
        cc = at("cc", AR + 80, [P, 2, Q, GC])
        cn = at("cn", 104, [P, 2, 8, 2, NS])
        kk = at("kk", 96, [P, 2, Q, GC])
        dbc = at("dbc", 100, [P, Q, 2, GC])
        uu = at("uu", 48, [P, G, NC])
        sst = at("sst", 64, [P, 2, Q, NC])
        hst = at("hst", 80, [P, 2, Q, NC])
        ang = at("ang", AR + 84, [P, 2, 160])
        posi = at("posi", AR + 85.25, [P, 2, TT], I32)
        posf = at("posf", AR + 85.3125, [P, 2, TT])
        inv1 = at("inv1", AR + 85.375, [P, 32])
        inv2 = at("inv2", AR + 85.5, [P, 8])
        a64t = at("a64t", AR + 85.5625, [P, 2, Q])
        ckv = at("ckv", AR, [P, TT, KVL + ROPE])
        cq = at("cq", AR + 5, [P, TT, QL])
        krd = at("krd", AR + 11, [P, TT, 2 * ROPE])
        junk = at("junk", AR + 13, [P, QL])
        kn = at("kn", AR, [P, NH, S])
        vv = at("vv", AR + 16, [P, TT, NH * VH])
        qn = at("qn", AR + 32, [P, NH, S])
        qrT = at("qrT", AR + 48, [P, NH // 2, S])
        krT = at("krT", AR + 56, [P, S])
        qrt = at("qrt", AR + 58, [P, TT, NH * ROPE])
        ckvh = at("ckvh", AR + 66, [P, 2, S], F32R)
        ckvl = at("ckvl", AR + 70, [P, 2, S], F32R)
        cqh = at("cqh", AR + 74, [P, 3, S], F32R)
        cql = at("cql", AR + 80, [P, 3, S], F32R)
        pn1 = at("pn1", AR + 58, [P, 3, S])
        pt1 = [at("pt1a", AR + 64, [P, TT, S]), at("pt1b", AR + 72, [P, TT, S])]
        qT = at("qT", AR, [P, 4, S])
        kT = at("kT", AR + 8, [P, 2, S])
        qiT = at("qiT", AR + 12, [P, 2, S])
        kiT = at("kiT", AR + 16, [P, S])
        kvq = at("kvq", AR + 18, [P, TT, 512])
        qtok = at("qtok", AR + 26, [P, TT, 512])
        gu = at("gu", AR + 34, [P, TT, 512])
        vs = at("vs", AR + 42, [P, TT, 512])
        kiw = at("kiw", AR + 50, [P, TT, 68])
        kid = at("kid", AR + 52, [P, TT, 128])
        kdd = at("kdd", AR + 54, [P, TT, 256])
        mask = at("mask", AR + 58, [P, TT, S], BF16)
        scr = at("scr", AR + 66, [P, 3, S])
        pn2 = at("pn2", AR + 66, [P, 3, S])
        pt2 = [at("pt2a", AR + 26, [P, TT, S]), at("pt2b", AR + 76, [P, TT, S])]
        rl = [at("rl_a", AR + 76, [P, NI, S]), at("rl_b", AR + 26, [P, NI, S])]
        rot_i = at("rot_i", AR + 62, [P, 4, TT * 4 * 8])
        rot_q = at("rot_q", AR + 72, [P, 4, TT * 8 * 8])
        wsn = at("wsn", 104, [P, SGG, P])
        wsT = at("wsT", 108, [P, SGG, P])
        sgp = at("sgp", 96, [P, 2, SGW])
        bsn = at("bsn", AR + 84, [SGG, P])
        pin = at("pin", AR + 64, [P, TT, PLE])
        pTh = at("pTh", AR + 68, [P, 2, S], F32R)
        pTl = at("pTl", AR + 72, [P, 2, S], F32R)
        plt = at("plt", AR + 76, [P, TT, 512])
        ps = ctx.enter_context(nc.psum_tensor("ps", [P, 8, 512], F32))

        landed = [sem("landed0"), sem("landed1")]
        hi_ready = sem("hi_ready")
        lo_ready = sem("lo_ready")
        chunk_used = sem("chunk_used")
        act_r = sem("act_r")
        dve_f = sem("dve_f")
        act_h = sem("act_h")
        dve_l = sem("dve_l")
        b_done = sem("b_done")
        b_free = [sem(f"b_free{t}") for t in range(TT)]

        def val(b, i, per):
            return b if i is None else i * per + b

        def pairs(eng, n, first, tail, body):
            m = (n - first - tail) // 2
            for j in range(first):
                body(j, None)
            if m > 1:
                with eng.Fori(0, m) as i:
                    body(first, i)
                    body(first + 1, i)
            else:
                m = 0
            for j in range(first + 2 * m, n):
                body(j, None)

        def xf(c):
            return (rt, ft)[c // 2 % 2][:, S * (c % 2):S * (c % 2 + 1)]

        def f32(x):
            return x.bitcast(F32)

        def rope(eng, link, x1, x2, cs, sn, o1, o2, t):
            eng.tensor_tensor(t[0], x1, cs, ALU.mult)
            eng.tensor_tensor(t[1], x2, sn, ALU.mult)
            eng.tensor_tensor(t[2], x1, sn, ALU.mult)
            link(eng.tensor_tensor(t[3], x2, cs, ALU.mult))
            eng.tensor_tensor(o1, t[0], t[1], ALU.subtract)
            return eng.tensor_tensor(o2, t[2], t[3], ALU.add)

        def cmul(eng, link, o_re, o_im, x_re, x_im, y_re, y_im, t0, t1):
            link(eng.tensor_tensor(t0, x_re, y_re, ALU.mult))
            link(eng.tensor_tensor(t1, x_im, y_im, ALU.mult))
            link(eng.tensor_tensor(o_re, t0, t1, ALU.subtract))
            link(eng.tensor_tensor(t0, x_re, y_im, ALU.mult))
            link(eng.tensor_tensor(t1, x_im, y_re, ALU.mult))
            return eng.tensor_tensor(o_im, t0, t1, ALU.add)

        def wide(x):
            return x.unsqueeze(2).broadcast_to([P, Q, GC])

        def rope_heads(eng, link, x, n, room):
            r = ROT // 2
            v = x.rearrange("p t (h d) -> p t h d", d=HD)
            cs, sn = (y[:].unsqueeze(2).broadcast_to([P, TT, n, r]) for y in (cos2, sin2))
            t = [room[:, i, 0:TT * n * r].rearrange("p (t h k) -> p t h k", t=TT, h=n) for i in range(4)]
            return rope(eng, link, v[:, :, :, 0:r], v[:, :, :, r:2 * r], cs, sn, v[:, :, :, 0:r], v[:, :, :, r:2 * r], t)

        block = ctx.enter_context(nc.Block())

        @block.sync
        def _(sp):
            for i, nm in enumerate(("ssm_lam_re", "ssm_lam_im")):
                sp.dma_start(lam[:, i, :].rearrange("q (a p) -> q a p", a=2),
                             w[nm][0].rearrange("(q a) p -> q a p", a=2)).then_inc(sem("lam_in"), 16)
            sp.dma_start(ldt[:], w["ssm_log_dt"][0].rearrange("(q a) -> q a", a=2)).then_inc(sem("lam_in"), 16)
            for i, nm in enumerate(("ssm_c_re", "ssm_c_im")):
                for d in range(2):
                    sp.dma_start(cn[:, i, :, d, :], w[nm][0].rearrange("(n g) c p -> (g c) n p", g=8))\
                      .then_inc(sem("c_in"), 16)
            sp.dma_start(xc[:], w["x"][0].rearrange("(c j) d -> c j d", j=L)).then_inc(sem("x_in"), 16)
            for i, nm in enumerate(("ssm_b_re", "ssm_b_im")):
                sp.dma_start(b_in[:, i], w[nm][0].rearrange("(q a) p c -> (a p) q c", a=2)).then_inc(sem("b_in"), 16)
            sp.wait_ge(sem("ca_ok"), 1)
            g = 0

            def load(g0, parts, cols, j, i):
                gg = g0 + j
                if gg >= 2:
                    sp.wait_ge(lo_ready, val(gg - 1, i, 2))
                s = gg % 2
                idx = j if i is None else i * 2 + j
                for c0, src in parts(idx):
                    k, m = src.shape[1], src.shape[2]
                    dst = raw[:, s, c0:c0 + k * m].rearrange("p (k n) -> p k n", k=k)
                    sp.dma_start(dst, src).then_inc(landed[s], 16)

            for name, n, cols, parts in stream:
                pairs(sp, n, 2 if g == 0 else 0, 0, lambda j, i: load(g, parts, cols, j, i))
                g += n
            for t in range(TT):
                sp.wait_ge(sem("out_ok"), t + 1)
                sp.dma_start(out[0, t * P:(t + 1) * P, :], res[:, t, :]).then_inc(sem("stored"), 16)
            sp.wait_ge(sem("stored"), 16 * TT)

        @block.gpsimd
        def _(pool):
            seq = sem("pool_seq")
            n = [0]

            def link(ins):
                n[0] += 1
                ins.then_inc(seq, 1)
                pool.wait_ge(seq, n[0])

            def load(dst, src, name, slow=False):
                pool.dma_start(dst, src, allow_slow_non_contiguous=slow).then_inc(sem(name), 16)

            link(pool.memset(ident[:], 0.0))
            link(pool.memset(scratch[:], 0.0))
            link(pool.memset(chunkm[:], 0.0))
            link(pool.memset(ustep[:], 1.0))
            link(pool.affine_select(out=ustep[:], in_=ustep[:], compare_op=ALU.is_ge, fill=0.0, base=0,
                                    pattern=[[1, P]], channel_multiplier=-1))
            link(pool.affine_select(out=ident[:], in_=ident[:], compare_op=ALU.not_equal, fill=1.0, base=0,
                                    pattern=[[-1, 240]], channel_multiplier=1))
            link(pool.affine_select(out=scratch[:], in_=scratch[:], compare_op=ALU.is_ge,
                                    fill=NEG, base=0, pattern=[[-1, P]], channel_multiplier=1))
            link(pool.tensor_copy(causal[:], scratch[:]))
            link(pool.tensor_copy(identb[:], ident[:, 0:P]))
            link(pool.memset(chunkm[0:64, 64:128], NEG))
            for i, v in enumerate((LN_EPS, RMS_EPS, math.pi / 2)):
                link(pool.memset(consts[:, i:i + 1], v))
            for i in range(32):
                pool.memset(inv1[:, i:i + 1], THETA1 ** (-i / 32))
            for i in range(8):
                ins = pool.memset(inv2[:, i:i + 1], THETA2 ** (-2.0 * i / ROT))
            ins.then_inc(sem("pool_const"), 1)
            for i, nm in enumerate(("positions", "positions_2")):
                load(posi[:, i, :], w[nm][0].rearrange("(t p) -> p t", p=P), "pos_in", slow=True)
            load(dbc[:].rearrange("p q a c -> p (q a c)"), w["ssm_d"][0].partition_broadcast(P), "dbc_in")
            load(kvg[:], w["kv_norm_g"].rearrange("(k p) -> p k", p=P), "lng_in", slow=True)
            load(qg[:], w["q_norm_g"][0].rearrange("(k p) -> p k", p=P), "lng_in", slow=True)
            pool.wait_ge(sem("bb_ok"), 1)
            for j in AB_POOL:
                ins = cmul(pool, link, ab[:, 0, :, j, :], ab[:, 1, :, j, :], wide(pw[:, 0, L - 1 - j, :]),
                           wide(pw[:, 1, L - 1 - j, :]), bb[:, 0], bb[:, 1], pa[0][:], pa[1][:])
                ins.then_inc(sem("ab_pool"), 1)
                pool.wait_ge(sem("ab_pool"), j - AB_POOL[0] + 1)
            pool.wait_ge(sem("c_rd"), 4)
            for i in range(L):
                wd = [wide(pw[:, x, i + 1, :]) for x in range(2)]
                for x, op in ((0, ALU.add), (1, ALU.subtract)):
                    pool.tensor_tensor(pa[0][:], cc[:, x], wd[0], ALU.mult)
                    link(pool.tensor_tensor(pa[1][:], cc[:, 1 - x], wd[1], ALU.mult))
                    ins = pool.tensor_tensor(ca[:, :, x, i, :], pa[0][:], pa[1][:], op)
                    if i < L - 1 or x == 0:
                        link(ins)
            ins.then_inc(sem("ca_ok"), 1)
            pool.wait_ge(sem("dbc_in"), 16)
            dm = ident[:, (L - 1) * GC:L * GC].unsqueeze(1).broadcast_to([P, Q, GC])
            for a in range(2):
                link(pool.tensor_tensor(dbc[:, :, a, :], dbc[:, :, a, :], dm, ALU.mult))
            for k, (nm, l) in enumerate(NORMS):
                sfx = "_2" if k >= 4 else ""
                for i, gb in enumerate("gb"):
                    load(lng[:, k, i, :], w[nm + gb + sfx][l].rearrange("(k p) -> p k", p=P), "lng_in", slow=True)
            for a in range(2):
                pool.wait_ge(sem("kk_rd"), a + 1)
                pool.tensor_tensor(kk[:, a], kk[:, a], dbc[:, :, a, :], ALU.add).then_inc(sem("kk_ok"), 1)
            pool.wait_ge(sem("y_mm"), 16)
            for t in range(TT):
                load(res[:, t, :], w["x"][0, t * P:(t + 1) * P, :], "res_in")

            def ln_params(k):
                nm, l = NORMS[k]
                sfx = "_2" if k >= 4 else ""
                load(lnp[:, 0, :], w[nm + "g" + sfx][l].partition_broadcast(P), "lnp_in")
                load(lnp[:, 1, :], w[nm + "b" + sfx][l].partition_broadcast(P), "lnp_in")

            def scale_res(k):
                pool.wait_ge(sem("lnp_in"), 32 * (k + 1))
                pool.wait_ge(sem("xt_pe"), KD * (k + 1))
                for t in range(TT):
                    link(pool.tensor_tensor(res[:, t, :], res[:, t, :], lnp[:, 0, :], ALU.mult))
                    pool.tensor_tensor(res[:, t, :], res[:, t, :], lnp[:, 1, :], ALU.add).then_inc(sem("res_ok"), 1)
                pool.wait_ge(sem("res_ok"), TT * (k + 1))

            for k in range(4):
                ln_params(k)
                scale_res(k)
            for l in range(2):
                k = 4 + 2 * l
                pool.wait_ge(sem("xt_lo"), KD * k)
                load(sgp[:, 0, :], w["sgu_ln_g_2"][l].partition_broadcast(P), "sgu_in")
                load(sgp[:, 1, :], w["sgu_ln_b_2"][l].partition_broadcast(P), "sgu_in")
                load(wsn[:], w["sgu_w_2"][l].rearrange("g t s -> t g s"), "sgu_in")
                load(bsn[:], w["sgu_b_2"][l], "sgu_in")
                for t in range(TT):
                    pool.wait_ge(b_free[t], GROUPS_1 + GROUPS_2 * l + 1)
                pool.wait_ge(sem("trig_ok"), 1)
                link(rope_heads(pool, link, kvq[:, :, 0:128], 2, rot_q))
                for r in range(2):
                    link(pool.tensor_copy(kdd[:].rearrange("p t (g r d) -> p t g r d", g=2, r=2)[:, :, :, r],
                                          kvq[:, :, 0:128].rearrange("p t (g d) -> p t g d", g=2)))
                pool.wait_ge(sem("sgu_in"), 64 * (l + 1))
                for t in range(TT):
                    pool.wait_ge(sem("vs_z"), 4 * l + t + 1)
                    link(pool.tensor_tensor(vs[:, t, :], vs[:, t, :], sgp[:, 0, :], ALU.mult))
                    pool.tensor_tensor(vs[:, t, :], vs[:, t, :], sgp[:, 1, :], ALU.add).then_inc(sem("vs_ok"), 1)
                pool.wait_ge(sem("vs_ok"), 4 * (l + 1))
                pool.wait_ge(sem("ws_rd"), l + 1)
                pool.tensor_tensor(wsT[:], wsT[:], ustep[:].unsqueeze(1).broadcast_to([P, SGG, P]), ALU.mult)\
                    .then_inc(sem("ws_ok"), 1)
                for t in range(TT):
                    pool.wait_ge(b_free[t], GROUPS_1 + GROUPS_2 * l + 5)
                rope_heads(pool, link, qtok[:], NH, rot_q).then_inc(sem("q_rot"), 1)
                ln_params(k)
                pool.wait_ge(sem("xt_pe"), KD * k + 1)
                load(pin[:], w["p_2"][l, 0].rearrange("(t p) c -> p t c", p=P), "p_in")
                scale_res(k)
                ln_params(k + 1)
                if l == 0:
                    scale_res(k + 1)

        @block.tensor
        def _(pe):
            st = {"g": 0, "a": 0, "b": 0, "u": 0}

            def mm3(o, lh, ll, rh, rl, start, stop):
                pe.matmul(o, lh, rh, start=start, stop=False)
                pe.matmul(o, lh, rl, start=False, stop=False)
                return pe.matmul(o, ll, rh, start=False, stop=stop)

            def channel_major(n, k_tiles, ah, al, first, ready=None):
                g0, a0 = st["g"], st["a"]

                def body(j, i):
                    s, pair = (g0 + j) % 2, (a0 + j) % 2
                    pe.wait_ge(lo_ready, val(g0 + j + 1, i, 2))
                    if a0 + j >= 2:
                        pe.wait_ge(dve_f, val(a0 + j - 1, i, 2))
                    for o in range(2):
                        for k in range(k_tiles):
                            if ready is not None and j == 0 and i is None and o == 0:
                                pe.wait_ge(sem("xt_lo"), ready + k + 1)
                            c = (o * k_tiles + k) * P
                            ins = mm3(ps[:, 2 * pair + o, :], whi[:, s, c:c + P], wlo[:, s, c:c + P],
                                      ah[:, k, :], al[:, k, :], k == 0, k == k_tiles - 1)
                    ins.then_inc(chunk_used, 1)

                pairs(pe, n, first, 0, body)
                st["g"] += n
                st["a"] += n

            def token_major(k_tiles, width, ah, al, ready=None, between=None):
                k0 = 0
                k = 0
                while k < k_tiles:
                    s = st["g"] % 2
                    m = min(4 if width > 256 else 8, k_tiles - k)
                    if between and k + m == k_tiles:
                        between()
                    pe.wait_ge(lo_ready, st["g"] + 1)
                    if ready is not None and k == 0:
                        pe.wait_ge(sem("xt_lo"), ready + KD)
                    for t in range(TT):
                        if k == 0 and st["b"] > 0:
                            pe.wait_ge(b_free[t], st["b"])
                        for q in range(m):
                            ins = mm3(ps[:, 4 + t, 0:width], ah[:, k0 + k + q, t * P:(t + 1) * P],
                                      al[:, k0 + k + q, t * P:(t + 1) * P],
                                      whi[:, s, q * width:(q + 1) * width], wlo[:, s, q * width:(q + 1) * width],
                                      k + q == 0, k + q == k_tiles - 1)
                        if k + m == k_tiles and t < TT - 1:
                            ins.then_inc(b_done, 1)
                    ins.then_inc(chunk_used, 1)
                    st["g"] += 1
                    k += m
                st["b"] += 1

            def to_channels(k):
                for t in range(TT):
                    pe.wait_ge(sem("ln_z"), TT * k + t + 1)
                    for c in range(KD // 2 if t < TT - 1 else KD):
                        for u in ([t] if c < KD // 2 else range(TT)):
                            ins = pe.transpose(ps[:, c, u * P:(u + 1) * P], res[:, u, c * P:(c + 1) * P], ident[:, 0:P])
                        if t == TT - 1:
                            ins.then_inc(sem("xt_pe"), 1)

            def turn(name, parts, rd=None):
                for n, piece in enumerate(parts):
                    if n >= 4:
                        pe.wait_ge(*(rd[n - 4] if rd else (sem(name + "_rd"), n - 3)))
                    for t in range(TT):
                        ins = pe.transpose(ps[:, n % 4, t * P:(t + 1) * P], piece(t), ident[:, 0:P])
                    ins.then_inc(sem(name + "_pe"), 1)

            pe.wait_ge(sem("lam_in"), 48)
            pe.wait_ge(sem("c_in"), 64)
            pe.wait_ge(sem("pool_const"), 1)
            pe.wait_ge(sem("ldt_wide"), 1)
            for i in range(3):
                ins = pe.transpose(ps[:, 0, i * Q:(i + 1) * Q], lam[:, i, :], ident[0:Q, 0:Q])
            ins.then_inc(sem("lam_pe"), 1)
            for i in range(2):
                for n in range(8):
                    ins = pe.transpose(ps[:, 1 + 2 * i + n // 4, (n % 4) * P:(n % 4 + 1) * P],
                                       cn[:, i, n].rearrange("r d p -> r (d p)"), ident[:, 0:P])
            ins.then_inc(sem("c_pe"), 1)
            for n in range(8):
                if n >= 3:
                    pe.wait_ge(sem("u_rd"), n - 2)
                pe.wait_ge(sem("xg_ok"), n + 1)
                for gg in range(8):
                    ins = pe.transpose(ps[:, 5 + n % 3, gg * NC:(gg + 1) * NC], xg[:, 8 * n + gg, :],
                                       ident[0:NC, 0:NC])
                ins.then_inc(sem("u_pe"), 1)
            pe.wait_ge(sem("u_rd"), 8)
            pe.wait_ge(sem("ab_ok"), 1)
            pe.wait_ge(sem("ab_pool"), len(AB_POOL))
            pe.wait_ge(sem("ab_act"), 2)
            for m in range(16):
                if m >= 4:
                    pe.wait_ge(sem(f"mt_rd{m % 2}"), (m - 4) // 2 + 1)
                for qq in range(4):
                    ins = pe.transpose(ps[:, MB[m % 4], qq * P:(qq + 1) * P],
                                       ab[:, m // 8, 4 * (m % 8) + qq].rearrange("p j c -> p (j c)"), ident[:, 0:P])
                ins.then_inc(sem("mt_pe"), 1)
            for m in range(8):
                if m == 0:
                    pe.wait_ge(sem("mt_rd0"), 4)
                    pe.wait_ge(sem("mt_rd1"), 4)
                if m == 4:
                    pe.wait_ge(sem("mt_rd0"), 8)
                    pe.wait_ge(sem("mt_rd1"), 8)
                if m >= 2:
                    pe.wait_ge(sem(f"s_rd{m % 2}"), (m - 2) // 2 + 1)
                for qq in range(8):
                    q = 8 * (m % 4) + qq
                    for a in range(2):
                        ins = pe.matmul(ps[a * NS:(a + 1) * NS, 5 + m % 2, qq * NC:(qq + 1) * NC],
                                        mt[m // 4][:, q, a * NS:(a + 1) * NS], uu[:, 2 * q + a, :], start=True, stop=True)
                ins.then_inc(sem("s_pe"), 1)
            for a in range(2):
                for q in range(Q):
                    for r in range(2):
                        ins = pe.matmul(ps[:, 1 + a, q * GC:(q + 1) * GC], ab[a * NS:(a + 1) * NS, r, q],
                                        cc[a * NS:(a + 1) * NS, r, q, :], start=r == 0, stop=r == 1)
            ins.then_inc(sem("kk_pe"), 1)
            pe.wait_ge(sem("kk_ok"), 2)
            for i in range(L):
                for a in range(2):
                    n = 2 * i + a
                    if n >= 2:
                        pe.wait_ge(sem("tm_rd"), n - 1)
                    pe.matmul(ps[:, 1 + n % 2, :], ident[:, (L - 1 - i) * GC:(L - 1 - i) * GC + P],
                              kk[:, a].rearrange("p q c -> p (q c)"), start=True, stop=True).then_inc(sem("tm_pe"), 1)
            pe.wait_ge(sem("ca_ok"), 1)
            pe.wait_ge(sem("scan2"), 6 * (SB_J - 1))
            pe.wait_ge(sem("tm_rd"), 16)
            for m in range(16):
                if m >= 2:
                    pe.wait_ge(sem("y_rd"), m - 1)
                for a in range(2):
                    for qq in range(2):
                        q = 2 * m + qq
                        o = ps[0:NC, 2 * (m % 2) + a, qq * P:(qq + 1) * P]
                        for r in range(2):
                            pe.matmul(o, hst[a * NS:(a + 1) * NS, r, q, :], ca[a * NS:(a + 1) * NS, q, r],
                                      start=r == 0, stop=False)
                        ins = pe.matmul(o, uu[:, 2 * q + a, :], tm[:, :, a, q, :], start=False, stop=True)
                ins.then_inc(sem("y_mm"), 1)
            pe.wait_ge(sem("y_rd"), 16)
            for c in range(KD):
                if c >= 4:
                    pe.wait_ge(sem("yt_lo"), c - 3)
                for j in range(L):
                    ins = pe.transpose(ps[:, c % 4, j * NC:(j + 1) * NC], yg[:, j, c * P:(c + 1) * P], ident[0:NC, 0:NC])
                ins.then_inc(sem("yt_pe"), 1)
            pe.wait_ge(sem("yt_lo"), KD)

            def relu_mlp(k):
                for half in range(2):
                    channel_major(8, KD, xh, xl, 2 if half == 0 else 0, KD * (k - 1) if half == 0 else None)
                    pe.wait_ge(dve_l, st["a"])
                    for n in range(2):
                        token_major(16, 512, hidh, hidl)

            channel_major(KD, KD, xh, xl, 2)
            pe.wait_ge(dve_l, st["a"])
            for n in range(2):
                token_major(KD, 512, hidh, hidl)
            to_channels(0)
            relu_mlp(1)
            to_channels(1)

            token_major(KD, KVL + ROPE, xh, xl, KD)
            token_major(KD, QL, xh, xl)
            pe.wait_ge(sem("rms_ok"), 1)
            turn("lat", [lambda t, c=c: ckv[:, t, c * P:(c + 1) * P] for c in range(2)]
                 + [lambda t, c=c: cq[:, t, c * P:(c + 1) * P] for c in range(3)] + [lambda t: krd[:, t, :]])
            pe.wait_ge(sem("lat_rd"), 6)
            for c in range(2):
                s = st["g"] % 2
                pe.wait_ge(lo_ready, st["g"] + 1)
                if c > 0:
                    pe.wait_ge(sem("kn_rd"), c)
                for h in range(4):
                    for k in range(2):
                        o = k * 1024 + h * 256
                        ins = mm3(ps[:, h, :], whi[:, s, o:o + P], wlo[:, s, o:o + P], ckvh[:, k, :], ckvl[:, k, :],
                                  k == 0, k == 1)
                ins.then_inc(sem("kn_pe"), 1)
                if c > 0:
                    pe.wait_ge(sem("v_rd"), c)
                else:
                    for t in range(TT):
                        pe.wait_ge(b_free[t], st["b"])
                for t in range(TT):
                    for k in range(2):
                        def part(x):
                            v = x[:, s, k * 1024:(k + 1) * 1024].rearrange("p (h n) -> p h n", h=4)
                            return v[:, :, NOPE:NOPE + VH]
                        ins = mm3(ps[:, 4 + t, :], ckvh[:, k, t * P:(t + 1) * P], ckvl[:, k, t * P:(t + 1) * P],
                                  part(whi), part(wlo), k == 0, k == 1)
                ins.then_inc(chunk_used, 1)
                st["g"] += 1
            for c in range(4):
                s = st["g"] % 2
                pe.wait_ge(lo_ready, st["g"] + 1)
                if c == 0:
                    pe.wait_ge(sem("kn_rd"), 2)
                    pe.wait_ge(sem("v_rd"), 2)
                if c >= 2:
                    pe.wait_ge(sem("qn_rd"), c - 1)
                    pe.wait_ge(sem("qr_rd"), c - 1)
                for h in range(2):
                    for k in range(3):
                        o = k * 384 + h * 192
                        mm3(ps[:, 2 * (c % 2) + h, :], whi[:, s, o:o + P], wlo[:, s, o:o + P], cqh[:, k, :],
                            cql[:, k, :], k == 0, k == 2)
                for t in range(TT):
                    for k in range(3):
                        def part(x):
                            v = x[:, s, k * 384:(k + 1) * 384].rearrange("p (h n) -> p h n", h=2)
                            return v[:, :, NOPE:NOPE + ROPE]
                        ins = mm3(ps[:, 4 + c % 2, t * P:(t + 1) * P], cqh[:, k, t * P:(t + 1) * P],
                                  cql[:, k, t * P:(t + 1) * P], part(whi), part(wlo), k == 0, k == 2)
                ins.then_inc(chunk_used, 1)
                st["g"] += 1
            pe.wait_ge(sem("qrope_ok"), TT)
            pe.wait_ge(sem("qn_rd"), 4)
            turn("qrt", [lambda t, c=c: qrt[:, t, c * P:(c + 1) * P] for c in range(4)])
            pe.wait_ge(sem("qrt_rd"), 4)

            def attention(name, score, value, pt, per):
                units = [(h, t) for h in range(NH) for t in range(TT)]

                def scores(u):
                    if u >= 4:
                        pe.wait_ge(sem(name + "_e"), u - 3)
                    score(*units[u], ps[:, SB[u % 4], 0:(units[u][1] + 1) * P]).then_inc(sem(name + "_s"), 1)

                for u in range(3):
                    scores(u)
                for u, (h, t) in enumerate(units):
                    if u + 3 < len(units):
                        scores(u + 3)
                    pe.wait_ge(sem(name + "_pn"), u + 1)
                    if u >= 2:
                        pe.wait_ge(sem(name + "_pt"), u - 1)
                    for b in range(t + 1):
                        ins = pe.transpose(ps[:, 2 + u % 2, b * P:(b + 1) * P], pt[2][:, u % 3, b * P:(b + 1) * P],
                                           ident[:, 0:P])
                    ins.then_inc(sem(name + "_tp"), 1)
                    for hh in ([h - 1] if t == 1 and h > 0 else []) + ([h] if u == len(units) - 1 else []):
                        pe.wait_ge(sem(name + "_pt"), (hh + 1) * TT)
                        n = hh // per
                        if hh % per == 0 and n >= 2:
                            pe.wait_ge(sem(name + "_o_lo"), n - 1)
                        r0 = (hh % per) * (P // per)
                        for b in range(TT):
                            ins = pe.matmul(ps[r0:r0 + P // per, 4 + n % 2, b * P:S], value(hh, b),
                                            pt[hh % 2][:, b, b * P:S], start=b == 0, stop=b == TT - 1)
                        ins.then_inc(sem(name + "_o"), 1)

            def mla_score(h, t, o):
                n = (t + 1) * P
                r = (h % 2) * ROPE
                pe.matmul(o, qn[:, h, t * P:(t + 1) * P], kn[:, h, 0:n], start=True, stop=False)
                pe.matmul(o, qrT[r:r + ROPE, h // 2, t * P:(t + 1) * P], krT[r:r + ROPE, 0:n], start=False, stop=False)
                return pe.matmul(o[:, t * P:n], identb[:], causal[:], start=False, stop=True)

            attention("mla", mla_score, lambda h, b: vv[:, b, h * VH:(h + 1) * VH], pt1 + [pn1], 1)
            pe.wait_ge(sem("mla_o_lo"), NH)
            for n in range(2):
                token_major(KD, 512, xh, xl)
            to_channels(2)
            relu_mlp(3)
            to_channels(3)

            for l in range(2):
                kx = 4 + 2 * l
                nm = f"dsa{l}"
                assert st["b"] == GROUPS_1 + GROUPS_2 * l

                def turn_index():
                    pe.wait_ge(sem("i_rot"), l + 1)
                    turn(f"in{l}", [lambda t, c=c: kvq[:, t, 256 + c * P:256 + (c + 1) * P] for c in range(2)]
                         + [lambda t: kid[:, t, :]])

                def turn_sgu():
                    pe.wait_ge(sem("sgu_in"), 64 * (l + 1))
                    pe.wait_ge(sem("lg_rd"), 12 * (l + 1))
                    for g in range(SGG):
                        ins = pe.transpose(ps[:, g // 4, (g % 4) * P:(g % 4 + 1) * P], wsn[:, g, :], ident[:, 0:P])
                    ins.then_inc(sem("ws_pe"), 1)
                    pe.transpose(ps[:, 2, 0:SGG], bsn[:], ident[0:SGG, 0:SGG]).then_inc(sem("ws_pe"), 1)

                def spatial_gate():
                    pe.wait_ge(sem("ws_ok"), l + 1)
                    pe.wait_ge(sem("bs_rd"), l + 1)
                    pe.wait_ge(sem("vs_ok"), 4 * (l + 1))
                    for g in range(SGG):
                        ins = pe.matmul(ps[:, g // 2, (g % 2) * 256:(g % 2 + 1) * 256], wsT[:, g, :],
                                        vs[:, :, g * 64:(g + 1) * 64], start=True, stop=True)
                    ins.then_inc(sem("sg_pe"), 1)

                token_major(KD, 512, xh, xl, KD * (kx - 1))
                token_major(KD, 68, xh, xl)
                token_major(KD, 512, xh, xl, between=turn_index)
                pe.wait_ge(sem(f"in{l}_rd"), 3)
                for t in range(1, TT):
                    n = (t + 1) * P
                    for h in range(NI):
                        if t >= 2:
                            pe.wait_ge(sem("lg_rd"), 4 * (3 * l + t - 2) + h + 1)
                        r = (h % 2) * IXD
                        pe.matmul(ps[:, h, 0:n], qiT[r:r + IXD, h // 2, t * P:(t + 1) * P], kiT[r:r + IXD, 0:n],
                                  start=True, stop=True).then_inc(sem("lg_pe"), 1)
                token_major(KD, 512, xh, xl, between=turn_sgu)
                token_major(KD, 512, xh, xl, between=spatial_gate)
                pe.wait_ge(sem("bo_ok"), l + 1)
                pe.wait_ge(sem("q_rot"), l + 1)
                turn(f"bo{l}", [lambda t, c=c: kdd[:, t, c * P:(c + 1) * P] for c in range(2)]
                     + [lambda t, c=c: gu[:, t, c * P:(c + 1) * P] for c in range(4)]
                     + [lambda t, c=c: qtok[:, t, c * P:(c + 1) * P] for c in range(4)],
                     [(sem(f"kt{l}_rd"), c + 1) for c in range(2)] + [(sem(f"bo{l}_rd"), c + 1) for c in range(4)])
                pe.wait_ge(sem(f"qt{l}_rd"), 4)

                def dsa_score(h, t, o):
                    r = (h % 2) * HD
                    if h == 0:
                        pe.wait_ge(sem("mask_ok"), TT * l + t + 1)
                    pe.matmul(o, qT[r:r + HD, h // 2, t * P:(t + 1) * P], kT[r:r + HD, h // 4, 0:(t + 1) * P],
                              start=True, stop=False)
                    return pe.matmul(o, identb[:], mask[:, t, 0:(t + 1) * P], start=False, stop=True)

                attention(nm, dsa_score, lambda h, b: kvq[:, b, 128 + (h // 4) * HD:128 + (h // 4 + 1) * HD],
                          pt2 + [pn2], 2)
                pe.wait_ge(sem(nm + "_o_lo"), 4)
                for n in range(2):
                    token_major(KD, 512, xh, xl)
                to_channels(kx)
                pe.wait_ge(sem("p_in"), 16 * (l + 1))
                pe.wait_ge(sem("xt_lo"), KD * (kx + 1))
                turn(f"pt{l}", [lambda t, c=c: pin[:, t, c * P:(c + 1) * P] for c in range(2)])
                pe.wait_ge(sem(f"pt{l}_rd"), 2)
                for n in range(2):
                    token_major(2, 512, pTh, pTl)
                    token_major(KD, 512, xh, xl)
                for half in range(2):
                    channel_major(11, KD, xh, xl, 0)
                    pe.wait_ge(dve_l, st["a"])
                    for n in range(2):
                        token_major(11, 512, hidh, hidl)
                if l == 0:
                    to_channels(kx + 1)

        @block.scalar
        def _(act):
            st = {"g": 0, "a": 0, "b": 0, "s": 0}
            seq = sem("act_seq")

            def link(ins):
                st["s"] += 1
                ins.then_inc(seq, 1)
                act.wait_ge(seq, st["s"])

            def split(g, i=None):
                if g >= n_chunks:
                    return
                s, n = g % 2, chunk_cols[g]
                act.wait_ge(landed[s], val(32 * (g // 2 + 1), i, 32))
                if g >= 2:
                    act.wait_ge(chunk_used, val(g - 1, i, 2))
                act.activation(whi[:, s, 0:n], raw[:, s, 0:n], ACT.Copy).then_inc(hi_ready, 1)

            def channel_major(n, kind, first):
                g0, a0 = st["g"], st["a"]
                tail = 0 if all(c == chunk_cols[g0] for c in chunk_cols[g0:g0 + n + 2]) else 2

                def body(j, i):
                    pair = (a0 + j) % 2
                    a = a0 + j
                    act.wait_ge(chunk_used, val(g0 + j + 1, i, 2))
                    if a >= 1:
                        act.wait_ge(dve_f, val(a, i, 2))
                    if kind == "relu2":
                        act.activation(rt[:], ps[:, 2 * pair:2 * pair + 2, :].rearrange("p b n -> p (b n)"),
                                       ACT.Relu).then_inc(act_r, 1)
                    elif kind == "glu":
                        act.activation(rt[:, 0:S], ps[:, 2 * pair + 1, :], ACT.Sigmoid).then_inc(act_r, 1)
                    else:
                        act.activation(rt[:, 0:S], ps[:, 2 * pair, :], ACT.Silu).then_inc(act_r, 1)
                    split(g0 + j + 2, i)
                    act.wait_ge(dve_f, val(a + 1, i, 2))
                    idx = j if i is None else i * 2 + j
                    if kind == "relu2":
                        o = hidh[:, 2 * j:2 * j + 2, :] if i is None else hidh[:, bass.ds(i * 4 + 2 * j, 2), :]
                        act.activation(o, ft[:].rearrange("p (b n) -> p b n", b=2), ACT.Copy).then_inc(act_h, 1)
                    else:
                        o = hidh[:, j:j + 1, :] if i is None else hidh[:, bass.ds(i * 2 + j, 1), :]
                        act.activation(o, ft[:, 0:S].rearrange("p (b n) -> p b n", b=1), ACT.Copy).then_inc(act_h, 1)

                pairs(act, n, first, tail, body)
                st["g"] += n
                st["a"] += n

            def token_major(k_tiles, width, evac=None, hold=False, between=None):
                k = 0
                while k < k_tiles:
                    m = min(4 if width > 256 else 8, k_tiles - k)
                    if between and k + m == k_tiles:
                        between()
                    k += m
                    st["g"] += 1
                    if k == k_tiles:
                        if evac:
                            for t in range(TT):
                                if t < TT - 1:
                                    act.wait_ge(b_done, 3 * st["b"] + t + 1)
                                else:
                                    act.wait_ge(chunk_used, st["g"])
                                evac(t, ps[:, 4 + t, 0:width])
                        st["b"] += 1
                    if not (hold and k == k_tiles):
                        split(st["g"] + 1)

            def row_norms(x, n0, var_sem, sd_sem, rs_sem, z_sem):
                for t in range(TT + 1):
                    if t < TT:
                        act.wait_ge(var_sem, n0 + t + 1)
                        act.activation(sd[:, t:t + 1], mv[:, t, 1:2], ACT.Sqrt, bias=consts[:, 0:1]).then_inc(sd_sem, 1)
                    if t > 0:
                        act.wait_ge(rs_sem, n0 + t)
                        act.activation(x[:, t - 1, :], x[:, t - 1, :], ACT.Identity, scale=rstd[:, t - 1:t],
                                       bias=nmr[:, t - 1:t]).then_inc(z_sem, 1)

            def norm(k, last=False):
                row_norms(res, TT * k, sem("ln_var"), sem("ln_sd"), sem("ln_rs"), sem("ln_z"))
                for c in range(KD if not last else 0):
                    act.wait_ge(sem("xt_f"), KD * k + c + 1)
                    act.activation(xh[:, c, :], xf(c), ACT.Copy).then_inc(sem("xt_hi"), 1)
                split(st["g"] + 1)

            def trig(sn, cs, r, absr):
                act.activation(sn, r, ACT.Sin)
                link(act.activation(absr, r, ACT.Abs))
                return act.activation(cs, absr, ACT.Sin, scale=-1.0, bias=consts[:, 2:3])

            act.wait_ge(sem("x_in"), 16)
            for n in range(8):
                act.activation(xg[:, 8 * n:8 * n + 8, :].rearrange("p g (j c) -> p g j c", j=L),
                               xc[:, :, n * P:(n + 1) * P].rearrange("p j (g c) -> p g j c", g=8),
                               ACT.Copy).then_inc(sem("xg_ok"), 1)
            act.wait_ge(sem("pool_const"), 1)
            act.wait_ge(sem("lam_rd"), 1)
            act.activation(sc[:, 3, :], sc[:, 2, :], ACT.Exp).then_inc(sem("dt_ok"), 1)
            act.wait_ge(sem("ang_ok"), 1)
            act.activation(sc[:, 10, :], sc[:, 4, :], ACT.Exp).then_inc(sem("mag_ok"), 1)
            trig(sc[:, 8, :], sc[:, 9, :], sc[:, 6, :], sc[:, 7, :]).then_inc(sem("mag_ok"), 1)
            for n in range(8):
                act.wait_ge(sem("u_pe"), n + 1)
                act.activation(uu[:, 8 * n:8 * n + 8, :], ps[:, 5 + n % 3, :].rearrange("p (g c) -> p g c", g=8),
                               ACT.Copy).then_inc(sem("u_rd"), 1)
            act.wait_ge(sem("bb_ok"), 1)
            for r in range(2):
                act.activation(ab[:, r, :, L - 1, :], bb[:, r], ACT.Copy).then_inc(sem("ab_act"), 1)

            def mt_copy(m):
                act.wait_ge(sem("mt_pe"), m + 1)
                n = m % 8
                act.activation(mt[m // 8][:, 4 * n:4 * n + 4, :], ps[:, MB[m % 4], :].rearrange("p (q c) -> p q c", q=4),
                               ACT.Copy).then_inc(sem("mt_rd0"), 1)

            for m in range(0, 16, 2):
                mt_copy(m)
            for m in range(0, 8, 2):
                act.wait_ge(sem("s_pe"), m + 1)
                n = m % 4
                act.activation(sst[:, m // 4, 8 * n:8 * n + 8, :], ps[:, 5 + m % 2, :].rearrange("p (q c) -> p q c", q=8),
                               ACT.Copy).then_inc(sem("s_rd0"), 1)
            for a in range(2):
                act.wait_ge(sem("kk_pe"), 1)
                act.activation(kk[:, a], ps[:, 1 + a, :].rearrange("p (q c) -> p q c", c=GC), ACT.Copy)\
                   .then_inc(sem("kk_rd"), 1)
            for n in range(16):
                act.wait_ge(sem("tm_pe"), n + 1)
                act.activation(tm[:, n // 2, n % 2], ps[:, 1 + n % 2, :].rearrange("p (q c) -> p q c", q=Q),
                               ACT.Copy).then_inc(sem("tm_rd"), 1)
            act.wait_ge(sem("ang_ok"), 2)
            trig(sin1[:].rearrange("p t k -> p (t k)"), cos1[:].rearrange("p t k -> p (t k)"),
                 ang[:, 0, 0:128], ang[:, 1, 0:128])
            trig(sin2[:].rearrange("p t k -> p (t k)"), cos2[:].rearrange("p t k -> p (t k)"),
                 ang[:, 0, 128:160], ang[:, 1, 128:160]).then_inc(sem("trig_ok"), 1)
            for m in range(16):
                act.wait_ge(sem("y_mm"), m + 1)
                for a in range(2):
                    q0 = 2 * m
                    o = yg[:, :, q0 * 32:q0 * 32 + 64].rearrange("p j (q a c) -> p q a j c", q=2, a=2)[:, :, a]
                    v = ps[0:NC, 2 * (m % 2) + a, 0:256].rearrange("p (q j c) -> p q j c", q=2, j=L)
                    ins = act.activation(o, v, ACT.Gelu_apprx_tanh)
                ins.then_inc(sem("y_rd"), 1)
            for c in range(KD):
                act.wait_ge(sem("yt_pe"), c + 1)
                act.activation(xh[:, c, :].rearrange("p (n j) -> p n j", j=L),
                               ps[:, c % 4, :].rearrange("p (j n) -> p n j", j=L), ACT.Copy).then_inc(sem("yt_hi"), 1)
                if c == 5:
                    split(0)
            split(1)

            def relu_mlp(last_k):
                for half in range(2):
                    channel_major(8, "relu2", 0)
                    for n in range(2):
                        token_major(16, 512, hold=half == 1 and n == 1)
                norm(last_k)

            channel_major(KD, "glu", 2)
            token_major(KD, 512)
            token_major(KD, 512, hold=True)
            norm(0)
            relu_mlp(1)

            def keep(dst):
                def evac(t, src):
                    act.activation(dst(t), src, ACT.Copy).then_inc(b_free[t], 1)
                return evac

            token_major(KD, KVL + ROPE, keep(lambda t: ckv[:, t, :]))
            token_major(KD, QL, keep(lambda t: cq[:, t, :]))
            for t in range(TT):
                act.wait_ge(b_free[t], st["b"])
            for t in range(TT):
                link(act.activation(junk[:, 0:KVL], ckv[:, t, 0:KVL], ACT.Square, accum_out=mv[:, t, 0:1]))
                link(act.activation(junk[:], cq[:, t, :], ACT.Square, accum_out=mv[:, t, 1:2]))
            link(act.activation(bst[:, :, 0, 0:1], mv[:, :, 0:1], ACT.Sqrt, scale=1.0 / KVL, bias=consts[:, 1:2]))
            act.activation(bst[:, :, 1, 0:1], mv[:, :, 1:2], ACT.Sqrt, scale=1.0 / QL, bias=consts[:, 1:2])\
               .then_inc(sem("rms_sd"), 1)
            for n, (dst, g) in enumerate([(ckvh[:, c, :], kvg[:, c:c + 1]) for c in range(2)]
                                         + [(cqh[:, c, :], qg[:, c:c + 1]) for c in range(3)]):
                act.wait_ge(sem("lat_pe"), n + 1)
                act.activation(dst, ps[:, n % 4, :], ACT.Identity, scale=g).then_inc(sem("lat_hi"), 1)
            for c in range(2):
                st["g"] += 1
                act.wait_ge(sem("kn_pe"), c + 1)
                act.activation(kn[:, 4 * c:4 * c + 4, :], ps[:, 0:4, :], ACT.Copy).then_inc(sem("kn_rd"), 1)
                split(st["g"] + 1)
            for c in range(4):
                st["g"] += 1
                act.wait_ge(chunk_used, st["g"])
                act.activation(qrt[:, :, c * P:(c + 1) * P], ps[:, 4 + c % 2, :].rearrange("p (t n) -> p t n", t=TT),
                               ACT.Copy).then_inc(sem("qr_rd"), 1)
                split(st["g"] + 1)
            for n in range(4):
                act.wait_ge(sem("qrt_pe"), n + 1)
                act.activation(qrT[:, n, :], ps[:, n % 4, :], ACT.Copy, scale=SM_SCALE).then_inc(sem("qrt_rd"), 1)

            def attention(name, pt, per, dst):
                def exps(u):
                    n = (u % TT + 1) * P
                    act.wait_ge(sem(name + "_mx"), u + 1)
                    if u >= 3:
                        act.wait_ge(sem(name + "_tp"), u - 2)
                    act.activation(pt[2][:, u % 3, 0:n], ps[:, SB[u % 4], 0:n], ACT.Exp,
                                   bias=nmax[:, u % 4:u % 4 + 1],
                                   accum_out=rsum[:, u % 4:u % 4 + 1]).then_inc(sem(name + "_e"), 1)

                def high(n0):
                    act.wait_ge(sem(name + "_o"), (n0 + 1) * per)
                    act.activation(xh[:, dst + n0, :], ps[:, 4 + n0 % 2, :], ACT.Copy).then_inc(sem(name + "_o_hi"), 1)

                exps(0)
                exps(1)
                for u in range(NH * TT):
                    h, t = u // TT, u % TT
                    if u + 2 < NH * TT:
                        exps(u + 2)
                    act.wait_ge(sem(name + "_tp"), u + 1)
                    if t == 0 and h >= 2:
                        act.wait_ge(sem(name + "_o"), h - 1)
                    act.activation(pt[h % 2][:, 0:t + 1, t * P:(t + 1) * P],
                                   ps[:, 2 + u % 2, 0:(t + 1) * P].rearrange("p (b n) -> p b n", n=P),
                                   ACT.Copy).then_inc(sem(name + "_pt"), 1)
                    if t == 2 and h >= per and h % per == 0:
                        high(h // per - 1)
                high(NH // per - 1)

            attention("mla", pt1 + [pn1], 1, 0)
            token_major(KD, 512)
            token_major(KD, 512, hold=True)
            norm(2)
            relu_mlp(3)

            for l in range(2):
                kx = 4 + 2 * l
                token_major(KD, 512, keep(lambda t: kvq[:, t, :]))
                token_major(KD, 68, keep(lambda t: kiw[:, t, :]))

                def gelu(dst):
                    def evac(t, src):
                        act.activation(dst[:, t, :], src, ACT.Gelu_apprx_tanh).then_inc(b_free[t], 1)
                    return evac

                def index_turned():
                    for n, dst in enumerate([qiT[:, c, :] for c in range(2)] + [kiT[:]]):
                        act.wait_ge(sem(f"in{l}_pe"), n + 1)
                        act.activation(dst, ps[:, n % 4, :], ACT.Copy).then_inc(sem(f"in{l}_rd"), 1)

                def sgu_turned():
                    act.wait_ge(sem("ws_pe"), 2 * l + 2)
                    act.activation(wsT[:], ps[:, 0:2, :].rearrange("p b (g n) -> p (b g) n", n=P), ACT.Copy)\
                       .then_inc(sem("ws_rd"), 1)
                    act.activation(bsT[:], ps[:, 2, 0:SGG], ACT.Copy).then_inc(sem("bs_rd"), 1)

                token_major(KD, 512, gelu(vs), between=index_turned)
                for t in range(1, TT):
                    for h in range(NI):
                        m = 4 * (3 * l + t - 1) + h
                        act.wait_ge(sem("lg_pe"), m + 1)
                        if t >= 3:
                            act.wait_ge(sem("sc_ok"), 4 * (3 * l + t - 3) + h + 1)
                        act.activation(rl[t % 2][:, h, 0:(t + 1) * P], ps[:, h, 0:(t + 1) * P], ACT.Relu)\
                           .then_inc(sem("lg_rd"), 1)
                row_norms(vs, TT * l, sem("vs_var"), sem("vs_sd"), sem("vs_rs"), sem("vs_z"))
                token_major(KD, 512, gelu(gu), between=sgu_turned)
                act.wait_ge(sem("sc_ok"), 12 * (l + 1))
                token_major(KD, 512, keep(lambda t: qtok[:, t, :]))
                for n, (dst, scale, what) in enumerate([(kT[:, c, :], 1.0, f"kt{l}_rd") for c in range(2)]
                                                       + [(xh[:, 4 + c, :], 1.0, f"bo{l}_hi") for c in range(4)]
                                                       + [(qT[:, c, :], HD ** -0.5, f"qt{l}_rd") for c in range(4)]):
                    act.wait_ge(sem(f"bo{l}_pe"), n + 1)
                    act.activation(dst, ps[:, n % 4, :], ACT.Copy, scale=scale).then_inc(sem(what), 1)
                attention(f"dsa{l}", pt2 + [pn2], 2, 0)
                token_major(KD, 512)
                token_major(KD, 512, hold=True)
                norm(kx)
                for n in range(2):
                    act.wait_ge(sem(f"pt{l}_pe"), n + 1)
                    act.activation(pTh[:, n, :], ps[:, n, :], ACT.Copy).then_inc(sem(f"pt{l}_hi"), 1)
                for n in range(2):
                    def ple_evac(t, src, n=n):
                        if n == 1:
                            act.wait_ge(sem("pg_ok"), 8 * l + t + 1)
                        act.activation(plt[:, t, :], src, ACT.Copy).then_inc(b_free[t], 1)

                    def gate_evac(t, src, n=n):
                        m = 8 * l + 4 * n + t
                        if m >= 2:
                            act.wait_ge(sem("pg_ok"), m - 1)
                        act.activation((rt, ft)[t % 2][:, 0:512], src, ACT.Sigmoid).then_inc(sem("pg_sig"), 1)

                    token_major(2, 512, ple_evac)
                    token_major(KD, 512, gate_evac)
                act.wait_ge(sem("pg_ok"), 8 * (l + 1))
                for half in range(2):
                    channel_major(11, "swiglu", 0)
                    for n in range(2):
                        token_major(11, 512, hold=half == 1 and n == 1)
                norm(kx + 1, last=l == 1)

        @block.vector
        def _(dve):
            st = {"g": 0, "a": 0, "b": 0, "s": 0}
            seq = sem("dve_seq")

            def link(ins):
                st["s"] += 1
                ins.then_inc(seq, 1)
                dve.wait_ge(seq, st["s"])

            def split(g, i=None):
                if g >= n_chunks:
                    return
                s, n = g % 2, chunk_cols[g]
                dve.wait_ge(hi_ready, val(g + 1, i, 2))
                dve.tensor_tensor(wlo[:, s, 0:n], raw[:, s, 0:n], f32(whi[:, s, 0:n]), ALU.subtract).then_inc(lo_ready, 1)

            def channel_major(n, kind, first):
                g0, a0 = st["g"], st["a"]
                tail = 0 if all(c == chunk_cols[g0] for c in chunk_cols[g0:g0 + n + 2]) else 2

                def body(j, i):
                    pair = (a0 + j) % 2
                    a = a0 + j
                    dve.wait_ge(act_r, val(a + 1, i, 2))
                    if a >= 1:
                        dve.wait_ge(act_h, val(a, i, 2))
                        dve.wait_ge(dve_l, val(a, i, 2))
                    if kind == "relu2":
                        dve.tensor_tensor(ft[:], rt[:], rt[:], ALU.mult).then_inc(dve_f, 1)
                    elif kind == "glu":
                        dve.tensor_tensor(ft[:, 0:S], rt[:, 0:S], ps[:, 2 * pair, :], ALU.mult).then_inc(dve_f, 1)
                    else:
                        dve.tensor_tensor(ft[:, 0:S], rt[:, 0:S], ps[:, 2 * pair + 1, :], ALU.mult).then_inc(dve_f, 1)
                    split(g0 + j + 2, i)
                    dve.wait_ge(act_h, val(a + 1, i, 2))
                    if kind == "relu2":
                        sl = slice(2 * j, 2 * j + 2) if i is None else bass.ds(i * 4 + 2 * j, 2)
                        v = ft[:].rearrange("p (b n) -> p b n", b=2)
                    else:
                        sl = slice(j, j + 1) if i is None else bass.ds(i * 2 + j, 1)
                        v = ft[:, 0:S].rearrange("p (b n) -> p b n", b=1)
                    dve.tensor_tensor(hidl[:, sl, :], v, f32(hidh[:, sl, :]), ALU.subtract).then_inc(dve_l, 1)

                pairs(dve, n, first, tail, body)
                st["g"] += n
                st["a"] += n

            def token_major(k_tiles, width, evac=None, hold=False):
                k = 0
                while k < k_tiles:
                    m = min(4 if width > 256 else 8, k_tiles - k)
                    k += m
                    st["g"] += 1
                    if k == k_tiles:
                        if evac:
                            for t in range(TT):
                                if t < TT - 1:
                                    dve.wait_ge(b_done, 3 * st["b"] + t + 1)
                                else:
                                    dve.wait_ge(chunk_used, st["g"])
                                evac(t, ps[:, 4 + t, 0:width])
                        st["b"] += 1
                    if not (hold and k == k_tiles):
                        split(st["g"] + 1)

            def stats(x, t, width, name):
                for h in range(width // 512):
                    link(dve.bn_stats(bst[:, t, h, :], x[:, t, 512 * h:512 * h + 512]))
                dve.bn_aggr(mv[:, t, :], bst[:, t, 0:width // 512, :].rearrange("p h k -> p (h k)")).then_inc(sem(name), 1)

            def inverse(t, sd_sem, sd_n, rs_sem):
                dve.wait_ge(sd_sem, sd_n)
                link(dve.reciprocal(rstd[:, t:t + 1], sd[:, t:t + 1]))
                dve.scalar_tensor_tensor(out=nmr[:, t:t + 1], in0=mv[:, t, 0:1], scalar=-1.0, in1=rstd[:, t:t + 1],
                                         op0=ALU.mult, op1=ALU.mult).then_inc(rs_sem, 1)

            def add_to_res(n, alpha, half=None, k=0, res_n=0):
                def evac(t, src):
                    r = res[:, t, 512 * n:512 * n + 512]
                    if st["b"] > 0:
                        dve.wait_ge(b_free[t], st["b"])
                    if res_n:
                        dve.wait_ge(sem("res_ok"), TT * (res_n - 1) + t + 1)
                    dve.scalar_tensor_tensor(out=r, in0=r, scalar=alpha, in1=src, op0=ALU.mult, op1=ALU.add)\
                       .then_inc(b_free[t], 1)
                    if half is not None:
                        dve.wait_ge(b_free[t], st["b"] + 1)
                        link(dve.bn_stats(bst[:, t, half, :], r))
                        if half == 1:
                            dve.bn_aggr(mv[:, t, :], bst[:, t, :, :].rearrange("p h k -> p (h k)")).then_inc(sem("ln_var"), 1)
                            if t > 0:
                                inverse(t - 1, sem("ln_sd"), TT * k + t, sem("ln_rs"))
                            if t == TT - 1:
                                inverse(t, sem("ln_sd"), TT * k + TT, sem("ln_rs"))
                return evac

            def norm(k, last=False):
                if k == 0:
                    dve.wait_ge(sem("lng_in"), 16 * (2 * N_LN + 2))
                for c in range(KD + 1 if not last else 0):
                    if c < KD:
                        dve.wait_ge(sem("xt_pe"), KD * k + c + 1)
                        dve.tensor_scalar(xf(c), ps[:, c, :], lng[:, k, 0, c:c + 1], lng[:, k, 1, c:c + 1],
                                          ALU.mult, ALU.add).then_inc(sem("xt_f"), 1)
                    if c > 0:
                        dve.wait_ge(sem("xt_hi"), KD * k + c)
                        dve.tensor_tensor(xl[:, c - 1, :], xf(c - 1), f32(xh[:, c - 1, :]), ALU.subtract)\
                           .then_inc(sem("xt_lo"), 1)
                if last:
                    dve.wait_ge(sem("lnp_in"), 32 * (k + 1))
                    for t in range(TT):
                        dve.wait_ge(sem("ln_z"), TT * k + t + 1)
                        link(dve.tensor_tensor(res[:, t, :], res[:, t, :], lnp[:, 0, :], ALU.mult))
                        dve.tensor_tensor(res[:, t, :], res[:, t, :], lnp[:, 1, :], ALU.add).then_inc(sem("out_ok"), 1)
                else:
                    dve.wait_ge(sem("xt_lo"), KD * (k + 1))
                split(st["g"] + 1)

            dve.wait_ge(sem("lam_in"), 48)
            dve.tensor_copy(lam[:, 2, :].rearrange("q (a p) -> q a p", a=2),
                            ldt[:].unsqueeze(2).broadcast_to([Q, 2, NS])).then_inc(sem("ldt_wide"), 1)
            def wrap(x, n):
                link(dve.tensor_scalar(n, x, 1 / (2 * math.pi), MAGIC, ALU.mult, ALU.add))
                link(dve.tensor_scalar(n, n, -MAGIC, None, ALU.add))
                for c in TWO_PI:
                    link(dve.scalar_tensor_tensor(out=x, in0=n, scalar=-c, in1=x, op0=ALU.mult, op1=ALU.add))
                return dve.tensor_scalar(x, x, -PI_IN, PI_IN, ALU.max, ALU.min)

            dve.wait_ge(sem("lam_pe"), 1)
            dve.tensor_copy(sc[:, 0:3, :], ps[:, 0, 0:3 * Q].rearrange("p (i q) -> p i q", i=3)).then_inc(sem("lam_rd"), 1)
            dve.wait_ge(sem("dt_ok"), 1)
            for i in range(2):
                link(dve.tensor_tensor(sc[:, 4 + i, :], sc[:, i, :], sc[:, 3, :], ALU.mult))
            link(dve.tensor_copy(sc[:, 6, :], sc[:, 5, :]))
            wrap(sc[:, 6, :], sc[:, 7, :]).then_inc(sem("ang_ok"), 1)
            dve.wait_ge(sem("mag_ok"), 2)
            link(dve.memset(pw[:, 0, 0, :], 1.0))
            link(dve.memset(pw[:, 1, 0, :], 0.0))
            link(dve.tensor_tensor(pw[:, 0, 1, :], sc[:, 10, :], sc[:, 9, :], ALU.mult))
            link(dve.tensor_tensor(pw[:, 1, 1, :], sc[:, 10, :], sc[:, 8, :], ALU.mult))
            link(dve.tensor_scalar(sc[:, 12, :], pw[:, 0, 1, :], -1.0, None, ALU.add))
            for o, a, b in ((13, 0, 0), (14, 1, 1)):
                link(dve.tensor_tensor(sc[:, o, :], sc[:, a, :], sc[:, b, :], ALU.mult))
            link(dve.tensor_tensor(sc[:, 13, :], sc[:, 13, :], sc[:, 14, :], ALU.add))
            link(dve.reciprocal(sc[:, 14, :], sc[:, 13, :]))
            link(dve.tensor_tensor(sc[:, 15, :], sc[:, 12, :], sc[:, 0, :], ALU.mult))
            link(dve.tensor_tensor(sc[:, 16, :], pw[:, 1, 1, :], sc[:, 1, :], ALU.mult))
            link(dve.tensor_tensor(sc[:, 15, :], sc[:, 15, :], sc[:, 16, :], ALU.add))
            link(dve.tensor_tensor(sc[:, 15, :], sc[:, 15, :], sc[:, 14, :], ALU.mult))
            link(dve.tensor_tensor(sc[:, 16, :], pw[:, 1, 1, :], sc[:, 0, :], ALU.mult))
            link(dve.tensor_tensor(sc[:, 17, :], sc[:, 12, :], sc[:, 1, :], ALU.mult))
            link(dve.tensor_tensor(sc[:, 16, :], sc[:, 16, :], sc[:, 17, :], ALU.subtract))
            link(dve.tensor_tensor(sc[:, 16, :], sc[:, 16, :], sc[:, 14, :], ALU.mult))

            for lo, n in ((1, 1), (1, 2), (1, 4)):
                top = n
                bc = lambda r: pw[:, r, top:top + 1, :].broadcast_to([P, n, Q])
                t0, t1 = (rt[:, 512 * i:512 * i + n * Q].rearrange("p (n q) -> p n q", n=n) for i in range(2))
                dve.wait_ge(sem("c_pe"), 1)
                cmul(dve, link, pw[:, 0, top + 1:top + 1 + n, :], pw[:, 1, top + 1:top + 1 + n, :],
                     pw[:, 0, 1:1 + n, :], pw[:, 1, 1:1 + n, :], bc(0), bc(1), t0, t1).then_inc(sem("pw_ok"), 1)
                dve.wait_ge(sem("pw_ok"), {1: 1, 2: 2, 4: 3}[n])
            for r in range(2):
                for a in range(2):
                    v = ps[a * NS:(a + 1) * NS, 1 + 2 * r:3 + 2 * r, :].rearrange("p b (q a c) -> p (b q) a c", a=2, c=GC)
                    ins = dve.tensor_scalar(cc[a * NS:(a + 1) * NS, r], v[:, :, a, :], 1.0 - 2.0 * r, None, ALU.mult)
                    ins.then_inc(sem("c_rd"), 1)
            dve.wait_ge(sem("c_rd"), 4)

            dve.wait_ge(sem("b_in"), 32)
            T0, T1 = (x[:, 0:512].rearrange("p (q c) -> p q c", c=GC) for x in (rt, ft))
            cmul(dve, link, bb[:, 0], bb[:, 1], wide(sc[:, 15, :]), wide(sc[:, 16, :]), b_in[:, 0], b_in[:, 1], T0, T1)\
                .then_inc(sem("bb_ok"), 1)
            dve.wait_ge(sem("bb_ok"), 1)
            for j in range(AB_POOL[0]):
                k = L - 1 - j
                ins = cmul(dve, link, ab[:, 0, :, j, :], ab[:, 1, :, j, :], wide(pw[:, 0, k, :]), wide(pw[:, 1, k, :]),
                           bb[:, 0], bb[:, 1], T0, T1)
                if j < AB_POOL[0] - 1:
                    link(ins)
            ins.then_inc(sem("ab_ok"), 1)
            for m in range(1, 16, 2):
                dve.wait_ge(sem("mt_pe"), m + 1)
                n = m % 8
                dve.tensor_copy(mt[m // 8][:, 4 * n:4 * n + 4, :], ps[:, MB[m % 4], :].rearrange("p (q c) -> p q c", q=4))\
                   .then_inc(sem("mt_rd1"), 1)
            for m in range(1, 8, 2):
                dve.wait_ge(sem("s_pe"), m + 1)
                n = m % 4
                dve.tensor_copy(sst[:, m // 4, 8 * n:8 * n + 8, :], ps[:, 5 + m % 2, :].rearrange("p (q c) -> p q c", q=8))\
                   .then_inc(sem("s_rd1"), 1)
            NB = NC // SB_J
            dve.wait_ge(sem("s_rd0"), 4)
            dve.wait_ge(sem("s_rd1"), 4)

            def blocks(x):
                return x[:].rearrange("p a q (b j) -> p a q b j", j=SB_J)

            def at_j(x, j):
                return blocks(x)[:, :, :, :, bass.ds(j, 1)].rearrange("p a q b o -> p a q (b o)")

            e = rt[:, 0:512].rearrange("p (a q b) -> p a q b", a=2, b=NB)
            t0 = rt[:, 512:1024].rearrange("p (a q b) -> p a q b", a=2, b=NB)
            t1 = ft[:, 0:512].rearrange("p (a q b) -> p a q b", a=2, b=NB)

            def step(name, i, first, ar, ai, h, sv, h2, u0, u1):
                sm, n = sem(name), lambda k: i * 6 + (k - 6 * first)
                dve.tensor_tensor(u0, ar, h, ALU.mult).then_inc(sm, 1)
                dve.tensor_tensor(u1[:, 0], ai, h[:, 1], ALU.mult).then_inc(sm, 1)
                dve.tensor_tensor(u1[:, 1], ai, h[:, 0], ALU.mult).then_inc(sm, 1)
                dve.wait_ge(sm, n(3))
                dve.tensor_tensor(u0, u0, sv, ALU.add).then_inc(sm, 1)
                dve.wait_ge(sm, n(4))
                dve.tensor_tensor(h2[:, 0], u0[:, 0], u1[:, 0], ALU.subtract).then_inc(sm, 1)
                dve.tensor_tensor(h2[:, 1], u0[:, 1], u1[:, 1], ALU.add).then_inc(sm, 1)
                dve.wait_ge(sm, n(6))

            a64 = a64t[:]
            link(dve.tensor_copy(a64, pw[:, :, L, :]))
            for _ in range(3):
                x, y = a64[:, 0], a64[:, 1]
                dve.tensor_tensor(t1[:, 0, :, 0], x, x, ALU.mult)
                dve.tensor_tensor(t1[:, 0, :, 1], y, y, ALU.mult)
                link(dve.tensor_tensor(t1[:, 0, :, 2], x, y, ALU.mult))
                dve.tensor_tensor(x, t1[:, 0, :, 0], t1[:, 0, :, 1], ALU.subtract)
                link(dve.tensor_scalar(y, t1[:, 0, :, 2], 2.0, None, ALU.mult))
            a8r = pw[:, 0, L, :].unsqueeze(1).unsqueeze(3).broadcast_to([P, 2, Q, NB])
            a8i = pw[:, 1, L, :].unsqueeze(2).broadcast_to([P, Q, NB])
            link(dve.memset(hst[:, :, :, 0], 0.0))
            link(dve.tensor_copy(e, blocks(sst)[:, :, :, :, 0]))
            with dve.Fori(1, SB_J) as j:
                step("scan1", j, 1, a8r, a8i, e, at_j(sst, j), e, t0, t1)
            link(dve.tensor_copy(hst[:, :, :, SB_J], e[:, :, :, 0]))
            with dve.Fori(1, NB - 1) as b:
                def first_of(x, o):
                    return x[:, :, :, bass.ds(b * SB_J + o, 1)].rearrange("p a q o -> p a (q o)")
                step("carry", b, 1, a64[:, 0].unsqueeze(1).broadcast_to([P, 2, Q]), a64[:, 1], first_of(hst, 0),
                     e[:, :, :, bass.ds(b, 1)].rearrange("p a q o -> p a (q o)"), first_of(hst, SB_J),
                     t0[:, :, :, 0], t1[:, :, :, 0])
            with dve.Fori(0, SB_J - 1) as j:
                step("scan2", j, 0, a8r, a8i, at_j(hst, j), at_j(sst, j), at_j(hst, j + 1), t0, t1)
            dve.wait_ge(sem("pos_in"), 32)
            link(dve.tensor_copy(posf[:], posi[:]))
            v1 = ang[:, 0, 0:128].rearrange("p (t k) -> p t k", t=TT)
            v2 = ang[:, 0, 128:160].rearrange("p (t k) -> p t k", t=TT)
            link(dve.tensor_tensor(v1, posf[:, 0, :].unsqueeze(2).broadcast_to([P, TT, 32]),
                                   inv1[:].unsqueeze(1).broadcast_to([P, TT, 32]), ALU.mult))
            link(dve.tensor_tensor(v2, posf[:, 1, :].unsqueeze(2).broadcast_to([P, TT, 8]),
                                   inv2[:].unsqueeze(1).broadcast_to([P, TT, 8]), ALU.mult))
            wrap(ang[:, 0, :], ang[:, 1, :]).then_inc(sem("ang_ok"), 1)
            for c in range(KD):
                dve.wait_ge(sem("yt_hi"), c + 1)
                dve.tensor_tensor(xl[:, c, :].rearrange("p (n j) -> p n j", j=L),
                                  ps[:, c % 4, :].rearrange("p (j n) -> p n j", j=L),
                                  f32(xh[:, c, :]).rearrange("p (n j) -> p n j", j=L), ALU.subtract).then_inc(sem("yt_lo"), 1)
            split(0)
            split(1)

            def relu_mlp(k):
                for half in range(2):
                    channel_major(8, "relu2", 0)
                    for n in range(2):
                        token_major(16, 512, add_to_res(n, ALPHA if half == 0 else 1.0, n if half == 1 else None, k,
                                                        k if half == 0 else 0), hold=half == 1 and n == 1)
                norm(k)

            def out_proj(k):
                token_major(KD, 512, add_to_res(0, ALPHA, 0, k, k))
                token_major(KD, 512, add_to_res(1, ALPHA, 1, k, k), hold=True)
                norm(k)

            channel_major(KD, "glu", 2)
            dve.wait_ge(sem("res_in"), 16 * TT)
            out_proj(0)
            relu_mlp(1)

            token_major(KD, KVL + ROPE)
            token_major(KD, QL)

            dve.wait_ge(sem("rms_sd"), 1)
            link(dve.reciprocal(mv[:], bst[:, :, :, 0]))
            for t in range(TT):
                link(dve.tensor_scalar(ckv[:, t, 0:KVL], ckv[:, t, 0:KVL], mv[:, t, 0:1], None, ALU.mult))
                link(dve.tensor_scalar(cq[:, t, :], cq[:, t, :], mv[:, t, 1:2], None, ALU.mult))
            link(rope(dve, link, ckv[:, :, KVL:KVL + 32], ckv[:, :, KVL + 32:KVL + 64], cos1[:], sin1[:],
                      krd[:, :, 0:32], krd[:, :, 32:64],
                      [rt[:, 128 * i:128 * i + 128].rearrange("p (t k) -> p t k", t=TT) for i in range(4)]))
            dve.tensor_copy(krd[:, :, 64:128], krd[:, :, 0:64]).then_inc(sem("rms_ok"), 1)
            for n, (lo, hi, g) in enumerate([(ckvl[:, c, :], ckvh[:, c, :], kvg[:, c:c + 1]) for c in range(2)]
                                            + [(cql[:, c, :], cqh[:, c, :], qg[:, c:c + 1]) for c in range(3)]):
                dve.wait_ge(sem("lat_hi"), n + 1)
                dve.scalar_tensor_tensor(out=lo, in0=ps[:, n % 4, :], scalar=g, in1=f32(hi), op0=ALU.mult,
                                         op1=ALU.subtract).then_inc(sem("lat_rd"), 1)
            dve.wait_ge(sem("lat_pe"), 6)
            dve.tensor_copy(krT[:], ps[:, 1, :]).then_inc(sem("lat_rd"), 1)
            for c in range(2):
                st["g"] += 1
                dve.wait_ge(chunk_used, st["g"])
                ins = dve.tensor_copy(vv[:, :, 512 * c:512 * c + 512], ps[:, 4:8, :])
                ins.then_inc(sem("v_rd"), 1)
                split(st["g"] + 1)
            for c in range(4):
                st["g"] += 1
                dve.wait_ge(chunk_used, st["g"])
                dve.tensor_scalar(qn[:, 2 * c:2 * c + 2, :], ps[:, 2 * (c % 2):2 * (c % 2) + 2, :], SM_SCALE, None,
                                  ALU.mult).then_inc(sem("qn_rd"), 1)
                split(st["g"] + 1)
            dve.wait_ge(sem("qr_rd"), 4)
            for t in range(TT):
                v = qrt[:, t, :].rearrange("p (h d) -> p h d", h=NH)
                cs, sn = (x[:, t:t + 1, :].broadcast_to([P, NH, 32]) for x in (cos1, sin1))
                rope(dve, link, v[:, :, 0:32], v[:, :, 32:64], cs, sn, v[:, :, 0:32], v[:, :, 32:64],
                     [rt[:, 256 * i:256 * i + 256].rearrange("p (h k) -> p h k", h=NH) for i in range(4)])\
                    .then_inc(sem("qrope_ok"), 1)
                dve.wait_ge(sem("qrope_ok"), t + 1)

            def attention(name, pt, per, dst):
                def first(u):
                    n = (u % TT + 1) * P
                    dve.wait_ge(sem(name + "_s"), u + 1)
                    dve.tensor_reduce(nmax[:, u % 4:u % 4 + 1], ps[:, SB[u % 4], 0:n], axis=AX.X, op=ALU.max,
                                      negate=True).then_inc(sem(name + "_mx"), 1)

                def low(n0):
                    dve.wait_ge(sem(name + "_o_hi"), n0 + 1)
                    dve.tensor_tensor(xl[:, dst + n0, :], ps[:, 4 + n0 % 2, :], f32(xh[:, dst + n0, :]), ALU.subtract)\
                       .then_inc(sem(name + "_o_lo"), 1)

                for u in range(3):
                    first(u)
                for u in range(NH * TT):
                    h, t = u // TT, u % TT
                    n = (t + 1) * P
                    dve.wait_ge(sem(name + "_e"), u + 1)
                    link(dve.reciprocal(rinv[:, u % 4:u % 4 + 1], rsum[:, u % 4:u % 4 + 1]))
                    dve.tensor_scalar(pt[2][:, u % 3, 0:n], pt[2][:, u % 3, 0:n], rinv[:, u % 4:u % 4 + 1], None,
                                      ALU.mult).then_inc(sem(name + "_pn"), 1)
                    if u + 3 < NH * TT:
                        first(u + 3)
                    if t == 3 and h >= per and h % per == 0:
                        low(h // per - 1)
                low(NH // per - 1)

            attention("mla", pt1 + [pn1], 1, 0)
            out_proj(2)
            relu_mlp(3)

            for l in range(2):
                kx = 4 + 2 * l
                token_major(KD, 512)
                token_major(KD, 68)
                for t in range(TT):
                    dve.wait_ge(b_free[t], st["b"])
                rope_heads(dve, link, kvq[:, :, 256:512], NI, rot_i).then_inc(sem("i_rot_q"), 1)
                dve.wait_ge(sem("i_rot_q"), l + 1)
                link(rope_heads(dve, link, kiw[:, :, 0:64], 1, rot_i))
                link(dve.tensor_scalar(kiw[:, :, 64:68], kiw[:, :, 64:68], (NI * IXD) ** -0.5, None, ALU.mult))
                link(dve.tensor_copy(kid[:, :, 0:64], kiw[:, :, 0:64]))
                dve.tensor_copy(kid[:, :, 64:128], kiw[:, :, 0:64]).then_inc(sem("i_rot"), 1)
                token_major(KD, 512)
                for t in range(1, TT):
                    n = (t + 1) * P
                    for h in range(NI):
                        m = 4 * (3 * l + t - 1) + h
                        dve.wait_ge(sem("lg_rd"), m + 1)
                        wcol = kiw[:, t, 64 + h:65 + h]
                        x = rl[t % 2][:, h, 0:n]
                        if h == 0:
                            ins = dve.tensor_scalar(scr[:, t - 1, 0:n], x, wcol, None, ALU.mult)
                        else:
                            ins = dve.scalar_tensor_tensor(out=scr[:, t - 1, 0:n], in0=x, scalar=wcol,
                                                           in1=scr[:, t - 1, 0:n], op0=ALU.mult, op1=ALU.add)
                        ins.then_inc(sem("sc_ok"), 1)
                        dve.wait_ge(sem("sc_ok"), m + 1)
                for t in range(TT):
                    dve.wait_ge(b_free[t], st["b"])
                    stats(vs, t, SGW, "vs_var")
                for t in range(TT):
                    inverse(t, sem("vs_sd"), 4 * l + t + 1, sem("vs_rs"))
                g0 = st["g"]
                st["g"] += 4
                st["b"] += 2

                def gate():
                    dve.wait_ge(sem("sg_pe"), l + 1)
                    dve.wait_ge(sem("bs_rd"), l + 1)
                    for g in range(SGG):
                        v = ps[:, g // 2, (g % 2) * 256:(g % 2 + 1) * 256].rearrange("p (t c) -> p t c", t=TT)
                        o = gu[:, :, g * 64:(g + 1) * 64]
                        ins = dve.scalar_tensor_tensor(out=o, in0=v, scalar=bsT[:, g:g + 1], in1=o, op0=ALU.add,
                                                       op1=ALU.mult)
                    ins.then_inc(sem("bo_ok"), 1)

                def gated_low():
                    for n in range(4):
                        dve.wait_ge(sem(f"bo{l}_hi"), n + 1)
                        dve.tensor_tensor(xl[:, 4 + n, :], ps[:, (n + 2) % 4, :], f32(xh[:, 4 + n, :]), ALU.subtract)\
                           .then_inc(sem(f"bo{l}_rd"), 1)

                meanwhile = {(1, 11): lambda: split(g0 + 2), (2, 3): lambda: split(g0 + 3),
                             (2, 11): lambda: split(g0 + 4), (2, 15): gate, (3, 3): lambda: split(g0 + 5),
                             (3, 8): gated_low}
                dve.tensor_copy(mask[:, 0, 0:P], chunkm[:]).then_inc(sem("mask_ok"), 1)
                for t in range(1, TT):
                    n = (t + 1) * P
                    x = scr[:, t - 1, 0:n]
                    link(dve.tensor_tensor(x[:, n - P:n], x[:, n - P:n], chunkm[:], ALU.add))
                    for r in range(TOPK // 8):
                        link(dve.max(m8[:], x))
                        link(dve.match_replace(x, m8[:], x, TAKEN))
                        if (t, r) in meanwhile:
                            meanwhile[t, r]()
                    dve.tensor_scalar(mask[:, t, 0:n], x, TAKEN / 2, NEG, ALU.is_gt, ALU.mult)\
                       .then_inc(sem("mask_ok"), 1)
                attention(f"dsa{l}", pt2 + [pn2], 2, 0)
                out_proj(kx)
                for n in range(2):
                    dve.wait_ge(sem(f"pt{l}_hi"), n + 1)
                    dve.tensor_tensor(pTl[:, n, :], ps[:, n, :], f32(pTh[:, n, :]), ALU.subtract).then_inc(sem(f"pt{l}_rd"), 1)

                for n in range(2):
                    def gate_evac(t, src, n=n):
                        m = 8 * l + 4 * n + t
                        dve.wait_ge(sem("pg_sig"), m + 1)
                        x = (rt, ft)[t % 2][:, 0:512]
                        dve.tensor_tensor(x, x, plt[:, t, :], ALU.mult).then_inc(b_free[t], 1)
                        dve.wait_ge(b_free[t], st["b"] + 1)
                        r = res[:, t, 512 * n:512 * n + 512]
                        dve.wait_ge(sem("res_ok"), TT * kx + t + 1)
                        dve.scalar_tensor_tensor(out=r, in0=r, scalar=ALPHA, in1=x, op0=ALU.mult, op1=ALU.add)\
                           .then_inc(sem("pg_ok"), 1)
                    token_major(2, 512)
                    token_major(KD, 512, gate_evac)
                for half in range(2):
                    channel_major(11, "swiglu", 0)
                    for n in range(2):
                        token_major(11, 512, add_to_res(n, 1.0, n if half == 1 else None, kx + 1),
                                    hold=half == 1 and n == 1)
                norm(kx + 1, last=l == 1)


IXD = 64
GROUPS_1 = 14
GROUPS_2 = 15

_INS = ['x', 'positions', 'ln_mix_g', 'ln_mix_b', 'ln_ffn_g', 'ln_ffn_b', 'w_ff1', 'w_ff2', 'ssm_lam_re',
        'ssm_lam_im', 'ssm_log_dt', 'ssm_b_re', 'ssm_b_im', 'ssm_c_re', 'ssm_c_im', 'ssm_d', 'ssm_w_glu',
        'ssm_w_out', 'kv_w_a', 'kv_norm_g', 'kv_w_b', 'q_w_a', 'q_norm_g', 'q_w_b', 'attn_w_o', 'p_2',
        'positions_2', 'w_in_2', 'w_o_2', 'ln1_g_2', 'ln1_b_2', 'ln2_g_2', 'ln2_b_2', 'sgu_w_2', 'sgu_b_2',
        'sgu_ln_g_2', 'sgu_ln_b_2', 'w_ffn_in_2', 'w_ffn_out_2', 'w_ple_2', 'w_ple_gate_2']


def kernel(**inputs):
    import numpy as _np
    import concourse.bacc as _bacc
    from concourse import mybir as _mybir
    from concourse.bass_utils import run_bass_kernel_spmd as _run

    nc = _bacc.Bacc("TRN2", target_bir_lowering=False, num_devices=1)
    arrays, w = {}, {}
    for name in _INS:
        a = _np.ascontiguousarray(inputs[name])
        arrays[f"in_{name}_dram"] = a
        w[name] = nc.dram_tensor(f"in_{name}_dram", a.shape, _mybir.dt.from_np(a.dtype), kind="ExternalInput").ap()
    out = nc.dram_tensor("out_0_dram", (1, S, D), _mybir.dt.float32, kind="ExternalOutput").ap()
    two_blocks(nc, w, out)
    r = _run(nc, [arrays], core_ids=[0])
    return r.results[0]["out_0_dram"]
```

```python
import math
from contextlib import ExitStack

import concourse.bass as bass
from concourse import mybir

F32 = mybir.dt.float32
F32R = mybir.dt.float32r
I32 = mybir.dt.int32
BF16 = mybir.dt.bfloat16
ALU = mybir.AluOpType
ACT = mybir.ActivationFunctionType
AX = mybir.AxisListType

P = 128
D = 1024
S = 512
TT = S // P
KD = D // P
FF1 = 4 * D
FF2 = 2816
DEPTH = 2
ALPHA = (2 * DEPTH) ** 0.25
LN_EPS, RMS_EPS = 1e-5, 1e-6
G, GC, NS = 64, 16, 64
L = 8
NC = S // L
Q = G // 2
NH, NOPE, ROPE, VH, QL, KVL = 8, 128, 64, 128, 384, 256
SM_SCALE = (NOPE + ROPE) ** -0.5
THETA1, THETA2 = 10000.0, 500000.0
HD, NI, TOPK, ROT = 64, 4, 128, 16
IN2_GROUPS = ((512, 512), (1024, 68), (1604, 512), (1092, 512), (0, 512))
SGW, SGG, PLE = 512, 8, 256
MB = (3, 4, 7, 0)
AB_POOL = (5, 6)
SB_J = 8
SB = (0, 1, 6, 7)
GATE_BANKS = (2, 3, 4, 5)
CAP = 2048
NEG = -1.0e30
TAKEN = -3.0e38
MAGIC = 12582912.0
NORMS = [("ln_mix_", 0), ("ln_ffn_", 0), ("ln_mix_", 1), ("ln_ffn_", 1), ("ln1_", 0), ("ln2_", 0), ("ln1_", 1), ("ln2_", 1)]
N_LN = len(NORMS)
TWO_PI = (6.28125, 0.0019350051879882812, 3.019916050e-07)
PI_IN = 3.1415925


def stages_of(w):
    out = []

    def add(name, n, cols, parts):
        out.append((name, n, cols, parts))

    def rows(x, k0, nk, c0, nc):
        return x[k0 * P:(k0 + nk) * P, c0:c0 + nc].rearrange("(k p) n -> p k n", p=P)

    def cols_at(x, j, step, base, width):
        v = x.rearrange("(k p) n -> p k n", p=P)
        if isinstance(j, int):
            return v[:, :, base + j * step:base + j * step + width]
        return v[:, :, bass.ds(j * step + base, width)]

    def channel(name, x, n, c0, c1, step):
        k = x.shape[0]
        add(name, n, 2 * k, lambda j: [(0, cols_at(x, j, step, c0, P)), (k, cols_at(x, j, step, c1, P))])

    def token(name, x, k0, nk, c0, nc):
        at = 0
        while at < nk:
            m = min(4 if nc > 256 else 8, nk - at)
            h = (m + 1) // 2
            add(name, 1, m * nc, lambda j, a=at, m=m, h=h: [
                (0, rows(x, k0 + a, h, c0, nc)), (h * nc, rows(x, k0 + a + h, m - h, c0, nc))])
            at += m

    channel("glu", w["ssm_w_glu"][0], KD, 0, D, P)
    for n in range(2):
        token("ssm_out", w["ssm_w_out"][0], 0, KD, 512 * n, 512)

    def relu_mlp(l):
        for half in range(2):
            c0 = half * FF1 // 2
            channel("ff_in", w["w_ff1"][l], 8, c0, c0 + P, 2 * P)
            for n in range(2):
                token("ff_out", w["w_ff2"][l], half * 16, 16, 512 * n, 512)

    relu_mlp(0)
    token("kv_a", w["kv_w_a"], 0, KD, 0, KVL + ROPE)
    token("q_a", w["q_w_a"][0], 0, KD, 0, QL)
    for c in range(2):
        add("kv_b", 1, 2048, lambda j, c=c: [(k * 1024, rows(w["kv_w_b"], k, 1, 1024 * c, 1024)) for k in range(2)])
    for c in range(4):
        add("q_b", 1, 1152, lambda j, c=c: [(0, rows(w["q_w_b"][0], 0, 2, 384 * c, 384)),
                                            (768, rows(w["q_w_b"][0], 2, 1, 384 * c, 384))])
    for n in range(2):
        token("attn_o", w["attn_w_o"][0], 0, KD, 512 * n, 512)
    relu_mlp(1)
    for l in range(2):
        wi = w["w_in_2"][l]
        for c0, nc in IN2_GROUPS:
            token("w_in", wi, 0, KD, c0, nc)
        for n in range(2):
            token("w_o", w["w_o_2"][l], 0, KD, 512 * n, 512)
        for n in range(2):
            token("ple", w["w_ple_2"][l], 0, 2, 512 * n, 512)
            token("ple_gate", w["w_ple_gate_2"][l], 0, KD, 512 * n, 512)
        for half in range(2):
            channel("ffn_in", w["w_ffn_in_2"][l], 11, half * 11 * P, FF2 + half * 11 * P, P)
            for n in range(2):
                token("ffn_out", w["w_ffn_out_2"][l], half * 11, 11, 512 * n, 512)
    return out


def two_blocks(nc, w, out):
    stream = stages_of(w)
    chunk_cols = [c for _, n, c, _ in stream for _ in range(n)]
    n_chunks = len(chunk_cols)
    first = [name for name, _, _, _ in stream].index("w_in")
    per_layer = sum(n for _, n, _, _ in stream[first:]) // 2
    LAYER_CHUNK = [n_chunks - 2 * per_layer, n_chunks - per_layer]

    with ExitStack() as ctx:
        sems = {}

        def sem(name):
            if name not in sems:
                sems[name] = ctx.enter_context(nc.semaphore(name))
            return sems[name]

        base = -(-nc.sbuf_base // 32) * 32
        KB = 1024

        def at(name, kb, shape, dt=F32):
            return nc.alloc_sbuf_tensor_at(name, shape, dt, offset=base + int(kb * KB))

        ctx.enter_context(nc.sbuf_tensor("arena_fence", [P, 207 * 256], F32))
        raw = at("raw", 0, [P, 2, CAP])
        whi = at("whi", 16, [P, 2, CAP], F32R)
        wlo = at("wlo", 32, [P, 2, CAP], F32R)
        res = at("res", 48, [P, TT, D])
        xh = at("xh", 64, [P, KD, S], F32R)
        xl = at("xl", 80, [P, KD, S], F32R)
        lnp = at("lnp", 96, [P, 2, D])
        rt = at("rt", 104, [P, 1024])
        ft = at("ft", 108, [P, 1024])
        ident = at("ident", 112, [P, 240])
        causal = at("causal", 113, [P, P], BF16)
        identb = at("identb", 113.25, [P, P], BF16)
        scratch = at("scratch", 113.5, [P, P])
        lng = at("lng", 114, [P, N_LN, 2, KD])
        chunkm = at("chunkm", 115, [P, P])
        cos1 = at("cos1", 115.5, [P, TT, 32])
        sin1 = at("sin1", 116, [P, TT, 32])
        cos2 = at("cos2", 116.5, [P, TT, 8])
        sin2 = at("sin2", 116.625, [P, TT, 8])
        pw = at("pw", 116.75, [P, 2, 9, Q])
        bst = at("bst", 119, [P, TT, 2, 6])
        mv = at("mv", 119.25, [P, TT, 2])
        sd = at("sd", 119.375, [P, TT])
        rstd = at("rstd", 119.4375, [P, TT])
        m8 = at("m8", 119.5, [P, 8])
        nmax = at("nmax", 119.5625, [P, 4])
        rsum = at("rsum", 119.625, [P, 4])
        rinv = at("rinv", 119.6875, [P, 4])
        consts = at("consts", 119.75, [P, 4])
        kvg = at("kvg", 119.8125, [P, 2])
        qg = at("qg", 119.875, [P, 3])
        bsT = at("bsT", 119.9375, [P, SGG])
        ustep = at("ustep", 120, [P, P])
        nmr = at("nmr", 120.5, [P, TT])
        AR = 120.75
        hidh = at("hidh", AR, [P, 16, S], F32R)
        hidl = at("hidl", AR + 32, [P, 16, S], F32R)
        xc = at("xc", AR, [NC, L, D])
        xg = at("xg", 64, [NC, G, L * GC])
        yg = at("yg", AR, [NC, L, D])
        ab = at("ab", AR + 32, [P, 2, Q, L, GC])
        tm = at("tm", AR + 32, [P, L, 2, Q, GC])
        mt = [at("mt_re", AR + 64, [P, Q, P]), at("mt_im", 80, [P, Q, P])]
        ca = at("ca", 16, [P, Q, 2, L, GC])
        pa = [at("pa0", 0, [P, Q, GC]), at("pa1", 2, [P, Q, GC])]
        b_in = at("b_in", AR + 64, [P, 2, Q, GC])
        bb = at("bb", AR + 68, [P, 2, Q, GC])
        sc = at("sc", AR + 72, [P, 20, Q])
        lam = at("lam", AR + 76, [Q, 3, P])
        ldt = at("ldt", AR + 78, [Q, 2])
        cc = at("cc", AR + 80, [P, 2, Q, GC])
        cn = at("cn", 104, [P, 2, 8, 2, NS])
        kk = at("kk", 96, [P, 2, Q, GC])
        dbc = at("dbc", 100, [P, Q, 2, GC])
        uu = at("uu", 48, [P, G, NC])
        sst = at("sst", 64, [P, 2, Q, NC])
        hst = at("hst", 80, [P, 2, Q, NC])
        ang = at("ang", AR + 84, [P, 2, 160])
        posi = at("posi", AR + 85.25, [P, 2, TT], I32)
        posf = at("posf", AR + 85.3125, [P, 2, TT])
        inv1 = at("inv1", AR + 85.375, [P, 32])
        inv2 = at("inv2", AR + 85.5, [P, 8])
        a64t = at("a64t", AR + 85.5625, [P, 2, Q])
        ckv = at("ckv", AR, [P, TT, KVL + ROPE])
        cq = at("cq", AR + 32, [P, TT, QL])
        krd = at("krd", AR + 11, [P, TT, 2 * ROPE])
        junk = at("junk", AR + 38, [P, 2, TT, QL])
        kn = at("kn", AR, [P, NH, S])
        vv = at("vv", AR + 16, [P, TT, NH * VH])
        qn = at("qn", AR + 32, [P, NH, S])
        qrT = at("qrT", AR + 48, [P, NH // 2, S])
        krT = at("krT", AR + 56, [P, S])
        qrt = at("qrt", AR + 58, [P, TT, NH * ROPE])
        ckvh = at("ckvh", AR + 66, [P, 2, S], F32R)
        ckvl = at("ckvl", AR + 70, [P, 2, S], F32R)
        cqh = at("cqh", AR + 74, [P, 3, S], F32R)
        cql = at("cql", AR + 80, [P, 3, S], F32R)
        pn1 = at("pn1", AR + 58, [P, 3, S])
        pt1 = [at("pt1a", AR + 64, [P, TT, S]), at("pt1b", AR + 72, [P, TT, S])]
        qT = at("qT", AR, [P, 4, S])
        kT = at("kT", AR + 8, [P, 2, S])
        qiT = at("qiT", AR + 12, [P, 2, S])
        kiT = at("kiT", AR + 16, [P, S])
        kvq = at("kvq", AR + 18, [P, TT, 512])
        qtok = at("qtok", AR + 26, [P, TT, 512])
        gu = at("gu", AR + 34, [P, TT, 512])
        vs = at("vs", AR + 42, [P, TT, 512])
        kiw = at("kiw", AR + 50, [P, TT, 68])
        kid = at("kid", AR + 52, [P, TT, 128])
        kdd = at("kdd", AR + 54, [P, TT, 256])
        mask = at("mask", AR + 58, [P, TT, S], BF16)
        scr = at("scr", AR + 66, [P, 3, S])
        pn2 = at("pn2", AR + 66, [P, 3, S])
        pt2 = [at("pt2a", AR + 26, [P, TT, S]), at("pt2b", AR + 76, [P, TT, S])]
        rl = [at("rl_a", AR + 76, [P, NI, S]), at("rl_b", AR + 26, [P, NI, S])]
        rot_i = at("rot_i", AR + 62, [P, 4, TT * 4 * 8])
        rot_q = at("rot_q", AR + 72, [P, 4, TT * 8 * 8])
        wsn = at("wsn", 104, [P, SGG, P])
        wsT = at("wsT", 108, [P, SGG, P])
        sgp = at("sgp", 96, [P, 2, SGW])
        bsn = at("bsn", AR + 84, [SGG, P])
        pin = at("pin", AR + 64, [P, TT, PLE])
        pTh = at("pTh", AR + 68, [P, 2, S], F32R)
        pTl = at("pTl", AR + 72, [P, 2, S], F32R)
        plt = at("plt", AR + 76, [P, TT, 512])
        ps = ctx.enter_context(nc.psum_tensor("ps", [P, 8, 512], F32))

        landed = [sem("landed0"), sem("landed1")]
        hi_ready = sem("hi_ready")
        lo_ready = sem("lo_ready")
        chunk_used = sem("chunk_used")
        act_r = sem("act_r")
        dve_f = sem("dve_f")
        act_h = sem("act_h")
        dve_l = sem("dve_l")
        b_done = sem("b_done")
        b_free = [sem(f"b_free{t}") for t in range(TT)]

        def val(b, i, per):
            return b if i is None else i * per + b

        def pairs(eng, n, first, tail, body):
            m = (n - first - tail) // 2
            for j in range(first):
                body(j, None)
            if m > 1:
                with eng.Fori(0, m) as i:
                    body(first, i)
                    body(first + 1, i)
            else:
                m = 0
            for j in range(first + 2 * m, n):
                body(j, None)

        def xf(c):
            return (rt, ft)[c // 2 % 2][:, S * (c % 2):S * (c % 2 + 1)]

        def f32(x):
            return x.bitcast(F32)

        def rope(eng, link, x1, x2, cs, sn, o1, o2, t):
            eng.tensor_tensor(t[0], x1, cs, ALU.mult)
            eng.tensor_tensor(t[1], x2, sn, ALU.mult)
            eng.tensor_tensor(t[2], x1, sn, ALU.mult)
            link(eng.tensor_tensor(t[3], x2, cs, ALU.mult))
            eng.tensor_tensor(o1, t[0], t[1], ALU.subtract)
            return eng.tensor_tensor(o2, t[2], t[3], ALU.add)

        def cmul(eng, link, o_re, o_im, x_re, x_im, y_re, y_im, t0, t1):
            link(eng.tensor_tensor(t0, x_re, y_re, ALU.mult))
            link(eng.tensor_tensor(t1, x_im, y_im, ALU.mult))
            link(eng.tensor_tensor(o_re, t0, t1, ALU.subtract))
            link(eng.tensor_tensor(t0, x_re, y_im, ALU.mult))
            link(eng.tensor_tensor(t1, x_im, y_re, ALU.mult))
            return eng.tensor_tensor(o_im, t0, t1, ALU.add)

        def wide(x):
            return x.unsqueeze(2).broadcast_to([P, Q, GC])

        def rope_heads(eng, link, x, n, room):
            r = ROT // 2
            v = x.rearrange("p t (h d) -> p t h d", d=HD)
            cs, sn = (y[:].unsqueeze(2).broadcast_to([P, TT, n, r]) for y in (cos2, sin2))
            t = [room[:, i, 0:TT * n * r].rearrange("p (t h k) -> p t h k", t=TT, h=n) for i in range(4)]
            return rope(eng, link, v[:, :, :, 0:r], v[:, :, :, r:2 * r], cs, sn, v[:, :, :, 0:r], v[:, :, :, r:2 * r], t)

        block = ctx.enter_context(nc.Block())

        @block.sync
        def _(sp):
            for i, nm in enumerate(("ssm_lam_re", "ssm_lam_im")):
                sp.dma_start(lam[:, i, :].rearrange("q (a p) -> q a p", a=2),
                             w[nm][0].rearrange("(q a) p -> q a p", a=2)).then_inc(sem("lam_in"), 16)
            sp.dma_start(ldt[:], w["ssm_log_dt"][0].rearrange("(q a) -> q a", a=2)).then_inc(sem("lam_in"), 16)
            for i, nm in enumerate(("ssm_c_re", "ssm_c_im")):
                for d in range(2):
                    sp.dma_start(cn[:, i, :, d, :], w[nm][0].rearrange("(n g) c p -> (g c) n p", g=8))\
                      .then_inc(sem("c_in"), 16)
            sp.dma_start(xc[:], w["x"][0].rearrange("(c j) d -> c j d", j=L)).then_inc(sem("x_in"), 16)
            for i, nm in enumerate(("ssm_b_re", "ssm_b_im")):
                sp.dma_start(b_in[:, i], w[nm][0].rearrange("(q a) p c -> (a p) q c", a=2)).then_inc(sem("b_in"), 16)
            sp.wait_ge(sem("ca_ok"), 1)
            g = 0

            def load(g0, parts, cols, j, i):
                gg = g0 + j
                if gg >= 2:
                    sp.wait_ge(lo_ready, val(gg - 1, i, 2))
                s = gg % 2
                idx = j if i is None else i * 2 + j
                for c0, src in parts(idx):
                    k, m = src.shape[1], src.shape[2]
                    dst = raw[:, s, c0:c0 + k * m].rearrange("p (k n) -> p k n", k=k)
                    sp.dma_start(dst, src).then_inc(landed[s], 16)

            for name, n, cols, parts in stream:
                pairs(sp, n, 2 if g == 0 else 0, 0, lambda j, i: load(g, parts, cols, j, i))
                g += n
            for t in range(TT):
                sp.wait_ge(sem("out_ok"), t + 1)
                sp.dma_start(out[0, t * P:(t + 1) * P, :], res[:, t, :]).then_inc(sem("stored"), 16)
            sp.wait_ge(sem("stored"), 16 * TT)

        @block.gpsimd
        def _(pool):
            seq = sem("pool_seq")
            n = [0]

            def link(ins):
                n[0] += 1
                ins.then_inc(seq, 1)
                pool.wait_ge(seq, n[0])

            def load(dst, src, name, slow=False):
                pool.dma_start(dst, src, allow_slow_non_contiguous=slow).then_inc(sem(name), 16)

            link(pool.memset(ident[:], 0.0))
            link(pool.memset(scratch[:], 0.0))
            link(pool.memset(chunkm[:], 0.0))
            link(pool.memset(ustep[:], 1.0))
            link(pool.affine_select(out=ustep[:], in_=ustep[:], compare_op=ALU.is_ge, fill=0.0, base=0,
                                    pattern=[[1, P]], channel_multiplier=-1))
            link(pool.affine_select(out=ident[:], in_=ident[:], compare_op=ALU.not_equal, fill=1.0, base=0,
                                    pattern=[[-1, 240]], channel_multiplier=1))
            link(pool.affine_select(out=scratch[:], in_=scratch[:], compare_op=ALU.is_ge,
                                    fill=NEG, base=0, pattern=[[-1, P]], channel_multiplier=1))
            link(pool.tensor_copy(causal[:], scratch[:]))
            link(pool.tensor_copy(identb[:], ident[:, 0:P]))
            link(pool.memset(chunkm[0:64, 64:128], NEG))
            for i, v in enumerate((LN_EPS, RMS_EPS, math.pi / 2)):
                pool.memset(consts[:, i:i + 1], v).then_inc(sem("ident_ok"), 1)
            pool.wait_ge(sem("ident_ok"), 3)
            for i in range(32):
                pool.memset(inv1[:, i:i + 1], THETA1 ** (-i / 32))
            for i in range(8):
                ins = pool.memset(inv2[:, i:i + 1], THETA2 ** (-2.0 * i / ROT))
            ins.then_inc(sem("pool_const"), 1)
            for i, nm in enumerate(("positions", "positions_2")):
                load(posi[:, i, :], w[nm][0].rearrange("(t p) -> p t", p=P), "pos_in", slow=True)
            load(dbc[:].rearrange("p q a c -> p (q a c)"), w["ssm_d"][0].partition_broadcast(P), "dbc_in")
            load(kvg[:], w["kv_norm_g"].rearrange("(k p) -> p k", p=P), "lng_in", slow=True)
            load(qg[:], w["q_norm_g"][0].rearrange("(k p) -> p k", p=P), "lng_in", slow=True)
            pool.wait_ge(sem("bb_ok"), 1)
            for j in AB_POOL:
                ins = cmul(pool, link, ab[:, 0, :, j, :], ab[:, 1, :, j, :], wide(pw[:, 0, L - 1 - j, :]),
                           wide(pw[:, 1, L - 1 - j, :]), bb[:, 0], bb[:, 1], pa[0][:], pa[1][:])
                ins.then_inc(sem("ab_pool"), 1)
                pool.wait_ge(sem("ab_pool"), j - AB_POOL[0] + 1)
            pool.wait_ge(sem("c_rd"), 4)
            for i in range(L):
                wd = [wide(pw[:, x, i + 1, :]) for x in range(2)]
                for x, op in ((0, ALU.add), (1, ALU.subtract)):
                    pool.tensor_tensor(pa[0][:], cc[:, x], wd[0], ALU.mult)
                    link(pool.tensor_tensor(pa[1][:], cc[:, 1 - x], wd[1], ALU.mult))
                    ins = pool.tensor_tensor(ca[:, :, x, i, :], pa[0][:], pa[1][:], op)
                    if i < L - 1 or x == 0:
                        link(ins)
            ins.then_inc(sem("ca_ok"), 1)
            pool.wait_ge(sem("dbc_in"), 16)
            dm = ident[:, (L - 1) * GC:L * GC].unsqueeze(1).broadcast_to([P, Q, GC])
            for a in range(2):
                link(pool.tensor_tensor(dbc[:, :, a, :], dbc[:, :, a, :], dm, ALU.mult))
            for k, (nm, l) in enumerate(NORMS):
                sfx = "_2" if k >= 4 else ""
                for i, gb in enumerate("gb"):
                    load(lng[:, k, i, :], w[nm + gb + sfx][l].rearrange("(k p) -> p k", p=P), "lng_in", slow=True)
            for a in range(2):
                pool.wait_ge(sem("kk_rd"), a + 1)
                pool.tensor_tensor(kk[:, a], kk[:, a], dbc[:, :, a, :], ALU.add).then_inc(sem("kk_ok"), 1)
            pool.wait_ge(sem("y_mm"), 16)
            for t in range(TT):
                load(res[:, t, :], w["x"][0, t * P:(t + 1) * P, :], "res_in")

            def ln_params(k):
                nm, l = NORMS[k]
                sfx = "_2" if k >= 4 else ""
                load(lnp[:, 0, :], w[nm + "g" + sfx][l].partition_broadcast(P), "lnp_in")
                load(lnp[:, 1, :], w[nm + "b" + sfx][l].partition_broadcast(P), "lnp_in")

            def scale_res(k):
                pool.wait_ge(sem("lnp_in"), 32 * (k + 1))
                pool.wait_ge(sem("xt_pe"), KD * (k + 1))
                for t in range(TT):
                    link(pool.tensor_tensor(res[:, t, :], res[:, t, :], lnp[:, 0, :], ALU.mult))
                    pool.tensor_tensor(res[:, t, :], res[:, t, :], lnp[:, 1, :], ALU.add).then_inc(sem("res_ok"), 1)
                pool.wait_ge(sem("res_ok"), TT * (k + 1))

            for k in range(4):
                ln_params(k)
                scale_res(k)
            for l in range(2):
                k = 4 + 2 * l
                pool.wait_ge(sem("xt_lo"), KD * k)
                load(sgp[:, 0, :], w["sgu_ln_g_2"][l].partition_broadcast(P), "sgu_in")
                load(sgp[:, 1, :], w["sgu_ln_b_2"][l].partition_broadcast(P), "sgu_in")
                load(wsn[:], w["sgu_w_2"][l].rearrange("g t s -> t g s"), "sgu_in")
                load(bsn[:], w["sgu_b_2"][l], "sgu_in")
                for t in range(TT):
                    pool.wait_ge(b_free[t], GROUPS_1 + GROUPS_2 * l + 1)
                pool.wait_ge(sem("trig_ok"), 1)
                link(rope_heads(pool, link, kvq[:, :, 0:128], 2, rot_q))
                for r in range(2):
                    link(pool.tensor_copy(kdd[:].rearrange("p t (g r d) -> p t g r d", g=2, r=2)[:, :, :, r],
                                          kvq[:, :, 0:128].rearrange("p t (g d) -> p t g d", g=2)))
                g0 = LAYER_CHUNK[l] + 5

                def low_part(g):
                    s, n = g % 2, chunk_cols[g]
                    pool.wait_ge(lo_ready, g)
                    pool.wait_ge(hi_ready, g + 1)
                    pool.tensor_tensor(wlo[:, s, 0:n], raw[:, s, 0:n], f32(whi[:, s, 0:n]), ALU.subtract)\
                        .then_inc(lo_ready, 1)

                low_part(g0 + 1)
                pool.wait_ge(sem("sgu_in"), 64 * (l + 1))
                for t in range(TT):
                    pool.wait_ge(sem("vs_z"), 4 * l + t + 1)
                    link(pool.tensor_tensor(vs[:, t, :], vs[:, t, :], sgp[:, 0, :], ALU.mult))
                    pool.tensor_tensor(vs[:, t, :], vs[:, t, :], sgp[:, 1, :], ALU.add).then_inc(sem("vs_ok"), 1)
                pool.wait_ge(sem("vs_ok"), 4 * (l + 1))
                low_part(g0 + 2)
                pool.wait_ge(sem("ws_rd"), l + 1)
                pool.tensor_tensor(wsT[:], wsT[:], ustep[:].unsqueeze(1).broadcast_to([P, SGG, P]), ALU.mult)\
                    .then_inc(sem("ws_ok"), 1)
                low_part(g0 + 3)
                low_part(g0 + 4)
                for t in range(TT):
                    pool.wait_ge(b_free[t], GROUPS_1 + GROUPS_2 * l + 5)
                rope_heads(pool, link, qtok[:], NH, rot_q).then_inc(sem("q_rot"), 1)
                low_part(g0 + 5)
                ln_params(k)
                pool.wait_ge(sem(f"dsa{l}_o_lo"), 4)
                load(pin[:], w["p_2"][l, 0].rearrange("(t p) c -> p t c", p=P), "p_in")
                low_part(LAYER_CHUNK[l] + 14)
                scale_res(k)
                ln_params(k + 1)
                if l == 0:
                    scale_res(k + 1)

        @block.tensor
        def _(pe):
            st = {"g": 0, "a": 0, "b": 0, "u": 0}

            def mm3(o, lh, ll, rh, rl, start, stop):
                pe.matmul(o, lh, rh, start=start, stop=False)
                pe.matmul(o, lh, rl, start=False, stop=False)
                return pe.matmul(o, ll, rh, start=False, stop=stop)

            def channel_major(n, k_tiles, ah, al, first, ready=None):
                g0, a0 = st["g"], st["a"]

                def body(j, i):
                    s, pair = (g0 + j) % 2, (a0 + j) % 2
                    pe.wait_ge(lo_ready, val(g0 + j + 1, i, 2))
                    if a0 + j >= 2:
                        pe.wait_ge(dve_f, val(a0 + j - 1, i, 2))
                    order = [(o, k) for o in range(2) for k in range(k_tiles)]
                    turned = ready is not None and j == 0 and i is None
                    if turned:
                        order.sort(key=lambda ok: ok[1])
                    for o, k in order:
                        if turned and o == 0:
                            pe.wait_ge(sem("xt_lo"), ready + k + 1)
                        c = (o * k_tiles + k) * P
                        ins = mm3(ps[:, 2 * pair + o, :], whi[:, s, c:c + P], wlo[:, s, c:c + P],
                                  ah[:, k, :], al[:, k, :], k == 0, k == k_tiles - 1)
                    ins.then_inc(chunk_used, 1)

                pairs(pe, n, first, 0, body)
                st["g"] += n
                st["a"] += n

            def token_major(k_tiles, width, ah, al, ready=None, between=None, hidden=None, bank0=4,
                            tiles=None):
                k = 0
                while k < k_tiles:
                    s = st["g"] % 2
                    m = min(4 if width > 256 else 8, k_tiles - k)
                    if between and k + m == k_tiles:
                        between()
                    pe.wait_ge(lo_ready, st["g"] + 1)
                    if hidden:
                        pe.wait_ge(dve_l, hidden[0] + (k + m) // hidden[1])
                    def product(t, q):
                        return mm3(ps[:, bank0 + t, 0:width], ah[:, k + q, t * P:(t + 1) * P],
                                   al[:, k + q, t * P:(t + 1) * P],
                                   whi[:, s, q * width:(q + 1) * width], wlo[:, s, q * width:(q + 1) * width],
                                   k + q == 0, k + q == k_tiles - 1)

                    if ready is not None and k == 0:
                        pe.wait_ge(sem("xt_f"), ready + bank0 + TT)
                        for q in range(m):
                            pe.wait_ge(sem("xt_lo"), ready + q + 1)
                            for t in range(TT):
                                ins = product(t, q)
                        ins.then_inc(chunk_used, 1)
                        st["g"] += 1
                        k += m
                        continue
                    if ready is not None:
                        pe.wait_ge(sem("xt_lo"), ready + KD)
                    for t in range(TT):
                        if k == 0 and st["b"] > 0:
                            pe.wait_ge(b_free[t], st["b"])
                        if tiles is not None and k == 0:
                            pe.wait_ge(sem("xt_f"), tiles + bank0 + t + 1)
                        for q in range(m):
                            ins = product(t, q)
                        if k + m == k_tiles and t < TT - 1:
                            ins.then_inc(b_done, 1)
                    ins.then_inc(chunk_used, 1)
                    st["g"] += 1
                    k += m
                st["b"] += 1

            def to_channels(k):
                for t in range(TT):
                    pe.wait_ge(sem("ln_z"), TT * k + t + 1)
                    for c in range(KD // 2 if t < TT - 1 else KD):
                        for u in ([t] if c < KD // 2 else range(TT)):
                            ins = pe.transpose(ps[:, c, u * P:(u + 1) * P], res[:, u, c * P:(c + 1) * P], ident[:, 0:P])
                        if t == TT - 1:
                            ins.then_inc(sem("xt_pe"), 1)

            def turn(name, parts, banks=(0, 1, 2, 3), base=0):
                for n, piece in enumerate(parts):
                    if n >= len(banks):
                        pe.wait_ge(sem(name + "_rd"), base + n - len(banks) + 1)
                    for t in range(TT):
                        ins = pe.transpose(ps[:, banks[n % len(banks)], t * P:(t + 1) * P], piece(t), ident[:, 0:P])
                    ins.then_inc(sem(name + "_pe"), 1)

            pe.wait_ge(sem("lam_in"), 48)
            pe.wait_ge(sem("ident_ok"), 3)
            pe.wait_ge(sem("ldt_wide"), 1)
            for i in range(3):
                ins = pe.transpose(ps[:, 0, i * Q:(i + 1) * Q], lam[:, i, :], ident[0:Q, 0:Q])
            ins.then_inc(sem("lam_pe"), 1)
            pe.wait_ge(sem("c_in"), 64)
            for i in range(2):
                for n in range(8):
                    ins = pe.transpose(ps[:, 1 + 2 * i + n // 4, (n % 4) * P:(n % 4 + 1) * P],
                                       cn[:, i, n].rearrange("r d p -> r (d p)"), ident[:, 0:P])
            ins.then_inc(sem("c_pe"), 1)
            for n in range(8):
                if n >= 3:
                    pe.wait_ge(sem("u_rd"), n - 2)
                pe.wait_ge(sem("xg_ok"), n + 1)
                for gg in range(8):
                    ins = pe.transpose(ps[:, 5 + n % 3, gg * NC:(gg + 1) * NC], xg[:, 8 * n + gg, :],
                                       ident[0:NC, 0:NC])
                ins.then_inc(sem("u_pe"), 1)
            pe.wait_ge(sem("u_rd"), 8)
            pe.wait_ge(sem("c_rd"), 4)
            pe.wait_ge(sem("ab_ok"), 1)
            pe.wait_ge(sem("ab_pool"), len(AB_POOL))
            pe.wait_ge(sem("ab_act"), 2)
            for m in range(16):
                if m >= 4:
                    pe.wait_ge(sem(f"mt_rd{m % 2}"), (m - 4) // 2 + 1)
                for qq in range(4):
                    ins = pe.transpose(ps[:, MB[m % 4], qq * P:(qq + 1) * P],
                                       ab[:, m // 8, 4 * (m % 8) + qq].rearrange("p j c -> p (j c)"), ident[:, 0:P])
                ins.then_inc(sem("mt_pe"), 1)
            for m in range(8):
                if m == 0:
                    pe.wait_ge(sem("mt_rd0"), 4)
                    pe.wait_ge(sem("mt_rd1"), 4)
                if m == 4:
                    pe.wait_ge(sem("mt_rd0"), 8)
                    pe.wait_ge(sem("mt_rd1"), 8)
                if m >= 2:
                    pe.wait_ge(sem(f"s_rd{m % 2}"), (m - 2) // 2 + 1)
                for qq in range(8):
                    q = 8 * (m % 4) + qq
                    for a in range(2):
                        ins = pe.matmul(ps[a * NS:(a + 1) * NS, 5 + m % 2, qq * NC:(qq + 1) * NC],
                                        mt[m // 4][:, q, a * NS:(a + 1) * NS], uu[:, 2 * q + a, :], start=True, stop=True)
                ins.then_inc(sem("s_pe"), 1)
            for a in range(2):
                for q in range(Q):
                    for r in range(2):
                        ins = pe.matmul(ps[:, 1 + a, q * GC:(q + 1) * GC], ab[a * NS:(a + 1) * NS, r, q],
                                        cc[a * NS:(a + 1) * NS, r, q, :], start=r == 0, stop=r == 1)
                ins.then_inc(sem("kk_pe"), 1)
            for n in range(2 * L):
                a, i = n // L, n % L
                if i == 0:
                    pe.wait_ge(sem("kk_ok"), a + 1)
                if n >= 2:
                    pe.wait_ge(sem("tm_rd"), n - 1)
                pe.matmul(ps[:, 3 + n % 2, :], ident[:, (L - 1 - i) * GC:(L - 1 - i) * GC + P],
                          kk[:, a].rearrange("p q c -> p (q c)"), start=True, stop=True).then_inc(sem("tm_pe"), 1)
            pe.wait_ge(sem("ca_ok"), 1)
            pe.wait_ge(sem("scan2"), 6 * (SB_J - 1))
            pe.wait_ge(sem("tm_rd"), 16)
            for m in range(16):
                if m >= 2:
                    pe.wait_ge(sem("y_rd"), m - 1)
                for a in range(2):
                    for qq in range(2):
                        q = 2 * m + qq
                        o = ps[0:NC, 2 * (m % 2) + a, qq * P:(qq + 1) * P]
                        for r in range(2):
                            pe.matmul(o, hst[a * NS:(a + 1) * NS, r, q, :], ca[a * NS:(a + 1) * NS, q, r],
                                      start=r == 0, stop=False)
                        ins = pe.matmul(o, uu[:, 2 * q + a, :], tm[:, :, a, q, :], start=False, stop=True)
                ins.then_inc(sem("y_mm"), 1)
            pe.wait_ge(sem("y_rd"), 16)
            for c in range(KD):
                if c >= 4:
                    pe.wait_ge(sem("yt_lo"), c - 3)
                for j in range(L):
                    ins = pe.transpose(ps[:, c % 4, j * NC:(j + 1) * NC], yg[:, j, c * P:(c + 1) * P], ident[0:NC, 0:NC])
                ins.then_inc(sem("yt_pe"), 1)
            pe.wait_ge(sem("yt_lo"), KD)

            def relu_mlp(k):
                for half in range(2):
                    a0 = st["a"]
                    channel_major(8, KD, xh, xl, 2 if half == 0 else 0, KD * (k - 1) if half == 0 else None)
                    for n in range(2):
                        token_major(16, 512, hidh, hidl, hidden=(a0, 2))

            channel_major(KD, KD, xh, xl, 2)
            for n in range(2):
                token_major(KD, 512, hidh, hidl, hidden=(0, 1))
            to_channels(0)
            relu_mlp(1)
            to_channels(1)

            token_major(KD, KVL + ROPE, xh, xl, KD, bank0=0)

            def turn_kv():
                pe.wait_ge(sem("kv_ok"), 1)
                turn("kvl", [lambda t, c=c: ckv[:, t, c * P:(c + 1) * P] for c in range(2)] + [lambda t: krd[:, t, :]])

            token_major(KD, QL, xh, xl, between=turn_kv)
            pe.wait_ge(sem("kvl_rd"), 3)

            def keys(c):
                s = st["g"] % 2
                for h in range(4):
                    for k in range(2):
                        o = k * 1024 + h * 256
                        ins = mm3(ps[:, h, :], whi[:, s, o:o + P], wlo[:, s, o:o + P], ckvh[:, k, :], ckvl[:, k, :],
                                  k == 0, k == 1)
                return ins

            def values(c):
                s = st["g"] % 2
                for t in range(TT):
                    for k in range(2):
                        def part(x):
                            v = x[:, s, k * 1024:(k + 1) * 1024].rearrange("p (h n) -> p h n", h=4)
                            return v[:, :, NOPE:NOPE + VH]
                        ins = mm3(ps[:, 4 + t, :], ckvh[:, k, t * P:(t + 1) * P], ckvl[:, k, t * P:(t + 1) * P],
                                  part(whi), part(wlo), k == 0, k == 1)
                return ins

            pe.wait_ge(lo_ready, st["g"] + 1)
            keys(0).then_inc(sem("kn_pe"), 1)
            for t in range(TT):
                pe.wait_ge(b_free[t], st["b"])
            values(0).then_inc(chunk_used, 1)
            st["g"] += 1
            pe.wait_ge(sem("kn_rd"), 1)
            pe.wait_ge(sem("q_ok"), 1)
            turn("ql", [lambda t, c=c: cq[:, t, c * P:(c + 1) * P] for c in range(3)])
            pe.wait_ge(lo_ready, st["g"] + 1)
            pe.wait_ge(sem("v_rd"), 1)
            values(1).then_inc(sem("v_pe"), 1)
            pe.wait_ge(sem("ql_rd"), 3)
            keys(1).then_inc(chunk_used, 1)
            st["g"] += 1

            def turn_q_rope(c):
                pe.wait_ge(sem("qrope_ok"), c + 1)
                if c >= 2:
                    pe.wait_ge(sem("qrt_rd"), c - 1)
                for t in range(TT):
                    ins = pe.transpose(ps[:, 6 + c % 2, t * P:(t + 1) * P], qrt[:, t, c * P:(c + 1) * P], ident[:, 0:P])
                ins.then_inc(sem("qrt_pe"), 1)

            for c in range(4):
                s = st["g"] % 2
                pe.wait_ge(lo_ready, st["g"] + 1)
                if c == 0:
                    pe.wait_ge(sem("kn_rd"), 2)
                    pe.wait_ge(sem("v_rd"), 2)
                if c >= 2:
                    pe.wait_ge(sem("qn_rd"), c - 1)
                    pe.wait_ge(sem("qr_rd"), c - 1)
                for t in range(TT):
                    for k in range(3):
                        def part(x):
                            v = x[:, s, k * 384:(k + 1) * 384].rearrange("p (h n) -> p h n", h=2)
                            return v[:, :, NOPE:NOPE + ROPE]
                        ins = mm3(ps[:, 4 + c % 2, t * P:(t + 1) * P], cqh[:, k, t * P:(t + 1) * P],
                                  cql[:, k, t * P:(t + 1) * P], part(whi), part(wlo), k == 0, k == 2)
                ins.then_inc(sem("qr_pe"), 1)
                for h in range(2):
                    for k in range(3):
                        o = k * 384 + h * 192
                        ins = mm3(ps[:, 2 * (c % 2) + h, :], whi[:, s, o:o + P], wlo[:, s, o:o + P], cqh[:, k, :],
                                  cql[:, k, :], k == 0, k == 2)
                ins.then_inc(chunk_used, 1)
                st["g"] += 1
                if c >= 1:
                    turn_q_rope(c - 1)
            turn_q_rope(3)
            pe.wait_ge(sem("qn_rd"), 4)
            pe.wait_ge(sem("qrt_rd"), 4)

            def attention(name, score, value, pt, per, read=None):
                units = [(h, t) for h in range(NH) for t in range(TT)]

                def scores(u):
                    if u >= 4:
                        pe.wait_ge(sem(name + "_e"), u - 3)
                    score(*units[u], ps[:, SB[u % 4], 0:(units[u][1] + 1) * P]).then_inc(sem(name + "_s"), 1)

                for u in range(3):
                    scores(u)
                if read:
                    pe.wait_ge(*read)
                for u, (h, t) in enumerate(units):
                    if u + 3 < len(units):
                        scores(u + 3)
                    pe.wait_ge(sem(name + "_pn"), u + 1)
                    if u >= 2:
                        pe.wait_ge(sem(name + "_pt"), u - 1)
                    for b in range(t + 1):
                        ins = pe.transpose(ps[:, 2 + u % 2, b * P:(b + 1) * P], pt[2][:, u % 3, b * P:(b + 1) * P],
                                           ident[:, 0:P])
                    ins.then_inc(sem(name + "_tp"), 1)
                    for hh in ([h - 1] if t == 1 and h > 0 else []) + ([h] if u == len(units) - 1 else []):
                        pe.wait_ge(sem(name + "_pt"), (hh + 1) * TT)
                        n = hh // per
                        if hh % per == 0 and n >= 2:
                            pe.wait_ge(sem(name + "_o_lo"), n - 1)
                        r0 = (hh % per) * (P // per)
                        for b in range(TT):
                            ins = pe.matmul(ps[r0:r0 + P // per, 4 + n % 2, b * P:S], value(hh, b),
                                            pt[hh % 2][:, b, b * P:S], start=b == 0, stop=b == TT - 1)
                        ins.then_inc(sem(name + "_o"), 1)

            def mla_score(h, t, o):
                n = (t + 1) * P
                r = (h % 2) * ROPE
                pe.matmul(o, qn[:, h, t * P:(t + 1) * P], kn[:, h, 0:n], start=True, stop=False)
                pe.matmul(o, qrT[r:r + ROPE, h // 2, t * P:(t + 1) * P], krT[r:r + ROPE, 0:n], start=False, stop=False)
                return pe.matmul(o[:, t * P:n], identb[:], causal[:], start=False, stop=True)

            attention("mla", mla_score, lambda h, b: vv[:, b, h * VH:(h + 1) * VH], pt1 + [pn1], 1)
            pe.wait_ge(sem("mla_o_lo"), NH)
            for n in range(2):
                token_major(KD, 512, xh, xl)
            to_channels(2)
            relu_mlp(3)
            to_channels(3)

            for l in range(2):
                kx = 4 + 2 * l
                nm = f"dsa{l}"
                assert (st["b"], st["g"]) == (GROUPS_1 + GROUPS_2 * l, LAYER_CHUNK[l])

                def index_logits():
                    pe.wait_ge(sem("i_rot"), l + 1)
                    turn("in", [lambda t, c=c: kvq[:, t, 256 + c * P:256 + (c + 1) * P] for c in range(2)]
                         + [lambda t: kid[:, t, :]], base=3 * l)
                    pe.wait_ge(sem("in_rd"), 3 * (l + 1))
                    for t in range(1, TT):
                        n = (t + 1) * P
                        for h in range(NI):
                            if t >= 2:
                                pe.wait_ge(sem("lg_rd"), 4 * (3 * l + t - 2) + h + 1)
                            r = (h % 2) * IXD
                            pe.matmul(ps[:, h, 0:n], qiT[r:r + IXD, h // 2, t * P:(t + 1) * P], kiT[r:r + IXD, 0:n],
                                      start=True, stop=True).then_inc(sem("lg_pe"), 1)

                def turn_sgu():
                    pe.wait_ge(sem("sgu_in"), 64 * (l + 1))
                    pe.wait_ge(sem("lg_rd"), 12 * (l + 1))
                    for g in range(SGG):
                        ins = pe.transpose(ps[:, g // 4, (g % 4) * P:(g % 4 + 1) * P], wsn[:, g, :], ident[:, 0:P])
                    ins.then_inc(sem("ws_pe"), 1)
                    pe.transpose(ps[:, 2, 0:SGG], bsn[:], ident[0:SGG, 0:SGG]).then_inc(sem("ws_pe"), 1)

                def spatial_gate():
                    pe.wait_ge(sem("ws_ok"), l + 1)
                    pe.wait_ge(sem("bs_rd"), l + 1)
                    pe.wait_ge(sem("vs_ok"), 4 * (l + 1))
                    for g in range(SGG):
                        ins = pe.matmul(ps[:, g // 2, (g % 2) * 256:(g % 2 + 1) * 256], wsT[:, g, :],
                                        vs[:, :, g * 64:(g + 1) * 64], start=True, stop=True)
                    ins.then_inc(sem("sg_pe"), 1)

                token_major(KD, 512, xh, xl, KD * (kx - 1), bank0=0)
                token_major(KD, 68, xh, xl)
                token_major(KD, 512, xh, xl, between=index_logits)
                token_major(KD, 512, xh, xl, between=turn_sgu)
                token_major(KD, 512, xh, xl, between=spatial_gate)
                pe.wait_ge(sem("bo_ok"), l + 1)
                for t in range(TT):
                    pe.wait_ge(b_free[t], st["b"])
                turn("bo", [lambda t, c=c: gu[:, t, c * P:(c + 1) * P] for c in range(4)], GATE_BANKS, 4 * l)
                pe.wait_ge(sem("q_rot"), l + 1)
                turn("qk", [lambda t, c=c: kdd[:, t, c * P:(c + 1) * P] for c in range(2)]
                     + [lambda t, c=c: qtok[:, t, c * P:(c + 1) * P] for c in range(4)], SB, 6 * l)
                pe.wait_ge(sem("qk_rd"), 6 * (l + 1))

                def dsa_score(h, t, o):
                    r = (h % 2) * HD
                    if h == 0:
                        pe.wait_ge(sem("mask_ok"), TT * l + t + 1)
                    pe.matmul(o, qT[r:r + HD, h // 2, t * P:(t + 1) * P], kT[r:r + HD, h // 4, 0:(t + 1) * P],
                              start=True, stop=False)
                    return pe.matmul(o, identb[:], mask[:, t, 0:(t + 1) * P], start=False, stop=True)

                attention(nm, dsa_score, lambda h, b: kvq[:, b, 128 + (h // 4) * HD:128 + (h // 4 + 1) * HD],
                          pt2 + [pn2], 2, (sem("bo_rd"), 4 * (l + 1)))
                pe.wait_ge(sem(nm + "_o_lo"), 4)
                def turn_p():
                    pe.wait_ge(sem("p_in"), 16 * (l + 1))
                    turn("pt", [lambda t, c=c: pin[:, t, c * P:(c + 1) * P] for c in range(2)], base=2 * l)

                token_major(KD, 512, xh, xl)
                token_major(KD, 512, xh, xl, between=turn_p)
                pe.wait_ge(sem("pt_rd"), 2 * (l + 1))
                to_channels(kx)
                for n in range(2):
                    token_major(2, 512, pTh, pTl, bank0=0, tiles=KD * kx if n == 0 else None)
                    token_major(KD, 512, xh, xl, KD * kx if n == 0 else None)
                for half in range(2):
                    a0 = st["a"]
                    channel_major(11, KD, xh, xl, 0)
                    for n in range(2):
                        token_major(11, 512, hidh, hidl, hidden=(a0, 1))
                if l == 0:
                    to_channels(kx + 1)

        @block.scalar
        def _(act):
            st = {"g": 0, "a": 0, "b": 0, "s": 0}
            seq = sem("act_seq")

            def link(ins):
                st["s"] += 1
                ins.then_inc(seq, 1)
                act.wait_ge(seq, st["s"])

            def split(g, i=None):
                if g >= n_chunks:
                    return
                s, n = g % 2, chunk_cols[g]
                act.wait_ge(landed[s], val(32 * (g // 2 + 1), i, 32))
                if g >= 2:
                    act.wait_ge(chunk_used, val(g - 1, i, 2))
                act.activation(whi[:, s, 0:n], raw[:, s, 0:n], ACT.Copy).then_inc(hi_ready, 1)

            def channel_major(n, kind, first):
                g0, a0 = st["g"], st["a"]
                tail = 0 if all(c == chunk_cols[g0] for c in chunk_cols[g0:g0 + n + 2]) else 2

                def body(j, i):
                    pair = (a0 + j) % 2
                    a = a0 + j
                    act.wait_ge(chunk_used, val(g0 + j + 1, i, 2))
                    if a >= 1:
                        act.wait_ge(dve_f, val(a, i, 2))
                    if kind == "relu2":
                        act.activation(rt[:], ps[:, 2 * pair:2 * pair + 2, :].rearrange("p b n -> p (b n)"),
                                       ACT.Relu).then_inc(act_r, 1)
                    elif kind == "glu":
                        act.activation(rt[:, 0:S], ps[:, 2 * pair + 1, :], ACT.Sigmoid).then_inc(act_r, 1)
                    else:
                        act.activation(rt[:, 0:S], ps[:, 2 * pair, :], ACT.Silu).then_inc(act_r, 1)
                    split(g0 + j + 2, i)
                    act.wait_ge(dve_f, val(a + 1, i, 2))
                    idx = j if i is None else i * 2 + j
                    if kind == "relu2":
                        o = hidh[:, 2 * j:2 * j + 2, :] if i is None else hidh[:, bass.ds(i * 4 + 2 * j, 2), :]
                        act.activation(o, ft[:].rearrange("p (b n) -> p b n", b=2), ACT.Copy).then_inc(act_h, 1)
                    else:
                        o = hidh[:, j:j + 1, :] if i is None else hidh[:, bass.ds(i * 2 + j, 1), :]
                        act.activation(o, ft[:, 0:S].rearrange("p (b n) -> p b n", b=1), ACT.Copy).then_inc(act_h, 1)

                pairs(act, n, first, tail, body)
                st["g"] += n
                st["a"] += n

            def token_major(k_tiles, width, evac=None, hold=False, between=None, bank0=4):
                k = 0
                while k < k_tiles:
                    m = min(4 if width > 256 else 8, k_tiles - k)
                    if between and k + m == k_tiles:
                        between()
                    k += m
                    st["g"] += 1
                    if k == k_tiles:
                        if evac:
                            for t in range(TT):
                                if t < TT - 1:
                                    act.wait_ge(b_done, 3 * st["b"] + t + 1)
                                else:
                                    act.wait_ge(chunk_used, st["g"])
                                evac(t, ps[:, bank0 + t, 0:width])
                        st["b"] += 1
                    if not (hold and k == k_tiles):
                        split(st["g"] + 1)

            def row_norms(x, n0, var_sem, sd_sem, rs_sem, z_sem):
                for t in range(TT + 1):
                    if t < TT:
                        act.wait_ge(var_sem, n0 + t + 1)
                        act.activation(sd[:, t:t + 1], mv[:, t, 1:2], ACT.Sqrt, bias=consts[:, 0:1]).then_inc(sd_sem, 1)
                    if t > 0:
                        act.wait_ge(rs_sem, n0 + t)
                        act.activation(x[:, t - 1, :], x[:, t - 1, :], ACT.Identity, scale=rstd[:, t - 1:t],
                                       bias=nmr[:, t - 1:t]).then_inc(z_sem, 1)

            def norm(k, last=False, amid=False):
                row_norms(res, TT * k, sem("ln_var"), sem("ln_sd"), sem("ln_rs"), sem("ln_z"))
                for c in range(KD if not last else 0):
                    act.wait_ge(sem("xt_f"), KD * k + c + 1)
                    act.activation(xh[:, c, :], xf(c), ACT.Copy).then_inc(sem("xt_hi"), 1)
                    if amid and c == 2:
                        split(st["g"] + 1)
                if not amid:
                    split(st["g"] + 1)

            def trig(sn, cs, r, absr):
                act.activation(sn, r, ACT.Sin)
                link(act.activation(absr, r, ACT.Abs))
                return act.activation(cs, absr, ACT.Sin, scale=-1.0, bias=consts[:, 2:3])

            act.wait_ge(sem("pool_const"), 1)
            act.wait_ge(sem("lam_rd"), 1)
            act.activation(sc[:, 3, :], sc[:, 2, :], ACT.Exp).then_inc(sem("dt_ok"), 1)
            act.wait_ge(sem("ang_ok"), 1)
            act.activation(sc[:, 10, :], sc[:, 4, :], ACT.Exp).then_inc(sem("mag_ok"), 1)
            trig(sc[:, 8, :], sc[:, 9, :], sc[:, 6, :], sc[:, 7, :]).then_inc(sem("mag_ok"), 1)
            act.wait_ge(sem("x_in"), 16)
            for n in range(8):
                act.activation(xg[:, 8 * n:8 * n + 8, :].rearrange("p g (j c) -> p g j c", j=L),
                               xc[:, :, n * P:(n + 1) * P].rearrange("p j (g c) -> p g j c", g=8),
                               ACT.Copy).then_inc(sem("xg_ok"), 1)
            for n in range(8):
                act.wait_ge(sem("u_pe"), n + 1)
                act.activation(uu[:, 8 * n:8 * n + 8, :], ps[:, 5 + n % 3, :].rearrange("p (g c) -> p g c", g=8),
                               ACT.Copy).then_inc(sem("u_rd"), 1)
            act.wait_ge(sem("c_pe"), 1)
            for r in range(2):
                for a in range(2):
                    v = ps[a * NS:(a + 1) * NS, 1 + 2 * r:3 + 2 * r, :].rearrange("p b (q a c) -> p (b q) a c", a=2, c=GC)
                    act.activation(cc[a * NS:(a + 1) * NS, r], v[:, :, a, :], ACT.Copy, scale=1.0 - 2.0 * r)\
                       .then_inc(sem("c_rd"), 1)
            act.wait_ge(sem("bb_ok"), 1)
            for r in range(2):
                act.activation(ab[:, r, :, L - 1, :], bb[:, r], ACT.Copy).then_inc(sem("ab_act"), 1)

            def mt_copy(m):
                act.wait_ge(sem("mt_pe"), m + 1)
                n = m % 8
                act.activation(mt[m // 8][:, 4 * n:4 * n + 4, :], ps[:, MB[m % 4], :].rearrange("p (q c) -> p q c", q=4),
                               ACT.Copy).then_inc(sem("mt_rd0"), 1)

            for m in range(0, 16, 2):
                mt_copy(m)
            for m in range(0, 8, 2):
                act.wait_ge(sem("s_pe"), m + 1)
                n = m % 4
                act.activation(sst[:, m // 4, 8 * n:8 * n + 8, :], ps[:, 5 + m % 2, :].rearrange("p (q c) -> p q c", q=8),
                               ACT.Copy).then_inc(sem("s_rd0"), 1)
            for a in range(2):
                act.wait_ge(sem("kk_pe"), a + 1)
                act.activation(kk[:, a], ps[:, 1 + a, :].rearrange("p (q c) -> p q c", c=GC), ACT.Copy)\
                   .then_inc(sem("kk_rd"), 1)
            for n in range(16):
                act.wait_ge(sem("tm_pe"), n + 1)
                act.activation(tm[:, n % L, n // L], ps[:, 3 + n % 2, :].rearrange("p (q c) -> p q c", q=Q),
                               ACT.Copy).then_inc(sem("tm_rd"), 1)
            act.wait_ge(sem("ang_ok"), 2)
            trig(sin1[:].rearrange("p t k -> p (t k)"), cos1[:].rearrange("p t k -> p (t k)"),
                 ang[:, 0, 0:128], ang[:, 1, 0:128])
            trig(sin2[:].rearrange("p t k -> p (t k)"), cos2[:].rearrange("p t k -> p (t k)"),
                 ang[:, 0, 128:160], ang[:, 1, 128:160]).then_inc(sem("trig_ok"), 1)
            for m in range(16):
                act.wait_ge(sem("y_mm"), m + 1)
                for a in range(2):
                    q0 = 2 * m
                    o = yg[:, :, q0 * 32:q0 * 32 + 64].rearrange("p j (q a c) -> p q a j c", q=2, a=2)[:, :, a]
                    v = ps[0:NC, 2 * (m % 2) + a, 0:256].rearrange("p (q j c) -> p q j c", q=2, j=L)
                    ins = act.activation(o, v, ACT.Gelu_apprx_tanh)
                ins.then_inc(sem("y_rd"), 1)
            for c in range(KD):
                act.wait_ge(sem("yt_pe"), c + 1)
                act.activation(xh[:, c, :].rearrange("p (n j) -> p n j", j=L),
                               ps[:, c % 4, :].rearrange("p (j n) -> p n j", j=L), ACT.Copy).then_inc(sem("yt_hi"), 1)
                if c == 5:
                    split(0)
            split(1)

            def relu_mlp(last_k):
                for half in range(2):
                    channel_major(8, "relu2", 0)
                    for n in range(2):
                        token_major(16, 512, hold=half == 1 and n == 1)
                norm(last_k)

            channel_major(KD, "glu", 2)
            token_major(KD, 512)
            token_major(KD, 512, hold=True)
            norm(0)
            relu_mlp(1)

            def keep(dst):
                def evac(t, src):
                    act.activation(dst(t), src, ACT.Copy).then_inc(b_free[t], 1)
                return evac

            def squares(dst, n, col):
                def evac(t, src):
                    act.activation(junk[:, col, t, 0:n], src[:, 0:n], ACT.Square, accum_out=mv[:, t, col:col + 1])
                    act.activation(dst[:, t, :], src, ACT.Copy).then_inc(b_free[t], 1)
                return evac

            def root(n, col):
                for t in range(TT):
                    act.wait_ge(b_free[t], st["b"])
                return act.activation(bst[:, :, col, 0:1], mv[:, :, col:col + 1], ACT.Sqrt, scale=1.0 / n,
                                      bias=consts[:, 1:2])

            def latent_high(name, high, gain):
                for c in range(high.shape[1]):
                    act.wait_ge(sem(name + "_pe"), c + 1)
                    act.activation(high[:, c, :], ps[:, c, :], ACT.Identity, scale=gain[:, c:c + 1])\
                       .then_inc(sem(name + "_hi"), 1)

            token_major(KD, KVL + ROPE, squares(ckv, KVL, 0), bank0=0)
            root(KVL, 0).then_inc(sem("kv_sd"), 1)
            token_major(KD, QL, squares(cq, QL, 1), between=lambda: latent_high("kvl", ckvh, kvg))
            root(QL, 1).then_inc(sem("q_sd"), 1)
            for c in range(2):
                st["g"] += 1
                if c == 0:
                    act.wait_ge(sem("kn_pe"), 1)
                else:
                    act.wait_ge(chunk_used, st["g"])
                act.activation(kn[:, 4 * c:4 * c + 4, :], ps[:, 0:4, :], ACT.Copy).then_inc(sem("kn_rd"), 1)
                if c == 0:
                    latent_high("ql", cqh, qg)
                split(st["g"] + 1)
            for c in range(5):
                if c < 4:
                    act.wait_ge(sem("qr_pe"), c + 1)
                    act.activation(qrt[:, :, c * P:(c + 1) * P], ps[:, 4 + c % 2, :].rearrange("p (t n) -> p t n", t=TT),
                                   ACT.Copy).then_inc(sem("qr_rd"), 1)
                    st["g"] += 1
                    split(st["g"] + 1)
                if c >= 1:
                    act.wait_ge(sem("qrt_pe"), c)
                    act.activation(qrT[:, c - 1, :], ps[:, 6 + (c - 1) % 2, :], ACT.Copy, scale=SM_SCALE)\
                       .then_inc(sem("qrt_rd"), 1)

            def attention(name, pt, per, dst):
                def exps(u):
                    n = (u % TT + 1) * P
                    act.wait_ge(sem(name + "_mx"), u + 1)
                    if u >= 3:
                        act.wait_ge(sem(name + "_tp"), u - 2)
                    act.activation(pt[2][:, u % 3, 0:n], ps[:, SB[u % 4], 0:n], ACT.Exp,
                                   bias=nmax[:, u % 4:u % 4 + 1],
                                   accum_out=rsum[:, u % 4:u % 4 + 1]).then_inc(sem(name + "_e"), 1)

                def high(n0):
                    act.wait_ge(sem(name + "_o"), (n0 + 1) * per)
                    act.activation(xh[:, dst + n0, :], ps[:, 4 + n0 % 2, :], ACT.Copy).then_inc(sem(name + "_o_hi"), 1)

                exps(0)
                exps(1)
                for u in range(NH * TT):
                    h, t = u // TT, u % TT
                    if u + 2 < NH * TT:
                        exps(u + 2)
                    act.wait_ge(sem(name + "_tp"), u + 1)
                    if t == 0 and h >= 2:
                        act.wait_ge(sem(name + "_o"), h - 1)
                    act.activation(pt[h % 2][:, 0:t + 1, t * P:(t + 1) * P],
                                   ps[:, 2 + u % 2, 0:(t + 1) * P].rearrange("p (b n) -> p b n", n=P),
                                   ACT.Copy).then_inc(sem(name + "_pt"), 1)
                    if t == 2 and h >= per and h % per == 0:
                        high(h // per - 1)
                high(NH // per - 1)

            attention("mla", pt1 + [pn1], 1, 0)
            token_major(KD, 512)
            token_major(KD, 512, hold=True)
            norm(2)
            relu_mlp(3)

            for l in range(2):
                kx = 4 + 2 * l
                token_major(KD, 512, keep(lambda t: kvq[:, t, :]), bank0=0)
                token_major(KD, 68, keep(lambda t: kiw[:, t, :]))

                def gelu(dst):
                    def evac(t, src):
                        act.activation(dst[:, t, :], src, ACT.Gelu_apprx_tanh).then_inc(b_free[t], 1)
                    return evac

                def index_turned():
                    for n, dst in enumerate([qiT[:, c, :] for c in range(2)] + [kiT[:]]):
                        act.wait_ge(sem("in_pe"), 3 * l + n + 1)
                        act.activation(dst, ps[:, n % 4, :], ACT.Copy).then_inc(sem("in_rd"), 1)
                    for t in range(1, TT):
                        for h in range(NI):
                            m = 4 * (3 * l + t - 1) + h
                            act.wait_ge(sem("lg_pe"), m + 1)
                            if t >= 3:
                                act.wait_ge(sem("sc_ok"), 4 * (3 * l + t - 3) + h + 1)
                            act.activation(rl[t % 2][:, h, 0:(t + 1) * P], ps[:, h, 0:(t + 1) * P], ACT.Relu)\
                               .then_inc(sem("lg_rd"), 1)

                def sgu_turned():
                    act.wait_ge(sem("ws_pe"), 2 * l + 2)
                    act.activation(wsT[:], ps[:, 0:2, :].rearrange("p b (g n) -> p (b g) n", n=P), ACT.Copy)\
                       .then_inc(sem("ws_rd"), 1)
                    act.activation(bsT[:], ps[:, 2, 0:SGG], ACT.Copy).then_inc(sem("bs_rd"), 1)

                token_major(KD, 512, gelu(vs), between=index_turned)
                row_norms(vs, TT * l, sem("vs_var"), sem("vs_sd"), sem("vs_rs"), sem("vs_z"))
                token_major(KD, 512, gelu(gu), between=sgu_turned)
                act.wait_ge(sem("sc_ok"), 12 * (l + 1))
                token_major(KD, 512, keep(lambda t: qtok[:, t, :]))
                for n in range(4):
                    act.wait_ge(sem("bo_pe"), 4 * l + n + 1)
                    act.activation(xh[:, 4 + n, :], ps[:, GATE_BANKS[n], :], ACT.Copy).then_inc(sem("bo_hi"), 1)
                for n, dst in enumerate([kT[:, c, :] for c in range(2)] + [qT[:, c, :] for c in range(4)]):
                    act.wait_ge(sem("qk_pe"), 6 * l + n + 1)
                    act.activation(dst, ps[:, SB[n % 4], :], ACT.Copy, scale=1.0 if n < 2 else HD ** -0.5)\
                       .then_inc(sem("qk_rd"), 1)
                attention(f"dsa{l}", pt2 + [pn2], 2, 0)
                def p_high():
                    for n in range(2):
                        act.wait_ge(sem("pt_pe"), 2 * l + n + 1)
                        act.activation(pTh[:, n, :], ps[:, n, :], ACT.Copy).then_inc(sem("pt_hi"), 1)

                token_major(KD, 512)
                token_major(KD, 512, hold=True, between=p_high)
                norm(kx, amid=True)
                for n in range(2):
                    def ple_evac(t, src, n=n):
                        if n == 1:
                            act.wait_ge(sem("pg_ok"), 8 * l + t + 1)
                        act.activation(plt[:, t, :], src, ACT.Copy).then_inc(b_free[t], 1)

                    def gate_evac(t, src, n=n):
                        m = 8 * l + 4 * n + t
                        if m >= 2:
                            act.wait_ge(sem("pg_ok"), m - 1)
                        act.activation((rt, ft)[t % 2][:, 0:512], src, ACT.Sigmoid).then_inc(sem("pg_sig"), 1)

                    token_major(2, 512, ple_evac, bank0=0)
                    token_major(KD, 512, gate_evac)
                act.wait_ge(sem("pg_ok"), 8 * (l + 1))
                for half in range(2):
                    channel_major(11, "swiglu", 0)
                    for n in range(2):
                        token_major(11, 512, hold=half == 1 and n == 1)
                norm(kx + 1, last=l == 1)

        @block.vector
        def _(dve):
            st = {"g": 0, "a": 0, "b": 0, "s": 0}
            seq = sem("dve_seq")

            def link(ins):
                st["s"] += 1
                ins.then_inc(seq, 1)
                dve.wait_ge(seq, st["s"])

            def split(g, i=None):
                if g >= n_chunks:
                    return
                s, n = g % 2, chunk_cols[g]
                if g in [c + n for c in LAYER_CHUNK for n in (11, 15)]:
                    dve.wait_ge(lo_ready, g)
                dve.wait_ge(hi_ready, val(g + 1, i, 2))
                dve.tensor_tensor(wlo[:, s, 0:n], raw[:, s, 0:n], f32(whi[:, s, 0:n]), ALU.subtract).then_inc(lo_ready, 1)

            def channel_major(n, kind, first):
                g0, a0 = st["g"], st["a"]
                tail = 0 if all(c == chunk_cols[g0] for c in chunk_cols[g0:g0 + n + 2]) else 2

                def body(j, i):
                    pair = (a0 + j) % 2
                    a = a0 + j
                    dve.wait_ge(act_r, val(a + 1, i, 2))
                    if a >= 1:
                        dve.wait_ge(act_h, val(a, i, 2))
                        dve.wait_ge(dve_l, val(a, i, 2))
                    if kind == "relu2":
                        dve.tensor_tensor(ft[:], rt[:], rt[:], ALU.mult).then_inc(dve_f, 1)
                    elif kind == "glu":
                        dve.tensor_tensor(ft[:, 0:S], rt[:, 0:S], ps[:, 2 * pair, :], ALU.mult).then_inc(dve_f, 1)
                    else:
                        dve.tensor_tensor(ft[:, 0:S], rt[:, 0:S], ps[:, 2 * pair + 1, :], ALU.mult).then_inc(dve_f, 1)
                    split(g0 + j + 2, i)
                    dve.wait_ge(act_h, val(a + 1, i, 2))
                    if kind == "relu2":
                        sl = slice(2 * j, 2 * j + 2) if i is None else bass.ds(i * 4 + 2 * j, 2)
                        v = ft[:].rearrange("p (b n) -> p b n", b=2)
                    else:
                        sl = slice(j, j + 1) if i is None else bass.ds(i * 2 + j, 1)
                        v = ft[:, 0:S].rearrange("p (b n) -> p b n", b=1)
                    dve.tensor_tensor(hidl[:, sl, :], v, f32(hidh[:, sl, :]), ALU.subtract).then_inc(dve_l, 1)

                pairs(dve, n, first, tail, body)
                st["g"] += n
                st["a"] += n

            def token_major(k_tiles, width, evac=None, hold=False, between=None):
                k = 0
                while k < k_tiles:
                    m = min(4 if width > 256 else 8, k_tiles - k)
                    if between and k + m == k_tiles:
                        between()
                    k += m
                    st["g"] += 1
                    if k == k_tiles:
                        if evac:
                            for t in range(TT):
                                if t < TT - 1:
                                    dve.wait_ge(b_done, 3 * st["b"] + t + 1)
                                else:
                                    dve.wait_ge(chunk_used, st["g"])
                                evac(t, ps[:, 4 + t, 0:width])
                        st["b"] += 1
                    if not (hold and k == k_tiles):
                        split(st["g"] + 1)

            def stats(x, t, width, name):
                for h in range(width // 512):
                    link(dve.bn_stats(bst[:, t, h, :], x[:, t, 512 * h:512 * h + 512]))
                dve.bn_aggr(mv[:, t, :], bst[:, t, 0:width // 512, :].rearrange("p h k -> p (h k)")).then_inc(sem(name), 1)

            def inverse(t, sd_sem, sd_n, rs_sem):
                dve.wait_ge(sd_sem, sd_n)
                link(dve.reciprocal(rstd[:, t:t + 1], sd[:, t:t + 1]))
                dve.scalar_tensor_tensor(out=nmr[:, t:t + 1], in0=mv[:, t, 0:1], scalar=-1.0, in1=rstd[:, t:t + 1],
                                         op0=ALU.mult, op1=ALU.mult).then_inc(rs_sem, 1)

            def add_to_res(n, alpha, half=None, k=0, res_n=0):
                def evac(t, src):
                    r = res[:, t, 512 * n:512 * n + 512]
                    if st["b"] > 0:
                        dve.wait_ge(b_free[t], st["b"])
                    if res_n:
                        dve.wait_ge(sem("res_ok"), TT * (res_n - 1) + t + 1)
                    dve.scalar_tensor_tensor(out=r, in0=r, scalar=alpha, in1=src, op0=ALU.mult, op1=ALU.add)\
                       .then_inc(b_free[t], 1)
                    if half is not None:
                        dve.wait_ge(b_free[t], st["b"] + 1)
                        link(dve.bn_stats(bst[:, t, half, :], r))
                        if half == 1:
                            dve.bn_aggr(mv[:, t, :], bst[:, t, :, :].rearrange("p h k -> p (h k)")).then_inc(sem("ln_var"), 1)
                            if t > 0:
                                inverse(t - 1, sem("ln_sd"), TT * k + t, sem("ln_rs"))
                            if t == TT - 1:
                                inverse(t, sem("ln_sd"), TT * k + TT, sem("ln_rs"))
                return evac

            def norm(k, last=False, next_chunk=True):
                if k == 0:
                    dve.wait_ge(sem("lng_in"), 16 * (2 * N_LN + 2))
                for c in range(KD + 1 if not last else 0):
                    if c < KD:
                        dve.wait_ge(sem("xt_pe"), KD * k + c + 1)
                        dve.tensor_scalar(xf(c), ps[:, c, :], lng[:, k, 0, c:c + 1], lng[:, k, 1, c:c + 1],
                                          ALU.mult, ALU.add).then_inc(sem("xt_f"), 1)
                    if c > 0:
                        dve.wait_ge(sem("xt_hi"), KD * k + c)
                        dve.tensor_tensor(xl[:, c - 1, :], xf(c - 1), f32(xh[:, c - 1, :]), ALU.subtract)\
                           .then_inc(sem("xt_lo"), 1)
                if last:
                    dve.wait_ge(sem("lnp_in"), 32 * (k + 1))
                    for t in range(TT):
                        dve.wait_ge(sem("ln_z"), TT * k + t + 1)
                        link(dve.tensor_tensor(res[:, t, :], res[:, t, :], lnp[:, 0, :], ALU.mult))
                        dve.tensor_tensor(res[:, t, :], res[:, t, :], lnp[:, 1, :], ALU.add).then_inc(sem("out_ok"), 1)
                else:
                    dve.wait_ge(sem("xt_lo"), KD * (k + 1))
                if next_chunk:
                    split(st["g"] + 1)

            dve.wait_ge(sem("lam_in"), 48)
            dve.tensor_copy(lam[:, 2, :].rearrange("q (a p) -> q a p", a=2),
                            ldt[:].unsqueeze(2).broadcast_to([Q, 2, NS])).then_inc(sem("ldt_wide"), 1)
            def wrap(x, n):
                link(dve.tensor_scalar(n, x, 1 / (2 * math.pi), MAGIC, ALU.mult, ALU.add))
                link(dve.tensor_scalar(n, n, -MAGIC, None, ALU.add))
                for c in TWO_PI:
                    link(dve.scalar_tensor_tensor(out=x, in0=n, scalar=-c, in1=x, op0=ALU.mult, op1=ALU.add))
                return dve.tensor_scalar(x, x, -PI_IN, PI_IN, ALU.max, ALU.min)

            dve.wait_ge(sem("lam_pe"), 1)
            dve.tensor_copy(sc[:, 0:3, :], ps[:, 0, 0:3 * Q].rearrange("p (i q) -> p i q", i=3)).then_inc(sem("lam_rd"), 1)
            dve.wait_ge(sem("dt_ok"), 1)
            for i in range(2):
                link(dve.tensor_tensor(sc[:, 4 + i, :], sc[:, i, :], sc[:, 3, :], ALU.mult))
            link(dve.tensor_copy(sc[:, 6, :], sc[:, 5, :]))
            wrap(sc[:, 6, :], sc[:, 7, :]).then_inc(sem("ang_ok"), 1)
            dve.wait_ge(sem("mag_ok"), 2)
            link(dve.memset(pw[:, 0, 0, :], 1.0))
            link(dve.memset(pw[:, 1, 0, :], 0.0))
            link(dve.tensor_tensor(pw[:, 0, 1, :], sc[:, 10, :], sc[:, 9, :], ALU.mult))
            link(dve.tensor_tensor(pw[:, 1, 1, :], sc[:, 10, :], sc[:, 8, :], ALU.mult))
            link(dve.tensor_scalar(sc[:, 12, :], pw[:, 0, 1, :], -1.0, None, ALU.add))
            for o, a, b in ((13, 0, 0), (14, 1, 1)):
                link(dve.tensor_tensor(sc[:, o, :], sc[:, a, :], sc[:, b, :], ALU.mult))
            link(dve.tensor_tensor(sc[:, 13, :], sc[:, 13, :], sc[:, 14, :], ALU.add))
            link(dve.reciprocal(sc[:, 14, :], sc[:, 13, :]))
            link(dve.tensor_tensor(sc[:, 15, :], sc[:, 12, :], sc[:, 0, :], ALU.mult))
            link(dve.tensor_tensor(sc[:, 16, :], pw[:, 1, 1, :], sc[:, 1, :], ALU.mult))
            link(dve.tensor_tensor(sc[:, 15, :], sc[:, 15, :], sc[:, 16, :], ALU.add))
            link(dve.tensor_tensor(sc[:, 15, :], sc[:, 15, :], sc[:, 14, :], ALU.mult))
            link(dve.tensor_tensor(sc[:, 16, :], pw[:, 1, 1, :], sc[:, 0, :], ALU.mult))
            link(dve.tensor_tensor(sc[:, 17, :], sc[:, 12, :], sc[:, 1, :], ALU.mult))
            link(dve.tensor_tensor(sc[:, 16, :], sc[:, 16, :], sc[:, 17, :], ALU.subtract))
            link(dve.tensor_tensor(sc[:, 16, :], sc[:, 16, :], sc[:, 14, :], ALU.mult))

            for lo, n in ((1, 1), (1, 2), (1, 4)):
                top = n
                bc = lambda r: pw[:, r, top:top + 1, :].broadcast_to([P, n, Q])
                t0, t1 = (rt[:, 512 * i:512 * i + n * Q].rearrange("p (n q) -> p n q", n=n) for i in range(2))
                dve.wait_ge(sem("c_pe"), 1)
                cmul(dve, link, pw[:, 0, top + 1:top + 1 + n, :], pw[:, 1, top + 1:top + 1 + n, :],
                     pw[:, 0, 1:1 + n, :], pw[:, 1, 1:1 + n, :], bc(0), bc(1), t0, t1).then_inc(sem("pw_ok"), 1)
                dve.wait_ge(sem("pw_ok"), {1: 1, 2: 2, 4: 3}[n])
            dve.wait_ge(sem("b_in"), 32)
            T0, T1 = (x[:, 0:512].rearrange("p (q c) -> p q c", c=GC) for x in (rt, ft))
            cmul(dve, link, bb[:, 0], bb[:, 1], wide(sc[:, 15, :]), wide(sc[:, 16, :]), b_in[:, 0], b_in[:, 1], T0, T1)\
                .then_inc(sem("bb_ok"), 1)
            dve.wait_ge(sem("bb_ok"), 1)
            for j in range(AB_POOL[0]):
                k = L - 1 - j
                ins = cmul(dve, link, ab[:, 0, :, j, :], ab[:, 1, :, j, :], wide(pw[:, 0, k, :]), wide(pw[:, 1, k, :]),
                           bb[:, 0], bb[:, 1], T0, T1)
                if j < AB_POOL[0] - 1:
                    link(ins)
            ins.then_inc(sem("ab_ok"), 1)
            for m in range(1, 16, 2):
                dve.wait_ge(sem("mt_pe"), m + 1)
                n = m % 8
                dve.tensor_copy(mt[m // 8][:, 4 * n:4 * n + 4, :], ps[:, MB[m % 4], :].rearrange("p (q c) -> p q c", q=4))\
                   .then_inc(sem("mt_rd1"), 1)
            for m in range(1, 8, 2):
                dve.wait_ge(sem("s_pe"), m + 1)
                n = m % 4
                dve.tensor_copy(sst[:, m // 4, 8 * n:8 * n + 8, :], ps[:, 5 + m % 2, :].rearrange("p (q c) -> p q c", q=8))\
                   .then_inc(sem("s_rd1"), 1)
            NB = NC // SB_J
            dve.wait_ge(sem("s_rd0"), 4)
            dve.wait_ge(sem("s_rd1"), 4)

            def blocks(x):
                return x[:].rearrange("p a q (b j) -> p a q b j", j=SB_J)

            def at_j(x, j):
                return blocks(x)[:, :, :, :, bass.ds(j, 1)].rearrange("p a q b o -> p a q (b o)")

            e = rt[:, 0:512].rearrange("p (a q b) -> p a q b", a=2, b=NB)
            t0 = rt[:, 512:1024].rearrange("p (a q b) -> p a q b", a=2, b=NB)
            t1 = ft[:, 0:512].rearrange("p (a q b) -> p a q b", a=2, b=NB)

            def step(name, i, first, ar, ai, h, sv, h2, u0, u1):
                sm, n = sem(name), lambda k: i * 6 + (k - 6 * first)
                dve.tensor_tensor(u0, ar, h, ALU.mult).then_inc(sm, 1)
                dve.tensor_tensor(u1[:, 0], ai, h[:, 1], ALU.mult).then_inc(sm, 1)
                dve.tensor_tensor(u1[:, 1], ai, h[:, 0], ALU.mult).then_inc(sm, 1)
                dve.wait_ge(sm, n(3))
                dve.tensor_tensor(u0, u0, sv, ALU.add).then_inc(sm, 1)
                dve.wait_ge(sm, n(4))
                dve.tensor_tensor(h2[:, 0], u0[:, 0], u1[:, 0], ALU.subtract).then_inc(sm, 1)
                dve.tensor_tensor(h2[:, 1], u0[:, 1], u1[:, 1], ALU.add).then_inc(sm, 1)
                dve.wait_ge(sm, n(6))

            a64 = a64t[:]
            link(dve.tensor_copy(a64, pw[:, :, L, :]))
            for _ in range(3):
                x, y = a64[:, 0], a64[:, 1]
                dve.tensor_tensor(t1[:, 0, :, 0], x, x, ALU.mult)
                dve.tensor_tensor(t1[:, 0, :, 1], y, y, ALU.mult)
                link(dve.tensor_tensor(t1[:, 0, :, 2], x, y, ALU.mult))
                dve.tensor_tensor(x, t1[:, 0, :, 0], t1[:, 0, :, 1], ALU.subtract)
                link(dve.tensor_scalar(y, t1[:, 0, :, 2], 2.0, None, ALU.mult))
            a8r = pw[:, 0, L, :].unsqueeze(1).unsqueeze(3).broadcast_to([P, 2, Q, NB])
            a8i = pw[:, 1, L, :].unsqueeze(2).broadcast_to([P, Q, NB])
            link(dve.memset(hst[:, :, :, 0], 0.0))
            link(dve.tensor_copy(e, blocks(sst)[:, :, :, :, 0]))
            with dve.Fori(1, SB_J) as j:
                step("scan1", j, 1, a8r, a8i, e, at_j(sst, j), e, t0, t1)
            link(dve.tensor_copy(hst[:, :, :, SB_J], e[:, :, :, 0]))
            with dve.Fori(1, NB - 1) as b:
                def first_of(x, o):
                    return x[:, :, :, bass.ds(b * SB_J + o, 1)].rearrange("p a q o -> p a (q o)")
                step("carry", b, 1, a64[:, 0].unsqueeze(1).broadcast_to([P, 2, Q]), a64[:, 1], first_of(hst, 0),
                     e[:, :, :, bass.ds(b, 1)].rearrange("p a q o -> p a (q o)"), first_of(hst, SB_J),
                     t0[:, :, :, 0], t1[:, :, :, 0])
            with dve.Fori(0, SB_J - 1) as j:
                step("scan2", j, 0, a8r, a8i, at_j(hst, j), at_j(sst, j), at_j(hst, j + 1), t0, t1)
            dve.wait_ge(sem("pos_in"), 32)
            link(dve.tensor_copy(posf[:], posi[:]))
            v1 = ang[:, 0, 0:128].rearrange("p (t k) -> p t k", t=TT)
            v2 = ang[:, 0, 128:160].rearrange("p (t k) -> p t k", t=TT)
            link(dve.tensor_tensor(v1, posf[:, 0, :].unsqueeze(2).broadcast_to([P, TT, 32]),
                                   inv1[:].unsqueeze(1).broadcast_to([P, TT, 32]), ALU.mult))
            link(dve.tensor_tensor(v2, posf[:, 1, :].unsqueeze(2).broadcast_to([P, TT, 8]),
                                   inv2[:].unsqueeze(1).broadcast_to([P, TT, 8]), ALU.mult))
            wrap(ang[:, 0, :], ang[:, 1, :]).then_inc(sem("ang_ok"), 1)
            for c in range(KD):
                dve.wait_ge(sem("yt_hi"), c + 1)
                dve.tensor_tensor(xl[:, c, :].rearrange("p (n j) -> p n j", j=L),
                                  ps[:, c % 4, :].rearrange("p (j n) -> p n j", j=L),
                                  f32(xh[:, c, :]).rearrange("p (n j) -> p n j", j=L), ALU.subtract).then_inc(sem("yt_lo"), 1)
            split(0)
            split(1)

            def relu_mlp(k):
                for half in range(2):
                    channel_major(8, "relu2", 0)
                    for n in range(2):
                        token_major(16, 512, add_to_res(n, ALPHA if half == 0 else 1.0, n if half == 1 else None, k,
                                                        k if half == 0 else 0), hold=half == 1 and n == 1)
                norm(k)

            def out_proj(k):
                token_major(KD, 512, add_to_res(0, ALPHA, 0, k, k))
                token_major(KD, 512, add_to_res(1, ALPHA, 1, k, k), hold=True)
                norm(k)

            channel_major(KD, "glu", 2)
            dve.wait_ge(sem("res_in"), 16 * TT)
            out_proj(0)
            relu_mlp(1)

            def latent_low(name, high, low, gain):
                for c in range(high.shape[1]):
                    dve.wait_ge(sem(name + "_hi"), c + 1)
                    dve.scalar_tensor_tensor(out=low[:, c, :], in0=ps[:, c, :], scalar=gain[:, c:c + 1],
                                             in1=f32(high[:, c, :]), op0=ALU.mult, op1=ALU.subtract)\
                       .then_inc(sem(name + "_rd"), 1)

            def unit_rows(x, n, col, name):
                dve.wait_ge(sem(name), 1)
                link(dve.reciprocal(mv[:, :, col:col + 1], bst[:, :, col, 0:1]))
                for t in range(TT):
                    ins = dve.tensor_scalar(x[:, t, 0:n], x[:, t, 0:n], mv[:, t, col:col + 1], None, ALU.mult)
                return ins

            token_major(KD, KVL + ROPE)
            link(unit_rows(ckv, KVL, 0, "kv_sd"))
            link(rope(dve, link, ckv[:, :, KVL:KVL + 32], ckv[:, :, KVL + 32:KVL + 64], cos1[:], sin1[:],
                      krd[:, :, 0:32], krd[:, :, 32:64],
                      [rt[:, 128 * i:128 * i + 128].rearrange("p (t k) -> p t k", t=TT) for i in range(4)]))
            dve.tensor_copy(krd[:, :, 64:128], krd[:, :, 0:64]).then_inc(sem("kv_ok"), 1)
            st["g"] += 1
            split(st["g"] + 1)
            latent_low("kvl", ckvh, ckvl, kvg)
            dve.wait_ge(sem("kvl_pe"), 3)
            dve.tensor_copy(krT[:], ps[:, 2, :]).then_inc(sem("kvl_rd"), 1)
            st["g"] += 1
            st["b"] += 1
            split(st["g"] + 1)
            unit_rows(cq, QL, 1, "q_sd").then_inc(sem("q_ok"), 1)
            for c in range(2):
                st["g"] += 1
                if c == 0:
                    dve.wait_ge(chunk_used, st["g"])
                else:
                    dve.wait_ge(sem("v_pe"), 1)
                dve.tensor_copy(vv[:, :, 512 * c:512 * c + 512], ps[:, 4:8, :]).then_inc(sem("v_rd"), 1)
                if c == 0:
                    latent_low("ql", cqh, cql, qg)
                split(st["g"] + 1)
            for c in range(4):
                dve.wait_ge(sem("qr_rd"), c + 1)
                v = qrt[:, :, c * P:(c + 1) * P].rearrange("p t (h d) -> p t h d", h=2)
                cs, sn = (x[:].unsqueeze(2).broadcast_to([P, TT, 2, 32]) for x in (cos1, sin1))
                rope(dve, link, v[:, :, :, 0:32], v[:, :, :, 32:64], cs, sn, v[:, :, :, 0:32], v[:, :, :, 32:64],
                     [rt[:, 256 * i:256 * i + 256].rearrange("p (t h k) -> p t h k", t=TT, h=2) for i in range(4)])\
                    .then_inc(sem("qrope_ok"), 1)
                st["g"] += 1
                dve.wait_ge(chunk_used, st["g"])
                dve.tensor_scalar(qn[:, 2 * c:2 * c + 2, :], ps[:, 2 * (c % 2):2 * (c % 2) + 2, :], SM_SCALE, None,
                                  ALU.mult).then_inc(sem("qn_rd"), 1)
                split(st["g"] + 1)
                dve.wait_ge(sem("qrope_ok"), c + 1)

            def attention(name, pt, per, dst):
                def first(u):
                    n = (u % TT + 1) * P
                    dve.wait_ge(sem(name + "_s"), u + 1)
                    dve.tensor_reduce(nmax[:, u % 4:u % 4 + 1], ps[:, SB[u % 4], 0:n], axis=AX.X, op=ALU.max,
                                      negate=True).then_inc(sem(name + "_mx"), 1)

                def low(n0):
                    dve.wait_ge(sem(name + "_o_hi"), n0 + 1)
                    dve.tensor_tensor(xl[:, dst + n0, :], ps[:, 4 + n0 % 2, :], f32(xh[:, dst + n0, :]), ALU.subtract)\
                       .then_inc(sem(name + "_o_lo"), 1)

                for u in range(3):
                    first(u)
                for u in range(NH * TT):
                    h, t = u // TT, u % TT
                    n = (t + 1) * P
                    dve.wait_ge(sem(name + "_e"), u + 1)
                    link(dve.reciprocal(rinv[:, u % 4:u % 4 + 1], rsum[:, u % 4:u % 4 + 1]))
                    dve.tensor_scalar(pt[2][:, u % 3, 0:n], pt[2][:, u % 3, 0:n], rinv[:, u % 4:u % 4 + 1], None,
                                      ALU.mult).then_inc(sem(name + "_pn"), 1)
                    if u + 3 < NH * TT:
                        first(u + 3)
                    if t == 3 and h >= per and h % per == 0:
                        low(h // per - 1)
                low(NH // per - 1)

            attention("mla", pt1 + [pn1], 1, 0)
            out_proj(2)
            relu_mlp(3)

            for l in range(2):
                kx = 4 + 2 * l
                token_major(KD, 512)
                token_major(KD, 68)
                for t in range(TT):
                    dve.wait_ge(b_free[t], st["b"])
                rope_heads(dve, link, kvq[:, :, 256:512], NI, rot_i).then_inc(sem("i_rot_q"), 1)
                dve.wait_ge(sem("i_rot_q"), l + 1)
                link(rope_heads(dve, link, kiw[:, :, 0:64], 1, rot_i))
                link(dve.tensor_scalar(kiw[:, :, 64:68], kiw[:, :, 64:68], (NI * IXD) ** -0.5, None, ALU.mult))
                link(dve.tensor_copy(kid[:, :, 0:64], kiw[:, :, 0:64]))
                dve.tensor_copy(kid[:, :, 64:128], kiw[:, :, 0:64]).then_inc(sem("i_rot"), 1)
                st["g"] += 1
                split(st["g"] + 1)
                for t in range(1, TT):
                    n = (t + 1) * P
                    for h in range(NI):
                        m = 4 * (3 * l + t - 1) + h
                        dve.wait_ge(sem("lg_rd"), m + 1)
                        wcol = kiw[:, t, 64 + h:65 + h]
                        x = rl[t % 2][:, h, 0:n]
                        if h == 0:
                            ins = dve.tensor_scalar(scr[:, t - 1, 0:n], x, wcol, None, ALU.mult)
                        else:
                            ins = dve.scalar_tensor_tensor(out=scr[:, t - 1, 0:n], in0=x, scalar=wcol,
                                                           in1=scr[:, t - 1, 0:n], op0=ALU.mult, op1=ALU.add)
                        ins.then_inc(sem("sc_ok"), 1)
                        dve.wait_ge(sem("sc_ok"), m + 1)
                st["g"] += 5
                st["b"] += 3

                def gate_norm():
                    for t in range(TT):
                        dve.wait_ge(b_free[t], st["b"] - 2)
                        stats(vs, t, SGW, "vs_var")
                    for t in range(TT):
                        inverse(t, sem("vs_sd"), 4 * l + t + 1, sem("vs_rs"))

                def gate():
                    dve.wait_ge(sem("sg_pe"), l + 1)
                    dve.wait_ge(sem("bs_rd"), l + 1)
                    for g in range(SGG):
                        v = ps[:, g // 2, (g % 2) * 256:(g % 2 + 1) * 256].rearrange("p (t c) -> p t c", t=TT)
                        o = gu[:, :, g * 64:(g + 1) * 64]
                        ins = dve.scalar_tensor_tensor(out=o, in0=v, scalar=bsT[:, g:g + 1], in1=o, op0=ALU.add,
                                                       op1=ALU.mult)
                    ins.then_inc(sem("bo_ok"), 1)

                def gated_low():
                    for n in range(4):
                        dve.wait_ge(sem("bo_hi"), 4 * l + n + 1)
                        dve.tensor_tensor(xl[:, 4 + n, :], ps[:, GATE_BANKS[n], :], f32(xh[:, 4 + n, :]), ALU.subtract)\
                           .then_inc(sem("bo_rd"), 1)

                meanwhile = {(1, 15): gate_norm, (3, 7): gate, (3, 15): gated_low}
                dve.tensor_copy(mask[:, 0, 0:P], chunkm[:]).then_inc(sem("mask_ok"), 1)
                for t in range(1, TT):
                    n = (t + 1) * P
                    x = scr[:, t - 1, 0:n]
                    link(dve.tensor_tensor(x[:, n - P:n], x[:, n - P:n], chunkm[:], ALU.add))
                    for r in range(TOPK // 8):
                        link(dve.max(m8[:], x))
                        link(dve.match_replace(x, m8[:], x, TAKEN))
                        if (t, r) in meanwhile:
                            meanwhile[t, r]()
                    dve.tensor_scalar(mask[:, t, 0:n], x, TAKEN / 2, NEG, ALU.is_gt, ALU.mult)\
                       .then_inc(sem("mask_ok"), 1)
                attention(f"dsa{l}", pt2 + [pn2], 2, 0)
                def p_low():
                    for n in range(2):
                        dve.wait_ge(sem("pt_hi"), 2 * l + n + 1)
                        dve.tensor_tensor(pTl[:, n, :], ps[:, n, :], f32(pTh[:, n, :]), ALU.subtract)\
                           .then_inc(sem("pt_rd"), 1)

                token_major(KD, 512, add_to_res(0, ALPHA, 0, kx, kx))
                token_major(KD, 512, add_to_res(1, ALPHA, 1, kx, kx), hold=True, between=p_low)
                norm(kx, next_chunk=False)

                for n in range(2):
                    def gate_evac(t, src, n=n):
                        m = 8 * l + 4 * n + t
                        dve.wait_ge(sem("pg_sig"), m + 1)
                        x = (rt, ft)[t % 2][:, 0:512]
                        dve.tensor_tensor(x, x, plt[:, t, :], ALU.mult).then_inc(b_free[t], 1)
                        dve.wait_ge(b_free[t], st["b"] + 1)
                        r = res[:, t, 512 * n:512 * n + 512]
                        dve.wait_ge(sem("res_ok"), TT * kx + t + 1)
                        dve.scalar_tensor_tensor(out=r, in0=r, scalar=ALPHA, in1=x, op0=ALU.mult, op1=ALU.add)\
                           .then_inc(sem("pg_ok"), 1)
                    token_major(2, 512)
                    token_major(KD, 512, gate_evac)
                for half in range(2):
                    channel_major(11, "swiglu", 0)
                    for n in range(2):
                        token_major(11, 512, add_to_res(n, 1.0, n if half == 1 else None, kx + 1),
                                    hold=half == 1 and n == 1)
                norm(kx + 1, last=l == 1)


IXD = 64
GROUPS_1 = 14
GROUPS_2 = 15

_INS = ['x', 'positions', 'ln_mix_g', 'ln_mix_b', 'ln_ffn_g', 'ln_ffn_b', 'w_ff1', 'w_ff2', 'ssm_lam_re',
        'ssm_lam_im', 'ssm_log_dt', 'ssm_b_re', 'ssm_b_im', 'ssm_c_re', 'ssm_c_im', 'ssm_d', 'ssm_w_glu',
        'ssm_w_out', 'kv_w_a', 'kv_norm_g', 'kv_w_b', 'q_w_a', 'q_norm_g', 'q_w_b', 'attn_w_o', 'p_2',
        'positions_2', 'w_in_2', 'w_o_2', 'ln1_g_2', 'ln1_b_2', 'ln2_g_2', 'ln2_b_2', 'sgu_w_2', 'sgu_b_2',
        'sgu_ln_g_2', 'sgu_ln_b_2', 'w_ffn_in_2', 'w_ffn_out_2', 'w_ple_2', 'w_ple_gate_2']


def kernel(**inputs):
    import numpy as _np
    import concourse.bacc as _bacc
    from concourse import mybir as _mybir
    from concourse.bass_utils import run_bass_kernel_spmd as _run

    nc = _bacc.Bacc("TRN2", target_bir_lowering=False, num_devices=1)
    arrays, w = {}, {}
    for name in _INS:
        a = _np.ascontiguousarray(inputs[name])
        arrays[f"in_{name}_dram"] = a
        w[name] = nc.dram_tensor(f"in_{name}_dram", a.shape, _mybir.dt.from_np(a.dtype), kind="ExternalInput").ap()
    out = nc.dram_tensor("out_0_dram", (1, S, D), _mybir.dt.float32, kind="ExternalOutput").ap()
    two_blocks(nc, w, out)
    r = _run(nc, [arrays], core_ids=[0])
    return r.results[0]["out_0_dram"]
```
